# Optimizing a Trainium2 kernel written in Bass

```python
import jax, jax.numpy as jnp
from jax import lax
import numpy as np

D_MODEL = 1024
BATCH = 1
SEQ = 256
DEPTH = 2

N_A_LAYERS = max(1, DEPTH // 2)
N_B_LAYERS = DEPTH - N_A_LAYERS
RMS_EPS = 1e-6
NEG_INF = -1e30
MLSTM_HEADS = 4
MLSTM_V_DIM = D_MODEL // MLSTM_HEADS
MLSTM_QK_DIM = MLSTM_V_DIM // 2
MLSTM_CHUNK = 64
GATE_SOFTCAP = 15.0
NSA_HEADS = 16
NSA_HEAD_DIM = D_MODEL // NSA_HEADS
NSA_KV_GROUPS = 4
NSA_GROUP_SIZE = NSA_HEADS // NSA_KV_GROUPS
CMP_BLOCK = 32
CMP_STRIDE = 16
SEL_BLOCK = 64
SEL_TOPK = 16
WINDOW = 512
Q_BLOCK = 128
FORCED_SCORE = 1e6
ROPE_THETA = 500000.0
ROPE_DIM = NSA_HEAD_DIM // 4
MOE_GROUPS = 4
MOE_EXPERTS_PER_GROUP = 8
MOE_EXPERTS = MOE_GROUPS * MOE_EXPERTS_PER_GROUP
MOE_TOPK = 2
MOE_HIDDEN = D_MODEL // 4

kernel_name = 'yoco_mlstm_nsa_hier_moe'

def rmsnorm(x, g):
    xf = x.astype(jnp.float32)
    y = xf * lax.rsqrt(jnp.mean(xf * xf, axis=-1, keepdims=True) + RMS_EPS)
    return (y * g.astype(jnp.float32)).astype(x.dtype)

def partial_rope(x, pos):
    half = ROPE_DIM // 2
    inv_freq = jnp.power(jnp.float32(ROPE_THETA), -jnp.arange(half, dtype=jnp.float32) * (2.0 / ROPE_DIM))
    ang = pos.astype(jnp.float32)[:, None] * inv_freq[None, :]
    cos = jnp.cos(ang)[None, :, None, :]
    sin = jnp.sin(ang)[None, :, None, :]
    xf = x.astype(jnp.float32)
    x1 = xf[..., :half]
    x2 = xf[..., half:ROPE_DIM]
    out = jnp.concatenate([x1 * cos - x2 * sin, x2 * cos + x1 * sin, xf[..., ROPE_DIM:]], axis=-1)
    return out.astype(x.dtype)

def mlstm_chunk_scan(q, k, v, log_i, log_f):
    B, H, S, dk = q.shape
    dv = v.shape[-1]
    L = MLSTM_CHUNK
    nc = S // L

    def to_chunks(t):
        return jnp.moveaxis(t.reshape((B, H, nc, L) + t.shape[3:]), 2, 0)

    causal = jnp.tril(jnp.ones((L, L), dtype=bool))

    def step(carry, xs):
        C, n, m = carry
        qc, kc, vc, li, lf = xs
        b = jnp.cumsum(lf, axis=-1)
        dmat = jnp.where(causal, b[..., :, None] - b[..., None, :] + li[..., None, :], NEG_INF)
        m_inter = b + m[..., None]
        m_t = jnp.maximum(m_inter, dmat.max(axis=-1))
        w_intra = jnp.exp(dmat - m_t[..., None])
        w_inter = jnp.exp(m_inter - m_t)
        s = jnp.einsum('bhtd,bhsd->bhts', qc, kc) * w_intra
        num = jnp.einsum('bhts,bhsv->bhtv', s, vc) + w_inter[..., None] * jnp.einsum('bhtd,bhdv->bhtv', qc, C)
        den = s.sum(axis=-1) + w_inter * jnp.einsum('bhtd,bhd->bht', qc, n)
        h = num / jnp.maximum(jnp.abs(den), jnp.exp(-m_t))[..., None]
        b_end = b[..., -1]
        g = b_end[..., None] - b + li
        m_new = jnp.maximum(b_end + m, g.max(axis=-1))
        ws = jnp.exp(g - m_new[..., None])
        decay = jnp.exp(b_end + m - m_new)
        C_new = decay[..., None, None] * C + jnp.einsum('bhsd,bhsv->bhdv', kc * ws[..., None], vc)
        n_new = decay[..., None] * n + jnp.einsum('bhs,bhsd->bhd', ws, kc)
        return (C_new, n_new, m_new), h

    init = (jnp.zeros((B, H, dk, dv), jnp.float32), jnp.zeros((B, H, dk), jnp.float32), jnp.zeros((B, H), jnp.float32))
    xs = (to_chunks(q), to_chunks(k), to_chunks(v), to_chunks(log_i), to_chunks(log_f))
    _, hs = lax.scan(step, init, xs)
    return jnp.moveaxis(hs, 0, 2).reshape(B, H, S, dv)

def mlstm_mixer(h, w_in, gate_bias, head_norm, w_out):
    B, S, _ = h.shape
    H, dk, dv = MLSTM_HEADS, MLSTM_QK_DIM, MLSTM_V_DIM
    f32 = jnp.float32
    proj = jnp.einsum('bsd,de->bse', h, w_in)
    o1 = H * dk
    o2 = 2 * H * dk
    o3 = o2 + H * dv
    o4 = o3 + H * dv

    def heads(t, d):
        return t.reshape(B, S, H, d).transpose(0, 2, 1, 3).astype(f32)

    q = heads(proj[..., :o1], dk)
    k = heads(proj[..., o1:o2], dk) * (dk ** -0.5)
    v = heads(proj[..., o2:o3], dv)
    o_gate = jax.nn.sigmoid(proj[..., o3:o4].astype(f32))
    gates = proj[..., o4:].astype(f32) + gate_bias.astype(f32)
    gates = GATE_SOFTCAP * jnp.tanh(gates / GATE_SOFTCAP)
    log_i = gates[..., :H].transpose(0, 2, 1)
    log_f = jax.nn.log_sigmoid(gates[..., H:]).transpose(0, 2, 1)
    hs = mlstm_chunk_scan(q, k, v, log_i, log_f)
    hs = hs * lax.rsqrt(jnp.mean(hs * hs, axis=-1, keepdims=True) + RMS_EPS)
    hs = hs.transpose(0, 2, 1, 3).reshape(B, S, H * dv) * head_norm.astype(f32)
    out = (hs * o_gate).astype(h.dtype)
    return jnp.einsum('bse,ed->bsd', out, w_out)

def compress_blocks(t, pe, w1, w2):
    B, S, G, dh = t.shape
    ncmp = (S - CMP_BLOCK) // CMP_STRIDE + 1
    idx = jnp.arange(ncmp)[:, None] * CMP_STRIDE + jnp.arange(CMP_BLOCK)[None, :]
    blk = t[:, idx] + pe[None, None, :, None, :]
    blk = blk.transpose(0, 1, 3, 2, 4).reshape(B, ncmp, G, CMP_BLOCK * dh)
    return jnp.einsum('bngf,fd->bngd', jax.nn.silu(jnp.einsum('bngi,if->bngf', blk, w1)), w2)

def nsa_shared_kv(x_mid, kv_norm, kv_w, cmp_pe_k, cmp_w1_k, cmp_w2_k, cmp_pe_v, cmp_w1_v, cmp_w2_v):
    B, S, _ = x_mid.shape
    G, dh = NSA_KV_GROUPS, NSA_HEAD_DIM
    hk = rmsnorm(x_mid, kv_norm)
    kv = jnp.einsum('bsd,de->bse', hk, kv_w).reshape(B, S, 6, G, dh)
    pos = jnp.arange(S)
    ncmp = (S - CMP_BLOCK) // CMP_STRIDE + 1
    cmp_pos = jnp.arange(ncmp) * CMP_STRIDE + CMP_BLOCK - 1
    k_cmp = partial_rope(compress_blocks(kv[:, :, 0], cmp_pe_k, cmp_w1_k, cmp_w2_k), cmp_pos)
    v_cmp = compress_blocks(kv[:, :, 1], cmp_pe_v, cmp_w1_v, cmp_w2_v)
    k_slc = partial_rope(kv[:, :, 2], pos)
    v_slc = kv[:, :, 3]
    k_win = partial_rope(kv[:, :, 4], pos)
    v_win = kv[:, :, 5]
    tg = lambda t: t.transpose(0, 2, 1, 3)
    return (tg(k_cmp), tg(v_cmp), tg(k_slc), tg(v_slc), tg(k_win), tg(v_win))

def nsa_mixer(h, w_q, w_out, k_cmp, v_cmp, k_slc, v_slc, k_win, v_win):
    B, S, _ = h.shape
    H, G, Hg, dh = NSA_HEADS, NSA_KV_GROUPS, NSA_GROUP_SIZE, NSA_HEAD_DIM
    f32 = jnp.float32
    scale = dh ** -0.5
    nqb = S // Q_BLOCK
    nsel = S // SEL_BLOCK
    ncmp = k_cmp.shape[2]
    k_eff = min(SEL_TOPK, nsel)
    proj = jnp.einsum('bsd,de->bse', h, w_q)
    q = partial_rope(proj[..., :H * dh].reshape(B, S, H, dh), jnp.arange(S))
    q = q.astype(f32).reshape(B, nqb, Q_BLOCK, G, Hg, dh).transpose(1, 0, 3, 4, 2, 5)
    gates = jax.nn.sigmoid(proj[..., H * dh:].astype(f32))
    gates = gates.reshape(B, nqb, Q_BLOCK, G, Hg, 3).transpose(1, 0, 3, 4, 2, 5)
    starts = jnp.arange(nqb, dtype=jnp.int32) * Q_BLOCK
    kc = k_cmp.astype(f32)
    vc = v_cmp.astype(f32)
    ks_blk = k_slc.astype(f32).reshape(B, G, nsel, SEL_BLOCK, dh)
    vs_blk = v_slc.astype(f32).reshape(B, G, nsel, SEL_BLOCK, dh)
    pad = ((0, 0), (0, 0), (WINDOW, 0), (0, 0))
    kw_pad = jnp.pad(k_win.astype(f32), pad)
    vw_pad = jnp.pad(v_win.astype(f32), pad)
    cmp_start = jnp.arange(ncmp) * CMP_STRIDE
    cmp_end = cmp_start + CMP_BLOCK - 1
    sel_start = jnp.arange(nsel) * SEL_BLOCK
    overlap = ((cmp_start[:, None] <= sel_start[None, :] + SEL_BLOCK - 1)
               & (cmp_end[:, None] >= sel_start[None, :])).astype(f32)
    sel_ids = jnp.arange(nsel)
    r = jnp.arange(SEL_BLOCK)
    win_off = jnp.arange(WINDOW + Q_BLOCK)
    gather = jax.vmap(jax.vmap(lambda blocks, idx: blocks[idx]))

    def block_fn(args):
        qb, gb, q0 = args
        tpos = q0 + jnp.arange(Q_BLOCK)
        valid_c = cmp_end[None, :] <= tpos[:, None]
        s_c = jnp.einsum('bghqd,bgnd->bghqn', qb, kc) * scale
        p_c = jax.nn.softmax(jnp.where(valid_c, s_c, NEG_INF), axis=-1) * valid_c.any(axis=-1)[:, None].astype(f32)
        o_c = jnp.einsum('bghqn,bgnd->bghqd', p_c, vc)
        imp = jnp.einsum('bghqn,nj->bgqj', p_c, overlap)
        cur = tpos // SEL_BLOCK
        forced = (sel_ids[None, :] == 0) | (sel_ids[None, :] == cur[:, None]) | (sel_ids[None, :] == cur[:, None] - 1)
        imp = jnp.where(forced, FORCED_SCORE, imp)
        imp = jnp.where(sel_ids[None, :] > cur[:, None], NEG_INF, imp)
        _, sel = lax.top_k(imp, k_eff)

        def slot(carry, bidx):
            m_run, l_run, acc = carry
            kj = gather(ks_blk, bidx)
            vj = gather(vs_blk, bidx)
            mask = (bidx[..., None] * SEL_BLOCK + r <= tpos[:, None])[:, :, None]
            s = jnp.where(mask, jnp.einsum('bghqd,bgqrd->bghqr', qb, kj) * scale, NEG_INF)
            m_new = jnp.maximum(m_run, s.max(axis=-1))
            p = jnp.exp(s - m_new[..., None]) * mask
            corr = jnp.exp(m_run - m_new)
            acc_new = acc * corr[..., None] + jnp.einsum('bghqr,bgqrd->bghqd', p, vj)
            return (m_new, l_run * corr + p.sum(axis=-1), acc_new), None

        init = (jnp.full(qb.shape[:-1], NEG_INF, f32), jnp.zeros(qb.shape[:-1], f32), jnp.zeros(qb.shape, f32))
        (_, l_s, acc_s), _ = lax.scan(slot, init, jnp.moveaxis(sel, -1, 0))
        o_s = acc_s / l_s[..., None]
        kw = lax.dynamic_slice_in_dim(kw_pad, q0, WINDOW + Q_BLOCK, axis=2)
        vw = lax.dynamic_slice_in_dim(vw_pad, q0, WINDOW + Q_BLOCK, axis=2)
        spos = q0 - WINDOW + win_off
        valid_w = (spos[None, :] <= tpos[:, None]) & (spos[None, :] > tpos[:, None] - WINDOW) & (spos[None, :] >= 0)
        s_w = jnp.einsum('bghqd,bgkd->bghqk', qb, kw) * scale
        p_w = jax.nn.softmax(jnp.where(valid_w, s_w, NEG_INF), axis=-1)
        o_w = jnp.einsum('bghqk,bgkd->bghqd', p_w, vw)
        return gb[..., 0:1] * o_c + gb[..., 1:2] * o_s + gb[..., 2:3] * o_w

    o = lax.map(block_fn, (q, gates, starts))
    o = o.transpose(1, 0, 4, 2, 3, 5).reshape(B, S, H * dh).astype(h.dtype)
    return jnp.einsum('bse,ed->bsd', o, w_out)

def hier_moe(h, w_group, b_group, w_router, b_router, w_gate, w_up, w_down):
    f32 = jnp.float32
    lg = jnp.einsum('bsd,dg->bsg', h, w_group).astype(f32) + b_group.astype(f32)
    pg = jax.nn.softmax(lg, axis=-1)
    g_onehot = jax.nn.one_hot(jnp.argmax(lg, axis=-1), MOE_GROUPS, dtype=f32)
    pg_top = jnp.sum(pg * g_onehot, axis=-1)
    le = jnp.einsum('bsd,de->bse', h, w_router).astype(f32) + b_router.astype(f32)
    le = le.reshape(h.shape[0], h.shape[1], MOE_GROUPS, MOE_EXPERTS_PER_GROUP)
    le_g = jnp.einsum('bsge,bsg->bse', le, g_onehot)
    top_v, top_i = lax.top_k(le_g, MOE_TOPK)
    w_sel = jax.nn.softmax(top_v, axis=-1) * pg_top[..., None]
    e_idx = jnp.argmax(g_onehot, axis=-1)[..., None] * MOE_EXPERTS_PER_GROUP + top_i
    gate = jnp.sum(jax.nn.one_hot(e_idx, MOE_EXPERTS, dtype=f32) * w_sel[..., None], axis=-2)

    def per_seq(args):
        xs, gs = args
        a = jnp.einsum('sd,edf->sef', xs, w_gate)
        u = jnp.einsum('sd,edf->sef', xs, w_up)
        hid = jax.nn.silu(a) * u * gs[..., None].astype(xs.dtype)
        return jnp.einsum('sef,efd->sd', hid, w_down)

    return lax.map(per_seq, (h, gate))

def setup_inputs(seed: int = 0) -> dict:
    key = jax.random.key(seed)
    ks = jax.random.split(key, 26)
    f32 = jnp.float32
    D = D_MODEL
    H, dk, dv = MLSTM_HEADS, MLSTM_QK_DIM, MLSTM_V_DIM
    G, dh = NSA_KV_GROUPS, NSA_HEAD_DIM
    E, F = MOE_EXPERTS, MOE_HIDDEN

    def nrm(k, shape, fan_in):
        return jax.random.normal(k, shape, f32) * (fan_in ** -0.5)

    def gain(k, shape):
        return 1.0 + 0.02 * jax.random.normal(k, shape, f32)

    n_in = 2 * H * dk + 2 * H * dv + 2 * H
    gate_base = jnp.concatenate([jnp.zeros((H,), f32), jnp.linspace(3.0, 6.0, H, dtype=f32)])
    return {
        'x': jax.random.normal(ks[0], (BATCH, SEQ, D), f32),
        'mlstm_norm': gain(ks[1], (N_A_LAYERS, D)),
        'mlstm_w_in': nrm(ks[2], (N_A_LAYERS, D, n_in), D),
        'mlstm_gate_bias': gate_base[None, :] + 0.1 * jax.random.normal(ks[3], (N_A_LAYERS, 2 * H), f32),
        'mlstm_head_norm': gain(ks[4], (N_A_LAYERS, H * dv)),
        'mlstm_w_out': nrm(ks[5], (N_A_LAYERS, H * dv, D), H * dv),
        'kv_norm': gain(ks[6], (D,)),
        'kv_w': nrm(ks[7], (D, 6 * G * dh), D),
        'cmp_pe_k': 0.02 * jax.random.normal(ks[8], (CMP_BLOCK, dh), f32),
        'cmp_w1_k': nrm(ks[9], (CMP_BLOCK * dh, dh), CMP_BLOCK * dh),
        'cmp_w2_k': nrm(ks[10], (dh, dh), dh),
        'cmp_pe_v': 0.02 * jax.random.normal(ks[11], (CMP_BLOCK, dh), f32),
        'cmp_w1_v': nrm(ks[12], (CMP_BLOCK * dh, dh), CMP_BLOCK * dh),
        'cmp_w2_v': nrm(ks[13], (dh, dh), dh),
        'nsa_norm': gain(ks[14], (N_B_LAYERS, D)),
        'nsa_w_q': nrm(ks[15], (N_B_LAYERS, D, NSA_HEADS * dh + 3 * NSA_HEADS), D),
        'nsa_w_out': nrm(ks[16], (N_B_LAYERS, NSA_HEADS * dh, D), NSA_HEADS * dh),
        'moe_norm': gain(ks[17], (DEPTH, D)),
        'moe_w_group': nrm(ks[18], (DEPTH, D, MOE_GROUPS), D),
        'moe_b_group': 0.01 * jax.random.normal(ks[19], (DEPTH, MOE_GROUPS), f32),
        'moe_w_router': nrm(ks[20], (DEPTH, D, E), D),
        'moe_b_router': 0.01 * jax.random.normal(ks[21], (DEPTH, E), f32),
        'moe_w_gate': nrm(ks[22], (DEPTH, E, D, F), D),
        'moe_w_up': nrm(ks[23], (DEPTH, E, D, F), D),
        'moe_w_down': nrm(ks[24], (DEPTH, E, F, D), F),
        'final_norm': gain(ks[25], (D,)),
    }

def reference(x, mlstm_norm, mlstm_w_in, mlstm_gate_bias, mlstm_head_norm, mlstm_w_out,
              kv_norm, kv_w, cmp_pe_k, cmp_w1_k, cmp_w2_k, cmp_pe_v, cmp_w1_v, cmp_w2_v,
              nsa_norm, nsa_w_q, nsa_w_out,
              moe_norm, moe_w_group, moe_b_group, moe_w_router, moe_b_router, moe_w_gate, moe_w_up, moe_w_down,
              final_norm):
    h = x
    shared = None
    for layer in range(DEPTH):
        if layer < N_A_LAYERS:
            i = layer
            h = h + mlstm_mixer(rmsnorm(h, mlstm_norm[i]), mlstm_w_in[i], mlstm_gate_bias[i],
                                mlstm_head_norm[i], mlstm_w_out[i])
        else:
            j = layer - N_A_LAYERS
            if j == 0:
                shared = nsa_shared_kv(h, kv_norm, kv_w, cmp_pe_k, cmp_w1_k, cmp_w2_k, cmp_pe_v, cmp_w1_v, cmp_w2_v)
            h = h + nsa_mixer(rmsnorm(h, nsa_norm[j]), nsa_w_q[j], nsa_w_out[j],
                              shared[0], shared[1], shared[2], shared[3], shared[4], shared[5])
        h = h + hier_moe(rmsnorm(h, moe_norm[layer]), moe_w_group[layer], moe_b_group[layer],
                         moe_w_router[layer], moe_b_router[layer], moe_w_gate[layer], moe_w_up[layer],
                         moe_w_down[layer])
    return rmsnorm(h, final_norm)


_drawn_inputs = setup_inputs


def setup_inputs(seed=0):
    import zlib

    import numpy as np

    out = dict(_drawn_inputs(seed))
    spreads = {}
    factors = {'kv_norm': 3.979,
     'cmp_pe_k': 8.0,
     'cmp_pe_v': 25.022,
     'nsa_norm': 8.0,
     'moe_b_group': 4.899,
     'moe_b_router': 3.901,
     'final_norm': 7.853}
    for name, (base, spread) in spreads.items():
        noise = np.random.default_rng([zlib.crc32(name.encode()), seed]).standard_normal(out[name].shape)
        drawn = base * np.exp(spread * noise) if base else spread * noise
        out[name] = __import__('jax').numpy.asarray(drawn.astype(out[name].dtype))
    for name, factor in factors.items():
        out[name] = (out[name] * factor).astype(out[name].dtype)
    return out
```

```python
from contextlib import ExitStack

import numpy as np
import concourse.bass as bass
from concourse import mybir

P = 128
D = 1024
S = 256
T = S // P
KT = D // P
EPS = 1e-6
NEG = -1e30
MH, MDK, MDV = 4, 128, 256
SOFTCAP = 15.0
NGATE = 2 * MH
O_GATES = 2 * MH * MDK + 2 * MH * MDV
NH, DH, NG = 16, 64, 4
HG = NH // NG
ROPE = DH // 4
HALF = ROPE // 2
THETA = 500000.0
CB, CS = 32, 16
NCMP = (S - CB) // CS + 1
NBR = 3
MG, ME = 4, 8
NE = MG * ME
F = D // 4
FT = F // P
NR = MG + NE
SLOTS = 2 * S
ST = SLOTS // P
WIN = 64
MAX_EXTRA = (SLOTS - 1) // WIN
PADDED = SLOTS + WIN
UC = 256
UNIT = KT * UC
RING = 12
U_A = 0
U_AOUT = 12
U_MOE = (16, 128)
U_N = 112
U_NOUT = 124
N_UNITS = 224
GROUP = 4
GPOS, UPOS, DPOS = (0, 2, 5, 8), (1, 3, 6, 9), (4, 7, 10, 11)
WINDOWS, REST = NE // GROUP, 3 * GROUP


def constants():
    f32 = np.float32
    row, col = np.arange(P)[:, None], np.arange(P)[None, :]
    inv = np.power(f32(THETA), -np.arange(HALF, dtype=f32) * f32(2.0 / ROPE)).astype(f32)

    def rope(pos):
        ang = (pos.astype(f32)[:, None] * inv[None, :]).astype(f32)
        c, s = np.cos(ang).astype(f32), np.sin(ang).astype(f32)
        return np.concatenate([c, c], 1), np.concatenate([-s, s], 1)

    c, s = rope(np.arange(S))
    tok = lambda a: a.reshape(T, P, -1).transpose(1, 0, 2).reshape(P, -1)
    cc, cs = rope(np.arange(NCMP) * CS + CB - 1)
    pad = lambda a: np.concatenate([a, np.zeros((P - a.shape[0], a.shape[1]), f32)])
    sel = np.zeros((P, MH, P), f32)
    for h in range(MH):
        sel[h, h] = 1
    ends = np.arange(NCMP) * CS + CB - 1
    ok = ends[None, :] <= np.arange(S)[:, None]
    parts = {
        "ident": np.eye(P), "mask_q": np.where(col > row, NEG, 0), "mask_k": np.where(col < row, NEG, 0),
        "before": row < col, "ones": np.ones((P, P)), "iota": np.tile(np.arange(SLOTS), (P, 1)),
        "cos": tok(c), "sin": tok(s), "ccos": pad(cc), "csin": pad(cs),
        "cmask": tok(np.where(ok, 0, NEG)), "cvalid": tok(ok.any(1)[:, None]),
        "sel": sel.reshape(P, -1), "ones_s": np.ones((P, S)), "desc": np.tile(np.arange(ME, 0, -1), (P, 1)),
    }
    at, place = 0, {}
    for name, a in parts.items():
        place[name] = (at, at + a.shape[1])
        at += a.shape[1]
    return np.ascontiguousarray(np.concatenate([np.asarray(a, f32) for a in parts.values()], 1)), place


def build(nc, x, mlstm_norm, mlstm_w_in, mlstm_gate_bias, mlstm_head_norm, mlstm_w_out, kv_norm, kv_w,
          cmp_pe_k, cmp_w1_k, cmp_w2_k, cmp_pe_v, cmp_w1_v, cmp_w2_v, nsa_norm, nsa_w_q, nsa_w_out,
          moe_norm, moe_w_group, moe_b_group, moe_w_router, moe_b_router, moe_w_gate, moe_w_up,
          moe_w_down, final_norm, consts, out, place, n_const):
    fp32, bf16, i32 = mybir.dt.float32, mybir.dt.bfloat16, mybir.dt.int32
    ALU, ACT, AX = mybir.AluOpType, mybir.ActivationFunctionType, mybir.AxisListType
    ds = bass.ds
    ctx = ExitStack()
    with ctx:
        def sb(name, shape, dt=fp32):
            return ctx.enter_context(nc.sbuf_tensor(name, shape, dt))

        def sem(name):
            return ctx.enter_context(nc.semaphore(name))

        const = sb("const", [P, n_const])
        ring = sb("ring", [P, RING, UNIT])
        h = sb("h", [P, T, D])
        xs = sb("xs", [P, T, KT, P])
        xT = [sb(f"xT{i}", [P, KT, S]) for i in range(2)]
        area = sb("area", [P, 16384])
        bank = [ctx.enter_context(nc.psum_tensor(f"bank{i}", [P, 512], fp32)) for i in range(8)]

        def c(name):
            return const[:, place[name][0]:place[name][1]]

        ident, ones, iota = c("ident"), c("ones"), c("iota")
        ident_b = sb("ident_b", [P, P], bf16)
        mask_qb = sb("mask_qb", [P, P], bf16)
        mask_kb = sb("mask_kb", [P, P], bf16)
        gains = sb("gains", [P, 6, KT])
        G_A, G_HEAD, G_KV, G_Q, G_MOE = 0, 1, 2, 3, 4
        w_mgate = sb("w_mgate", [P, KT, NGATE])
        b_mgate = sb("b_mgate", [P, NGATE])
        w_ngate = sb("w_ngate", [P, KT, NBR * NH])
        w_route = sb("w_route", [P, 2, KT, NR])
        b_route = sb("b_route", [P, 2, NR])
        pe_in = sb("pe_in", [CB, 2, DH])
        w_cmp2 = sb("w_cmp2", [DH, 2, DH])
        sq = sb("sq", [P, T])
        ms = sb("ms", [P, T])
        rstd = sb("rstd", [P, T])
        neghalf = sb("neghalf", [P, 8])

        def cut(a, b, shape=None, parts=P):
            v = area[0:parts, a:b]
            if shape:
                v = v.rearrange(shape[0], **shape[1])
            return v

        qkT = cut(0, 2048, ("p (u t) -> p u t", {"t": S}))
        vA = cut(2048, 4096, ("p (t h v) -> p t h v", {"t": T, "h": MH}))
        og = cut(4096, 6144, ("p (t h v) -> p t h v", {"t": T, "h": MH}))
        EA = cut(6144, 6912, ("p (b n) -> p b n", {"b": 2}))
        PA = cut(6912, 7680, ("p (b n) -> p b n", {"b": 2}))
        gA = [cut(7680 + i * S, 7680 + (i + 1) * S, parts=MH) for i in range(8)]
        hsA = cut(9728, 11776, ("p (t k q) -> p t k q", {"t": T, "k": KT}))
        tmpA = cut(11776, 13824, ("p (t h v) -> p t h v", {"t": T, "h": MH}))
        gpre = sb("gpre", [P, T, NGATE])
        a_col = sb("a_col", [P, T, MH])
        em_col = sb("em_col", [P, T, MH])
        ssA = sb("ssA", [P, T, MH])
        rA = sb("rA", [P, T, MH])
        uA = sb("uA", [P, T, MH])
        cA = sb("cA", [P, T, MH])
        KV = cut(0, 3072, ("p (t u n) -> p t u n", {"t": T, "u": 6}))
        QT = cut(3072, 5120, ("p (a j t) -> p a j t", {"a": 2, "j": HG}))
        KTn = cut(5120, 6144, ("p (b a t) -> p b a t", {"b": 2, "a": 2}))
        PN = cut(6144, 7168, ("p (b n) -> p b n", {"b": 2}))
        PTn = cut(7168, 8192, ("p (b n) -> p b n", {"b": 2}))
        QN = cut(8192, 10240, ("p (t a j r d) -> p t a j r d", {"t": T, "a": 2, "j": HG, "r": 2}))
        cT = cut(10240, 12800, ("p (b g t) -> p b g t", {"b": 2, "g": NG + 1}), parts=DH)
        PcT = cut(8192, 12288, ("p (h t) -> p h t", {"h": NH}), parts=NCMP)
        on = cut(12800, 14848, ("p (t k q) -> p t k q", {"t": T, "k": KT}))
        Pc = cut(14848, 15360, ("p (t h n) -> p t h n", {"t": T, "h": NH}))
        ngate = sb("ngate", [P, T, NH, NBR])
        rope_a = sb("rope_a", [P, T, 4, ROPE])
        rope_b = sb("rope_b", [P, T, 4, ROPE])
        c1 = sb("c1", [DH, NG * NCMP])
        c1e = sb("c1e", [DH, NG * NCMP])
        cbias = sb("cbias", [DH, 1])
        c1s = [sb(f"c1s{i}", [DH, NG * NCMP]) for i in range(2)]
        kcn = sb("kcn", [NCMP, NG, DH])
        vcn = sb("vcn", [NCMP, NG, DH])
        kcT = sb("kcT", [P, 2, NCMP])
        ccoef = sb("ccoef", [P, NH])
        nmax = sb("nmax", [P, 2, 2])
        lsum = sb("lsum", [P, 2, 2])
        ncoef = sb("ncoef", [P, 2, 2])
        Xs = cut(0, 4608, ("p (k n) -> p k n", {"k": KT}))
        Ys = cut(4608, 9216, ("p (k n) -> p k n", {"k": KT}))
        Yn = cut(9216, 13312, ("p (s n) -> p s n", {"s": ST}))
        Sel = cut(13312, 14336, ("p (t n) -> p t n", {"t": T}))
        Gm = cut(14336, 15360, ("p (t n) -> p t n", {"t": T}))
        GT = cut(15360, 16384, ("p (s n) -> p s n", {"s": ST}))
        spare = xT[1][:, :, :].rearrange("p k t -> p (k t)")
        xwin = spare[:, 0:1024].rearrange("p (b k n) -> p b k n", b=2, k=KT)
        sg = spare[:, 1024:1280].rearrange("p (b f n) -> p b f n", b=2, f=FT)
        hid = spare[:, 1280:1536].rearrange("p (b f n) -> p b f n", b=2, f=FT)
        lg = sb("lg", [P, T, NR])
        r4 = [sb(f"r4_{i}", [P, T, MG]) for i in range(2)]
        r8 = [sb(f"r8_{i}", [P, T, ME]) for i in range(4)]
        r32 = sb("r32", [P, T, ME, MG])
        hot = [sb(f"hot{i}", [P, T, NE]) for i in range(3)]
        place32 = sb("place32", [P, T, NE])
        prod32 = sb("prod32", [P, T, NE])
        cum = sb("cum", [P, NE])
        first = sb("first", [P, NE])
        one = [sb(f"one{i}", [P, T]) for i in range(10)]
        gexp = sb("gexp", [P, T, MG])
        table = sb("table", [1, 64], i32)
        T_COUNT, T_XFIRST, T_XID = 32, 40, 48
        n_max = sb("n_max", [1, 1])
        ex = [sb(f"ex{i}", [1, NE]) for i in range(4)]
        ex7 = [sb(f"ex7_{i}", [1, MAX_EXTRA, NE]) for i in range(3)]
        exr = [sb(f"exr{i}", [1, MAX_EXTRA]) for i in range(5)]
        gfin = cut(0, 1024)
        res = cut(1024, 3072, ("p (t n) -> p t n", {"t": T}))

        unit_in = [sem(f"unit_in{i}") for i in range(RING)]
        unit_used = sem("unit_used")
        x_in = sem("x_in")
        small_in = sem("small_in")
        gfin_in = sem("gfin_in")
        out_done = sem("out_done")
        h_ready = sem("h_ready")
        sq_ready = sem("sq_ready")
        ms_ready = sem("ms_ready")
        rstd_ready = sem("rstd_ready")
        xs_ready = sem("xs_ready")
        xt_done = sem("xt_done")
        xt_ready = sem("xt_ready")
        dve_step = sem("dve_step")
        act_step = sem("act_step")
        const_ready = sem("const_ready")
        dve_final = sem("dve_final")
        neghalf_ready = sem("neghalf_ready")
        mgate_done, mgate_ready, mgateT_done, tanh_ready = map(sem, ("mgate_done", "mgate_ready", "mgateT_done", "tanh_ready"))
        logf_ready, am_ready, col_done, col_ready = map(sem, ("logf_ready", "am_ready", "col_done", "col_ready"))
        em_ready = sem("em_ready")
        projA_read = sem("projA_read")
        og_ready = sem("og_ready")
        eA_done, eA_ready, sA_done, pA_ready, numA_done = map(sem, ("eA_done", "eA_ready", "sA_done", "pA_ready", "numA_done"))
        ssA_ready, uA_ready, powA_ready, hsA_ready, hsT_done, hsT_ready = map(sem, (
            "ssA_ready", "uA_ready", "powA_ready", "hsA_ready", "hsT_done", "hsT_ready"))
        projN_read = sem("projN_read")
        ngate_done, ngate_exp, ngate_read = map(sem, ("ngate_done", "ngate_exp", "ngate_read"))
        cT_done, cT_ready, c1_ready, c1_exp, c1s_ready, c2_done, c2_ready, kcT_done, kcT_ready = map(sem, (
            "cT_done", "cT_ready", "c1_ready", "c1_exp", "c1s_ready", "c2_done", "c2_ready", "kcT_done", "kcT_ready"))
        qkT_done, qkT_ready = sem("qkT_done"), sem("qkT_ready")
        sc_done, sc_ready, pc_exp, pc_ready, pcT_done, pcT_ready = map(sem, (
            "sc_done", "sc_ready", "pc_exp", "pc_ready", "pcT_done", "pcT_ready"))
        sN_done, mN_ready, eN_ready, pN_ready, ptN_done, ptN_v, ptN_a, oN_done, oN_read = map(sem, (
            "sN_done", "mN_ready", "eN_ready", "pN_ready", "ptN_done", "ptN_v", "ptN_a", "oN_done", "oN_read"))
        route_done, route_sub, route_exp, route_sub2, route_exp2, hot_ready, rank_done = map(sem, (
            "route_done", "route_sub", "route_exp", "route_sub2", "route_exp2", "hot_ready", "rank_done"))
        sel_ready, g_ready, gT_done, gT_ready, table_ready = map(sem, (
            "sel_ready", "g_ready", "gT_done", "gT_ready", "table_ready"))
        gather_done, gather_v, gather_a, pad_ready = map(sem, ("gather_done", "gather_v", "gather_a", "pad_ready"))
        win_ready, silu_ready, hid_ready, y_stored = map(sem, ("win_ready", "silu_ready", "hid_ready", "y_stored"))
        yT_done, yT_v, yT_a, comb_done = map(sem, ("yT_done", "yT_v", "yT_a", "comb_done"))
        extra = [{n: sem(f"x{n}{layer}") for n in ("table", "w", "win", "up", "silu", "hid", "down", "stored")}
                 for layer in range(2)]

        kpc = lambda w: w.rearrange("(p k) c -> p k c", k=KT)
        w_in, w_mout, w_kv, w_nq, w_nout = map(kpc, (mlstm_w_in[0], mlstm_w_out[0], kv_w, nsa_w_q[0], nsa_w_out[0]))
        pk = lambda g: g.rearrange("(p k) -> p k", k=KT)

        def unit(n):
            return ring[:, n % RING, :].rearrange("p (k c) -> p k c", k=KT)

        def arrived(eng, n, turn=0):
            eng.wait_ge(unit_in[n % RING], 16 * (n // RING + 1) + 16 * turn)

        block = ctx.enter_context(nc.Block())

        @block.sync
        def _(sp):
            sp.dma_start(h[:, 0, :], x[0, 0:P, :]).then_inc(x_in, 16)
            sp.dma_start(h[:, 1, :], x[0, P:S, :]).then_inc(x_in, 16)

            def load(n, src):
                if n >= RING:
                    sp.wait_ge(unit_used, n - RING + 1)
                sp.dma_start(unit(n), src).then_inc(unit_in[n % RING], 16)

            def load_moe(layer):
                base = U_MOE[layer]

                def group(i):
                    for j in range(GROUP):
                        jobs = [(GPOS[j], moe_w_gate, 0), (UPOS[j], moe_w_up, 0)]
                        if j:
                            jobs.append((DPOS[j - 1], moe_w_down, 1))
                        if j == GROUP - 1:
                            jobs.append((DPOS[j], moe_w_down, 0))
                        for pos, w, back in jobs:
                            n = base + pos
                            sp.wait_ge(unit_used, n - RING + 1 + REST * i)
                            e = i * GROUP + (j - back)
                            if w is moe_w_down:
                                src = w[layer, ds(e, 1)].rearrange("o (f p) d -> p (o f) d", p=P)
                                dst = ring[:, n % RING, :].rearrange("p (f d) -> p f d", f=FT)
                            else:
                                src = w[layer, ds(e, 1)].rearrange("o (p k) f -> p (o k) f", k=KT)
                                dst = unit(n)
                            sp.dma_start(dst, src).then_inc(unit_in[n % RING], 16)

                with sp.Fori(0, WINDOWS) as i:
                    group(i)
                sp.wait_ge(table_ready, layer + 1)
                n_top = sp.value_load(table[0:1, T_COUNT:T_COUNT + 1], min_val=0, max_val=S)
                q = extra[layer]
                with sp.If(n_top > WIN):
                    sp.wait_ge(unit_used, base + 3 * NE)
                    sp.wait_ge(q["table"], 1)

                    def again(j):
                        e = sp.value_load(table[0:1, ds(j + T_XID, 1)], min_val=0, max_val=NE - 1)
                        sp.dma_start(unit(0), moe_w_gate[layer, ds(e, 1)].rearrange("o (p k) f -> p (o k) f", k=KT)).then_inc(q["w"], 16)
                        sp.dma_start(unit(1), moe_w_up[layer, ds(e, 1)].rearrange("o (p k) f -> p (o k) f", k=KT)).then_inc(q["w"], 16)
                        sp.dma_start(ring[:, 2, :].rearrange("p (f d) -> p f d", f=FT),
                                     moe_w_down[layer, ds(e, 1)].rearrange("o (f p) d -> p (o f) d", p=P)).then_inc(q["w"], 16)

                    again(0)
                    with sp.Fori(1, MAX_EXTRA) as j:
                        sp.wait_ge(q["down"], j)
                        again(j)
                    sp.wait_ge(q["down"], MAX_EXTRA)

            for u in range(12):
                load(U_A + u, w_in[:, :, u * UC:(u + 1) * UC])
            for u in range(4):
                load(U_AOUT + u, w_mout[:, :, u * UC:(u + 1) * UC])
            load_moe(0)
            for u in range(2):
                load(U_N + u, w_kv[:, :, u * UC:(u + 1) * UC])
            for b, w in enumerate((cmp_w1_k, cmp_w1_v)):
                n = U_N + 2 + b
                sp.wait_ge(unit_used, n - RING + 1)
                sp.dma_start(ring[0:DH, n % RING, :].rearrange("d (l f) -> d l f", l=CB),
                             w.rearrange("(l d) f -> d l f", d=DH)).then_inc(unit_in[n % RING], 16)
            for u in range(2, 6):
                load(U_N + 2 + u, w_kv[:, :, u * UC:(u + 1) * UC])
            for u in range(4):
                load(U_N + 8 + u, w_nq[:, :, u * UC:(u + 1) * UC])
            for u in range(4):
                load(U_NOUT + u, w_nout[:, :, u * UC:(u + 1) * UC])
            load_moe(1)
            sp.wait_ge(h_ready, 16)
            sp.dma_start(gfin, final_norm.rearrange("(a n) -> a n", a=1).to_broadcast([P, D])).then_inc(gfin_in, 16)
            for t in range(T):
                sp.wait_ge(dve_final, t + 1)
                sp.dma_start(out[0, t * P:(t + 1) * P, :], res[:, t, :]).then_inc(out_done, 16)
            sp.wait_ge(out_done, 32)

        @block.gpsimd
        def _(pool):
            pool.memset(neghalf[:, :], -0.5).then_inc(neghalf_ready, 1)
            pool.wait_ge(neghalf_ready, 1)

            def rms(n):
                pool.wait_ge(ms_ready, n + 1)
                pool.tensor_tensor(rstd[:, :], ms[:, :], neghalf[:, 0:T], ALU.pow).then_inc(rstd_ready, 1)

            rms(0)
            pool.wait_ge(uA_ready, 1)
            pool.tensor_tensor(cA[:, :, :].rearrange("p t h -> p (t h)"), uA[:, :, :].rearrange("p t h -> p (t h)"),
                               neghalf[:, :], ALU.pow).then_inc(powA_ready, 1)
            for n in range(1, 5):
                rms(n)

        @block.scalar
        def _(act):
            smalls = [
                (gains[:, G_A, :], pk(mlstm_norm[0])), (gains[:, G_HEAD, :], pk(mlstm_head_norm[0])),
                (gains[:, G_KV, :], pk(kv_norm)), (gains[:, G_Q, :], pk(nsa_norm[0])),
                (gains[:, G_MOE, :], pk(moe_norm[0])), (gains[:, G_MOE + 1, :], pk(moe_norm[1])),
                (w_mgate[:, :, :], w_in[:, :, O_GATES:O_GATES + NGATE]),
                (b_mgate[:, :], mlstm_gate_bias[0:1, :].to_broadcast([P, NGATE])),
                (w_ngate[:, :, :], w_nq[:, :, NH * DH:NH * DH + NBR * NH]),
                (pe_in[:, 0, :], cmp_pe_k), (pe_in[:, 1, :], cmp_pe_v),
                (w_cmp2[:, 0, :], cmp_w2_k), (w_cmp2[:, 1, :], cmp_w2_v),
            ]
            for i in range(2):
                smalls += [
                    (w_route[:, i, :, 0:MG], kpc(moe_w_group[i])), (w_route[:, i, :, MG:NR], kpc(moe_w_router[i])),
                    (b_route[:, i, 0:MG], moe_b_group[i:i + 1, :].to_broadcast([P, MG])),
                    (b_route[:, i, MG:NR], moe_b_router[i:i + 1, :].to_broadcast([P, NE])),
                ]
            assert len(smalls) == N_SMALL - 1
            act.dma_start(const[:, :], consts).then_inc(small_in, 16)
            for dst, src in smalls:
                act.dma_start(dst, src).then_inc(small_in, 16)

            def squares(n):
                for t in range(T):
                    if n == 0:
                        act.wait_ge(x_in, 32)
                    else:
                        act.wait_ge(h_ready, 4 * n)
                    act.activation(xs[:, t, :, :].rearrange("p k q -> p (k q)"), h[:, t, :], ACT.Square,
                                   accum_out=sq[:, t:t + 1]).then_inc(sq_ready, 1)

            squares(0)
            act.wait_ge(mgateT_done, 4)
            act.activation(gA[0], bank[1][0:MH, 0:S], ACT.Tanh, scale=1.0 / SOFTCAP).then_inc(act_step, 1)
            act.activation(gA[1], bank[1][0:MH, S:2 * S], ACT.Tanh, scale=1.0 / SOFTCAP).then_inc(act_step, 1)
            act.wait_ge(act_step, 2)
            act.activation(gA[2], gA[1], ACT.Exp, scale=-SOFTCAP).then_inc(act_step, 1)
            act.wait_ge(act_step, 3)
            act.activation(gA[3], gA[2], ACT.Ln, bias=1.0).then_inc(logf_ready, 1)
            for u in range(8, 12):
                act.wait_ge(unit_used, U_A + u + 1)
                act.activation(og[:, :, u - 8, :], bank[4 + u % 4][:, :].rearrange("p (t v) -> p t v", t=T),
                               ACT.Tanh, scale=0.5).then_inc(og_ready, 1)
            act.wait_ge(col_ready, 2)
            act.activation(em_col[:, :, :], em_col[:, :, :], ACT.Exp, scale=-1.0).then_inc(em_ready, 1)
            for hd in range(MH):
                act.wait_ge(eA_done, hd + 1)
                if hd >= 2:
                    act.wait_ge(pA_ready, hd - 1)
                act.activation(EA[:, hd % 2, 0:S], bank[hd % 2][:, 0:S], ACT.Exp, bias=a_col[:, 0, hd:hd + 1]).then_inc(eA_ready, 1)
                act.activation(EA[:, hd % 2, S:S + P], bank[hd % 2][:, S:S + P], ACT.Exp, bias=a_col[:, 1, hd:hd + 1]).then_inc(eA_ready, 1)
            for hd in range(MH):
                for t in range(T):
                    act.wait_ge(numA_done, hd + 1)
                    act.activation(tmpA[:, t, hd, :], bank[4 + hd][:, t * MDV:(t + 1) * MDV], ACT.Square,
                                   accum_out=ssA[:, t, hd:hd + 1]).then_inc(ssA_ready, 1)

            def moe(layer):
                squares(2 * layer + 1)
                act.wait_ge(route_sub, layer + 1)
                act.activation(gexp[:, :, :], gexp[:, :, :], ACT.Exp).then_inc(route_exp, 1)
                act.wait_ge(route_sub2, layer + 1)
                act.activation(one[5][:, :], one[4][:, :], ACT.Exp).then_inc(route_exp2, 1)
                for k in range(1, KT, 2):
                    act.wait_ge(gather_done, KT * layer + k + 1)
                    act.activation(Xs[:, k, 0:SLOTS], bank[k % 4][:, :], ACT.Copy,
                                   scale=gains[:, G_MOE + layer, k:k + 1]).then_inc(gather_a, 1)
                base, e0 = U_MOE[layer], NE * layer
                act.wait_ge(gather_v, 4 * (layer + 1))
                act.wait_ge(gather_a, 4 * (layer + 1))
                act.wait_ge(pad_ready, layer + 1)
                act.wait_ge(table_ready, layer + 1)

                def window(i, j):
                    start = act.value_load(table[0:1, ds(i * GROUP + j, 1)], min_val=0, max_val=SLOTS)
                    act.activation(xwin[:, j % 2, :, :], Xs[:, :, ds(start, WIN)], ACT.Copy).then_inc(win_ready, 1)

                def silu(i, j):
                    act.wait_ge(unit_used, base + GPOS[j] + 1 + REST * i)
                    act.activation(sg[:, j % 2, :, :], bank[j % 2][:, 0:FT * WIN].rearrange("p (f n) -> p f n", f=FT),
                                   ACT.Silu).then_inc(silu_ready, 1)

                def group(i, firsts=False):
                    for j in range(GROUP):
                        if j >= 2:
                            act.wait_ge(unit_used, base + UPOS[j - 2] + 1 + REST * i)
                        elif not firsts:
                            act.wait_ge(unit_used, base + UPOS[j + 2] + 1 - REST + REST * i)
                        window(i, j)
                        if j:
                            if j - 1 >= 2 or not firsts:
                                act.wait_ge(hid_ready, e0 + j - 2 + GROUP * i)
                            silu(i, j - 1)
                    act.wait_ge(hid_ready, e0 + GROUP - 2 + GROUP * i)
                    silu(i, GROUP - 1)

                group(0, True)
                with act.Fori(1, WINDOWS) as i:
                    group(i)
                q = extra[layer]
                n_top = act.value_load(table[0:1, T_COUNT:T_COUNT + 1], min_val=0, max_val=S)
                with act.If(n_top > WIN):
                    act.wait_ge(q["table"], 1)
                    act.wait_ge(unit_used, base + 3 * NE)

                    def again(j):
                        start = act.value_load(table[0:1, ds(j + T_XFIRST, 1)], min_val=0, max_val=SLOTS)
                        act.activation(xwin[:, 0, :, :], Xs[:, :, ds(start, WIN)], ACT.Copy).then_inc(q["win"], 1)
                        act.wait_ge(q["up"], j + 1)
                        act.activation(sg[:, 0, :, :], bank[0][:, 0:FT * WIN].rearrange("p (f n) -> p f n", f=FT),
                                       ACT.Silu).then_inc(q["silu"], 1)

                    again(0)
                    with act.Fori(1, MAX_EXTRA) as j:
                        act.wait_ge(q["hid"], j)
                        again(j)
                for g in range(1, 2 * ST, 2):
                    act.wait_ge(yT_done, 2 * ST * layer + g + 1)
                    act.activation(Yn[:, g // 2, 512:1024], bank[(0, 1, 6, 7)[g % 4]][:, :], ACT.Copy).then_inc(yT_a, 1)

            moe(0)
            squares(2)
            act.wait_ge(c1_ready, 1)
            act.activation(c1e[:, :], c1[:, :], ACT.Exp, scale=-1.0).then_inc(c1_exp, 1)
            act.wait_ge(c1_ready, 2)
            act.activation(c1e[:, :], c1[:, :], ACT.Exp, scale=-1.0).then_inc(c1_exp, 1)
            act.wait_ge(ngate_done, 1)
            act.activation(ngate[:, :, :, :].rearrange("p t h b -> p t (h b)"),
                           bank[0][:, 0:2 * 64].rearrange("p (t n) -> p t n", t=T)[:, :, 0:NBR * NH],
                           ACT.Exp, scale=-1.0).then_inc(ngate_exp, 1)
            for t in range(T):
                act.wait_ge(sc_ready, t + 1)
                act.activation(Pc[:, t, :, 0:NCMP], Pc[:, t, :, 0:NCMP], ACT.Exp).then_inc(pc_exp, 1)

            def exps(u):
                n = P * (u // NH + 1)
                act.wait_ge(mN_ready, u + 1)
                if u >= 2:
                    act.wait_ge(ptN_done, u - 1)
                for b in range(2):
                    act.activation(PN[:, u % 2, b * n:(b + 1) * n], bank[u % 2][:, b * n:(b + 1) * n], ACT.Exp,
                                   bias=nmax[:, u % 2, b:b + 1], accum_out=lsum[:, u % 2, b:b + 1]).then_inc(eN_ready, 1)

            def evac(u):
                n = 2 * P * (u // NH + 1)
                act.wait_ge(ptN_done, u + 1)
                if u >= 2:
                    act.wait_ge(oN_done, u - 1)
                act.activation(PTn[:, u % 2, 0:n], bank[2 + u % 2][:, 0:n], ACT.Copy).then_inc(ptN_a, 1)

            exps(0)
            for u in range(1, T * NH):
                exps(u)
                evac(u - 1)
            evac(T * NH - 1)
            moe(1)
            squares(4)

        @block.vector
        def _(dve):
            steps = [0]

            def step(ins):
                steps[0] += 1
                ins.then_inc(dve_step, 1)
                dve.wait_ge(dve_step, steps[0])

            dve.wait_ge(small_in, 16 * N_SMALL)
            dve.tensor_copy(ident_b[:, :], ident).then_inc(const_ready, 1)
            dve.tensor_copy(mask_qb[:, :], c("mask_q")).then_inc(const_ready, 1)
            dve.tensor_copy(mask_kb[:, :], c("mask_k")).then_inc(const_ready, 1)

            def scale_rows(n):
                dve.wait_ge(sq_ready, T * (n + 1))
                dve.tensor_scalar(ms[:, :], sq[:, :], 1.0 / D, EPS, ALU.mult, ALU.add).then_inc(ms_ready, 1)
                dve.wait_ge(rstd_ready, n + 1)
                if n < 4:
                    for t in range(T):
                        dve.tensor_scalar(xs[:, t, :, :], h[:, t, :].rearrange("p (q k) -> p k q", k=KT),
                                          rstd[:, t:t + 1], None, ALU.mult).then_inc(xs_ready, 1)

            def evac_xT(done, gain_of, order):
                for b in range(4):
                    dve.wait_ge(xt_done, done + b + 1)
                    for i, g in enumerate(gain_of):
                        dve.tensor_tensor(xT[i][:, 2 * b:2 * b + 2, :], bank[b][:, :].rearrange("p (k t) -> p k t", k=2),
                                          gains[:, g, 2 * b:2 * b + 2].rearrange("p (k o) -> p k o", o=1).to_broadcast([P, 2, S]),
                                          ALU.mult).then_inc(xt_ready, 1)

            scale_rows(0)
            evac_xT(0, [G_A], None)
            dve.wait_ge(mgate_done, 1)
            dve.tensor_tensor(gpre[:, :, :], bank[0][:, 0:T * NGATE].rearrange("p (t n) -> p t n", t=T),
                              b_mgate[:, :].rearrange("p (o n) -> p o n", o=1).to_broadcast([P, T, NGATE]),
                              ALU.add).then_inc(mgate_ready, 1)

            def evac_projA(u):
                dve.wait_ge(unit_used, U_A + u + 1)
                src = bank[4 + u % 4][:, :].rearrange("p (a n) -> p a n", a=2)
                if u < 2:
                    ins = dve.tensor_copy(qkT[:, 2 * u:2 * u + 2, :], src)
                elif u < 4:
                    ins = dve.tensor_scalar(qkT[:, 2 * u:2 * u + 2, :], src, float(MDK) ** -0.5, None, ALU.mult)
                else:
                    ins = dve.tensor_copy(vA[:, :, u - 4, :], src)
                ins.then_inc(projA_read, 1)

            for u in range(4):
                evac_projA(u)
            ones_row = c("ones_s")[0:MH, :]
            dve.wait_ge(logf_ready, 1)
            step(dve.tensor_scalar(gA[3], gA[3], -1.0, None, ALU.mult))
            step(dve.tensor_tensor_scan(gA[4], ones_row, gA[3], 0.0, ALU.mult, ALU.add))
            step(dve.scalar_tensor_tensor(gA[5], gA[0], SOFTCAP, gA[4], ALU.mult, ALU.subtract))
            step(dve.tensor_tensor_scan(gA[6], ones_row, gA[5], 0.0, ALU.mult, ALU.max))
            step(dve.tensor_tensor(gA[7], gA[4], gA[6], ALU.add))
            dve.tensor_scalar(gA[6], gA[6], -1.0, None, ALU.mult).then_inc(am_ready, 1)
            for u in range(4, 8):
                evac_projA(u)
            dve.wait_ge(col_done, 1)
            dve.tensor_copy(a_col[:, :, :], bank[3][:, 0:8].rearrange("p (t h) -> p t h", t=T)).then_inc(col_ready, 1)
            dve.tensor_copy(em_col[:, :, :], bank[3][:, 8:16].rearrange("p (t h) -> p t h", t=T)).then_inc(col_ready, 1)
            for hd in range(MH):
                dve.wait_ge(eA_ready, 2 * hd + 2)
                dve.wait_ge(sA_done, hd + 1)
                if hd >= 2:
                    dve.wait_ge(numA_done, hd - 1)
                dve.tensor_tensor(PA[:, hd % 2, :], bank[2][:, 0:S + P], EA[:, hd % 2, :], ALU.mult).then_inc(pA_ready, 1)
            dve.wait_ge(og_ready, 4)
            dve.wait_ge(em_ready, 1)
            dve.wait_ge(numA_done, MH)
            den = bank[3][:, 16:24].rearrange("p (t h) -> p t h", t=T)
            step(dve.tensor_scalar(rA[:, :, :], den, -1.0, None, ALU.mult))
            step(dve.tensor_tensor(rA[:, :, :], den, rA[:, :, :], ALU.max))
            step(dve.tensor_tensor(rA[:, :, :], rA[:, :, :], em_col[:, :, :], ALU.max))
            step(dve.reciprocal(rA[:, :, :], rA[:, :, :]))
            dve.wait_ge(ssA_ready, T * MH)
            step(dve.tensor_tensor(uA[:, :, :], ssA[:, :, :], rA[:, :, :], ALU.mult))
            step(dve.tensor_tensor(uA[:, :, :], uA[:, :, :], rA[:, :, :], ALU.mult))
            step(dve.tensor_scalar(uA[:, :, :], uA[:, :, :], 1.0 / MDV, EPS, ALU.mult, ALU.add))
            dve.tensor_scalar(rA[:, :, :], rA[:, :, :], 0.5, None, ALU.mult).then_inc(uA_ready, 1)
            dve.wait_ge(uA_ready, 1)
            dve.wait_ge(powA_ready, 1)
            step(dve.tensor_tensor(cA[:, :, :], cA[:, :, :], rA[:, :, :], ALU.mult))
            for t in range(T):
                for hd in range(MH):
                    step(dve.scalar_tensor_tensor(tmpA[:, t, hd, :], og[:, t, hd, :], 1.0,
                                                  bank[4 + hd][:, t * MDV:(t + 1) * MDV], ALU.add, ALU.mult))
                    q = MDV // KT
                    dve.tensor_scalar(hsA[:, t, :, hd * q:(hd + 1) * q], tmpA[:, t, hd, :].rearrange("p (q k) -> p k q", k=KT),
                                      cA[:, t, hd:hd + 1], None, ALU.mult).then_inc(hsA_ready, 1)

            def evac_eT(first, gain):
                for b in range(4):
                    dve.wait_ge(hsT_done, first + b + 1)
                    src = bank[b][:, :].rearrange("p (k t) -> p k t", k=2)
                    if gain is None:
                        ins = dve.tensor_copy(xT[0][:, 2 * b:2 * b + 2, :], src)
                    else:
                        ins = dve.tensor_tensor(xT[0][:, 2 * b:2 * b + 2, :], src,
                                                gains[:, gain, 2 * b:2 * b + 2].rearrange("p (k o) -> p k o", o=1).to_broadcast([P, 2, S]),
                                                ALU.mult)
                    ins.then_inc(hsT_ready, 1)

            def add_out(first):
                for u in range(4):
                    dve.wait_ge(unit_used, first + u + 1)
                    dve.tensor_tensor(h[:, :, u * UC:(u + 1) * UC], bank[4 + u][:, :].rearrange("p (t n) -> p t n", t=T),
                                      h[:, :, u * UC:(u + 1) * UC], ALU.add).then_inc(h_ready, 1)

            evac_eT(0, G_HEAD)
            add_out(U_AOUT)

            def first_max(vals, top, onehot, key, n):
                step(dve.tensor_reduce(top, vals, AX.X, ALU.max))
                step(dve.tensor_tensor(key, vals, top.rearrange("p (t o) -> p t o", o=1).to_broadcast([P, T, n]), ALU.is_ge))
                step(dve.tensor_tensor(key, key, c("desc")[:, 0:n].rearrange("p (o n) -> p o n", o=1).to_broadcast([P, T, n]), ALU.mult))
                step(dve.tensor_reduce(one[9][:, :], key, AX.X, ALU.max))
                step(dve.tensor_tensor(onehot, key, one[9][:, :].rearrange("p (t o) -> p t o", o=1).to_broadcast([P, T, n]), ALU.is_ge))

            def moe(layer):
                scale_rows(2 * layer + 1)
                evac_xT((4, 12)[layer], [G_MOE + layer], None)
                dve.wait_ge(route_done, layer + 1)
                step(dve.tensor_tensor(lg[:, :, :], bank[4][:, 0:128].rearrange("p (t n) -> p t n", t=T)[:, :, 0:NR],
                                       b_route[:, layer:layer + 1, :].to_broadcast([P, T, NR]), ALU.add))
                first_max(lg[:, :, 0:MG], one[0][:, :], r4[0][:, :, :], r4[1][:, :, :], MG)
                dve.tensor_tensor(gexp[:, :, :], lg[:, :, 0:MG], one[0][:, :].rearrange("p (t o) -> p t o", o=1).to_broadcast([P, T, MG]),
                                  ALU.subtract).then_inc(route_sub, 1)
                for t in range(T):
                    dve.tensor_tensor(r32[:, t, :, :], lg[:, t, MG:NR].rearrange("p (g e) -> p e g", g=MG),
                                      r4[0][:, t:t + 1, :].to_broadcast([P, ME, MG]), ALU.mult).then_inc(dve_step, 1)
                steps[0] += T
                dve.wait_ge(dve_step, steps[0])
                step(dve.tensor_reduce(r8[0][:, :, :], r32[:, :, :, :], AX.X, ALU.add))
                first_max(r8[0][:, :, :], one[1][:, :], r8[1][:, :, :], r8[3][:, :, :], ME)
                step(dve.scalar_tensor_tensor(r8[2][:, :, :], r8[1][:, :, :], -3e38, r8[0][:, :, :], ALU.mult, ALU.add))
                first_max(r8[2][:, :, :], one[2][:, :], r8[0][:, :, :], r8[3][:, :, :], ME)
                dve.tensor_tensor(one[4][:, :], one[2][:, :], one[1][:, :], ALU.subtract).then_inc(route_sub2, 1)
                for t in range(T):
                    for i, r in ((0, r8[1]), (1, r8[0])):
                        dve.tensor_tensor(hot[i][:, t, :].rearrange("p (g e) -> p g e", g=MG),
                                          r4[0][:, t, :].rearrange("p (g o) -> p g o", o=1).to_broadcast([P, MG, ME]),
                                          r[:, t:t + 1, :].to_broadcast([P, MG, ME]), ALU.mult).then_inc(dve_step, 1)
                steps[0] += 2 * T
                dve.wait_ge(dve_step, steps[0])
                dve.tensor_tensor(hot[2][:, :, :], hot[0][:, :, :], hot[1][:, :, :], ALU.add).then_inc(hot_ready, 1)
                dve.wait_ge(route_exp, layer + 1)
                step(dve.tensor_reduce(one[3][:, :], gexp[:, :, :], AX.X, ALU.add))
                dve.wait_ge(route_exp2, layer + 1)
                step(dve.scalar_tensor_tensor(one[6][:, :], one[5][:, :], 1.0, one[3][:, :], ALU.add, ALU.mult))
                step(dve.reciprocal(one[6][:, :], one[6][:, :]))
                step(dve.tensor_tensor(one[7][:, :], one[6][:, :], one[5][:, :], ALU.mult))
                dve.wait_ge(rank_done, layer + 1)
                count = bank[5][:, 64:96]
                step(dve.tensor_copy(first[:, :], count))
                step(dve.tensor_tensor_scan(cum[:, :], ones[:, 0:NE], first[:, :], 0.0, ALU.mult, ALU.add))
                step(dve.tensor_reduce(n_max[:, :], first[0:1, :], AX.X, ALU.max))
                step(dve.tensor_tensor(first[:, :], cum[:, :], first[:, :], ALU.subtract))
                step(dve.tensor_copy(table[0:1, 0:NE], first[0:1, :]))
                dve.tensor_copy(table[0:1, T_COUNT:T_COUNT + 1], n_max[:, :]).then_inc(table_ready, 1)
                step(dve.tensor_tensor(place32[:, :, :], bank[5][:, 0:64].rearrange("p (t e) -> p t e", t=T),
                                       first[:, :].rearrange("p (o e) -> p o e", o=1).to_broadcast([P, T, NE]), ALU.add))
                for i in range(2):
                    step(dve.tensor_tensor(prod32[:, :, :], hot[i][:, :, :], place32[:, :, :], ALU.mult))
                    step(dve.tensor_reduce(one[i][:, :], prod32[:, :, :], AX.X, ALU.add))
                for t in range(T):
                    step(dve.tensor_scalar(Sel[:, t, :], iota, one[0][:, t:t + 1], None, ALU.is_equal))
                    dve.scalar_tensor_tensor(Sel[:, t, :], iota, one[1][:, t:t + 1], Sel[:, t, :], ALU.is_equal, ALU.add).then_inc(sel_ready, 1)
                for t in range(T):
                    step(dve.tensor_scalar(Gm[:, t, :], iota, one[0][:, t:t + 1], one[6][:, t:t + 1], ALU.is_equal, ALU.mult))
                    dve.tensor_scalar(Yn[:, t, 0:SLOTS], iota, one[1][:, t:t + 1], one[7][:, t:t + 1], ALU.is_equal, ALU.mult).then_inc(dve_step, 1)
                    steps[0] += 1
                    dve.wait_ge(dve_step, steps[0])
                    dve.tensor_tensor(Gm[:, t, :], Gm[:, t, :], Yn[:, t, 0:SLOTS], ALU.add).then_inc(g_ready, 1)
                dve.memset(Xs[:, :, SLOTS:PADDED], 0.0).then_inc(pad_ready, 1)
                for k in range(0, KT, 2):
                    dve.wait_ge(gather_done, KT * layer + k + 1)
                    dve.tensor_scalar(Xs[:, k, 0:SLOTS], bank[k % 4][:, :], gains[:, G_MOE + layer, k:k + 1], None,
                                      ALU.mult).then_inc(gather_v, 1)
                for b in range(2):
                    dve.wait_ge(gT_done, 2 * layer + b + 1)
                    dve.tensor_copy(GT[:, 2 * b:2 * b + 2, :], bank[6 + b][:, :].rearrange("p (s t) -> p s t", s=2)).then_inc(gT_ready, 1)
                base, e0 = U_MOE[layer], NE * layer

                def gated(i, j, firsts):
                    dve.wait_ge(silu_ready, e0 + j + 1 + GROUP * i)
                    dve.wait_ge(unit_used, base + UPOS[j] + 1 + REST * i)
                    if j >= 2:
                        dve.wait_ge(unit_used, base + DPOS[j - 2] + 1 + REST * i)
                    elif not firsts:
                        dve.wait_ge(unit_used, base + DPOS[j + 2] + 1 - REST + REST * i)
                    dve.tensor_tensor(hid[:, j % 2, :, :], bank[2 + j % 2][:, 0:FT * WIN].rearrange("p (f n) -> p f n", f=FT),
                                      sg[:, j % 2, :, :], ALU.mult).then_inc(hid_ready, 1)

                def store(i, j):
                    start = dve.value_load(table[0:1, ds(i * GROUP + j, 1)], min_val=0, max_val=SLOTS)
                    dve.wait_ge(unit_used, base + DPOS[j] + 1 + REST * i)
                    if layer or j or not isinstance(i, int):
                        dve.wait_ge(y_stored, e0 + j + GROUP * i)
                    dve.tensor_copy(Ys[:, :, ds(start, WIN)], bank[4 + j % 2][:, :].rearrange("p (k n) -> p k n", k=KT)).then_inc(y_stored, 1)

                def group(i, firsts=False):
                    for j in range(GROUP):
                        gated(i, j, firsts)
                        if j:
                            store(i, j - 1)
                    store(i, GROUP - 1)

                group(0, True)
                with dve.Fori(1, WINDOWS) as i:
                    group(i)
                q = extra[layer]
                n_top = dve.value_load(table[0:1, T_COUNT:T_COUNT + 1], min_val=0, max_val=S)
                with dve.If(n_top > WIN):
                    extras(layer, q)
                for g in range(0, 2 * ST, 2):
                    dve.wait_ge(yT_done, 2 * ST * layer + g + 1)
                    dve.tensor_copy(Yn[:, g // 2, 0:512], bank[(0, 1, 6, 7)[g % 4]][:, :]).then_inc(yT_v, 1)
                for t in range(T):
                    for b in range(2):
                        dve.wait_ge(comb_done, 4 * layer + 2 * t + b + 1)
                        dve.tensor_tensor(h[:, t, b * 512:(b + 1) * 512], bank[2 + 2 * t + b][:, :],
                                          h[:, t, b * 512:(b + 1) * 512], ALU.add).then_inc(h_ready, 1)

            def extras(layer, q):
                cnt, extra_of, before, tmp = (e[:, :] for e in ex)
                steps_in = [0]

                def xstep(ins):
                    steps_in[0] += 1
                    ins.then_inc(q["stored"], 1)
                    dve.wait_ge(q["stored"], steps_in[0])

                bc = lambda v: v.rearrange("p (o e) -> p o e", o=1).to_broadcast([1, MAX_EXTRA, NE])
                col = lambda v: v.rearrange("p (x o) -> p x o", o=1).to_broadcast([1, MAX_EXTRA, NE])
                xstep(dve.tensor_tensor(cnt, cum[0:1, :], first[0:1, :], ALU.subtract))
                xstep(dve.tensor_scalar(extra_of, cnt, float(WIN), None, ALU.is_gt))
                for m in range(2, S // WIN):
                    xstep(dve.scalar_tensor_tensor(extra_of, cnt, float(m * WIN), extra_of, ALU.is_gt, ALU.add))
                xstep(dve.tensor_tensor_scan(tmp, ones[0:1, 0:NE], extra_of, 0.0, ALU.mult, ALU.add))
                xstep(dve.tensor_tensor(before, tmp, extra_of, ALU.subtract))
                idx = iota[0:1, 0:MAX_EXTRA]
                mine, t0, t1 = (e[:, :, :] for e in ex7)
                xstep(dve.tensor_tensor(mine, bc(before), col(idx), ALU.is_le))
                xstep(dve.tensor_tensor(t0, bc(tmp), col(idx), ALU.is_gt))
                xstep(dve.tensor_tensor(mine, mine, t0, ALU.mult))
                eid, base_, nth, size, any_ = (e[:, :] for e in exr)
                for dst, src in ((eid, iota[0:1, 0:NE]), (base_, first[0:1, :]), (nth, before), (size, cnt)):
                    xstep(dve.tensor_tensor(t1, mine, bc(src), ALU.mult))
                    xstep(dve.tensor_reduce(dst, t1, AX.X, ALU.add))
                xstep(dve.tensor_reduce(any_, mine, AX.X, ALU.add))
                xstep(dve.tensor_tensor(nth, idx, nth, ALU.subtract))
                xstep(dve.tensor_scalar(nth, nth, 1.0, float(WIN), ALU.add, ALU.mult))
                xstep(dve.tensor_scalar(size, size, float(-WIN), None, ALU.add))
                xstep(dve.tensor_tensor(nth, nth, size, ALU.min))
                xstep(dve.tensor_tensor(base_, base_, nth, ALU.add))
                xstep(dve.tensor_scalar(base_, base_, float(-SLOTS), None, ALU.add))
                xstep(dve.tensor_tensor(base_, base_, any_, ALU.mult))
                xstep(dve.tensor_scalar(base_, base_, float(SLOTS), None, ALU.add))
                xstep(dve.tensor_copy(table[0:1, T_XFIRST:T_XFIRST + MAX_EXTRA], base_))
                dve.tensor_copy(table[0:1, T_XID:T_XID + MAX_EXTRA], eid).then_inc(q["table"], 1)
                dve.wait_ge(q["table"], 1)
                made = steps_in[0]
                assert made == XSTEPS

                def again(j):
                    start = dve.value_load(table[0:1, ds(j + T_XFIRST, 1)], min_val=0, max_val=SLOTS)
                    dve.wait_ge(q["silu"], j + 1)
                    dve.tensor_tensor(hid[:, 0, :, :], bank[2][:, 0:FT * WIN].rearrange("p (f n) -> p f n", f=FT),
                                      sg[:, 0, :, :], ALU.mult).then_inc(q["hid"], 1)
                    dve.wait_ge(q["down"], j + 1)
                    dve.wait_ge(q["stored"], made + j)
                    dve.tensor_copy(Ys[:, :, ds(start, WIN)], bank[4][:, :].rearrange("p (k n) -> p k n", k=KT)).then_inc(q["stored"], 1)

                dve.wait_ge(y_stored, NE * (layer + 1))
                again(0)
                with dve.Fori(1, MAX_EXTRA) as j:
                    again(j)

            moe(0)
            scale_rows(2)
            evac_xT(8, [G_KV, G_Q], None)
            dve.memset(cT[:, :, NG, :], 0.0).then_inc(dve_step, 1)
            steps[0] += 1

            def evac_kv(u):
                n = U_N + (u if u < 2 else u + 2)
                dve.wait_ge(unit_used, n + 1)
                src = bank[4 + u % 4][:, :].rearrange("p (t n) -> p t n", t=T)
                ins = dve.tensor_copy(KV[:, :, u, :], src)
                if u in (2, 4):
                    step(ins)
                    dst = KV[:, :, u, :].rearrange("p t (g d) -> p t g d", g=NG)
                    turn(dst)
                else:
                    ins.then_inc(projN_read, 1)

            def turn(x4):
                bc = lambda name: c(name).rearrange("p (t o n) -> p t o n", t=T, o=1).to_broadcast([P, T, 4, ROPE])
                cos, sin = bc("cos"), bc("sin")
                dve.tensor_tensor(rope_a[:, :, :, :], x4[:, :, :, 0:ROPE], cos, ALU.mult).then_inc(dve_step, 1)
                dve.tensor_tensor(rope_b[:, :, :, 0:HALF], x4[:, :, :, HALF:ROPE], sin[:, :, :, 0:HALF], ALU.mult).then_inc(dve_step, 1)
                dve.tensor_tensor(rope_b[:, :, :, HALF:ROPE], x4[:, :, :, 0:HALF], sin[:, :, :, HALF:ROPE], ALU.mult).then_inc(dve_step, 1)
                steps[0] += 3
                dve.wait_ge(dve_step, steps[0])
                dve.tensor_tensor(x4[:, :, :, 0:ROPE], rope_a[:, :, :, :], rope_b[:, :, :, :], ALU.add).then_inc(projN_read, 1)

            evac_kv(0)
            evac_kv(1)
            dve.wait_ge(dve_step, steps[0])
            for b in range(2):
                for half in range(2):
                    dve.wait_ge(cT_done, 2 * b + half + 1)
                    dve.tensor_copy(cT[:, b, 2 * half:2 * half + 2, :],
                                    bank[2 * b + half][0:DH, :].rearrange("p (g t) -> p g t", g=2)).then_inc(cT_ready, 1)
            dve.wait_ge(cT_done, 5)
            dve.tensor_copy(cT[:, :, NG, 0:CB], bank[6][0:DH, 0:2 * CB].rearrange("p (b l) -> p b l", b=2)).then_inc(cT_ready, 1)
            for b in range(2):
                dve.wait_ge(unit_used, U_N + 2 + b + 1)
                if b:
                    dve.wait_ge(c1s_ready, 1)
                step(dve.tensor_copy(cbias[:, :], bank[4 + b][0:DH, NG * NCMP:NG * NCMP + 1]))
                dve.tensor_scalar(c1[:, :], bank[4 + b][0:DH, 0:NG * NCMP], cbias[:, 0:1], None, ALU.add).then_inc(c1_ready, 1)
                dve.wait_ge(c1_exp, b + 1)
                step(dve.tensor_scalar(c1e[:, :], c1e[:, :], 1.0, None, ALU.add))
                step(dve.reciprocal(c1e[:, :], c1e[:, :]))
                dve.tensor_tensor(c1s[b][:, :], c1[:, :], c1e[:, :], ALU.mult).then_inc(c1s_ready, 1)
            for u in range(2, 6):
                evac_kv(u)
            dve.wait_ge(c2_done, 1)
            step(dve.tensor_copy(kcn[:, :, :], bank[0][0:NCMP, 0:NG * DH].rearrange("p (g d) -> p g d", g=NG)))
            bc = lambda name: c(name)[0:NCMP, :].rearrange("p (o n) -> p o n", o=1).to_broadcast([NCMP, NG, ROPE])
            ra, rb = rope_a[0:NCMP, 0, :, :], rope_b[0:NCMP, 0, :, :]
            dve.wait_ge(projN_read, 6)
            step(dve.tensor_tensor(ra, kcn[:, :, 0:ROPE], bc("ccos"), ALU.mult))
            step(dve.tensor_tensor(rb[:, :, 0:HALF], kcn[:, :, HALF:ROPE], bc("csin")[:, :, 0:HALF], ALU.mult))
            step(dve.tensor_tensor(rb[:, :, HALF:ROPE], kcn[:, :, 0:HALF], bc("csin")[:, :, HALF:ROPE], ALU.mult))
            dve.tensor_tensor(kcn[:, :, 0:ROPE], ra, rb, ALU.add).then_inc(c2_ready, 1)
            dve.wait_ge(c2_done, 2)
            dve.tensor_copy(vcn[:, :, :], bank[1][0:NCMP, 0:NG * DH].rearrange("p (g d) -> p g d", g=NG)).then_inc(c2_ready, 1)
            dve.wait_ge(kcT_done, 1)
            dve.tensor_copy(kcT[:, :, :], bank[2][:, 0:2 * NCMP].rearrange("p (a n) -> p a n", a=2)).then_inc(kcT_ready, 1)
            dve.wait_ge(c2_ready, 1)
            for u in range(4):
                dve.wait_ge(unit_used, U_N + 8 + u + 1)
                x4 = QN[:, :, u // 2, :, u % 2, :]
                step(dve.tensor_scalar(x4, bank[4 + (u + 6) % 4][:, :].rearrange("p (t h d) -> p t h d", t=T, h=4),
                                       float(DH) ** -0.5, None, ALU.mult))
                turn(x4)
                if u == 0:
                    dve.wait_ge(ngate_exp, 1)
                    g = ngate[:, :, :, :].rearrange("p t h b -> p (t h b)")
                    step(dve.tensor_scalar(g, g, 1.0, None, ALU.add))
                    step(dve.reciprocal(g, g))
            for i in range(6):
                dve.wait_ge(qkT_done, i + 1)
                if i < 2:
                    dst = KTn[:, i, :, :]
                else:
                    dst = QT[:, (i - 2) // 2, 2 * (i % 2):2 * (i % 2) + 2, :]
                dve.tensor_copy(dst, bank[i % 4][:, :].rearrange("p (a t) -> p a t", a=2)).then_inc(qkT_ready, 1)
            for t in range(T):
                dve.wait_ge(sc_done, t + 1)
                pc = Pc[:, t, :, 0:NCMP]
                for r in range(2):
                    step(dve.tensor_tensor(Pc[:, t, :, :].rearrange("p (a r j) n -> p r a j n", a=2, r=2)[:, r, :, :, 0:NCMP],
                                           bank[4 + 2 * t + r][:, 0:NH * 8].rearrange("p (a j n) -> p a j n", a=2, j=HG)[:, :, :, 0:NCMP],
                                           c("cmask")[:, t * NCMP:(t + 1) * NCMP].rearrange("p (o q n) -> p o q n", o=1, q=1)
                                           .to_broadcast([P, 2, HG, NCMP]), ALU.add))
                step(dve.tensor_reduce(ccoef[:, :], pc, AX.X, ALU.max))
                bcc = ccoef[:, :].rearrange("p (h o) -> p h o", o=1).to_broadcast([P, NH, NCMP])
                dve.tensor_tensor(pc, pc, bcc, ALU.subtract).then_inc(sc_ready, 1)
                dve.wait_ge(pc_exp, t + 1)
                step(dve.tensor_reduce(ccoef[:, :], pc, AX.X, ALU.add))
                step(dve.reciprocal(ccoef[:, :], ccoef[:, :]))
                step(dve.scalar_tensor_tensor(ccoef[:, :], ccoef[:, :], c("cvalid")[:, t:t + 1], ngate[:, t, :, 0], ALU.mult, ALU.mult))
                dve.tensor_tensor(pc, pc, bcc, ALU.mult).then_inc(pc_ready, 1)
                dve.wait_ge(pc_ready, t + 1)
            for i in range(8):
                dve.wait_ge(pcT_done, i + 1)
                dve.tensor_copy(PcT[:, 4 * (i % 4):4 * (i % 4) + 4, (i // 4) * P:(i // 4 + 1) * P],
                                bank[i % 4][0:NCMP, :].rearrange("p (h t) -> p h t", h=4)).then_inc(pcT_ready, 1)

            def maxima(u):
                n = P * (u // NH + 1)
                dve.wait_ge(sN_done, u + 1)
                if u >= 2:
                    dve.wait_ge(eN_ready, 2 * (u - 1))
                dve.tensor_reduce(nmax[:, u % 2, :], bank[u % 2][:, 0:2 * n].rearrange("p (b n) -> p b n", b=2), AX.X, ALU.max,
                                  negate=True).then_inc(mN_ready, 1)

            def normalise(u):
                t, hd = u // NH, u % NH
                n = P * (t + 1)
                dve.wait_ge(eN_ready, 2 * (u + 1))
                step(dve.reciprocal(ncoef[:, u % 2, :], lsum[:, u % 2, :]))
                step(dve.tensor_tensor(ncoef[:, u % 2, :], ncoef[:, u % 2, :], ngate[:, t, hd, 1:3], ALU.mult))
                for b in range(2):
                    dve.tensor_scalar(PN[:, u % 2, b * n:(b + 1) * n], PN[:, u % 2, b * n:(b + 1) * n],
                                      ncoef[:, u % 2, b:b + 1], None, ALU.mult).then_inc(pN_ready, 1)

            maxima(0)
            for u in range(T * NH):
                if u + 1 < T * NH:
                    maxima(u + 1)
                normalise(u)
                if u % 8 == 7:
                    b = u // 8
                    dve.wait_ge(oN_done, u + 1)
                    dve.tensor_copy(on[:, b // 2, :, 64 * (b % 2):64 * (b % 2) + 64],
                                    bank[4 + b][:, :].rearrange("p (q k) -> p k q", k=KT)).then_inc(oN_read, 1)
            evac_eT(4, None)
            add_out(U_NOUT)
            moe(1)
            scale_rows(4)
            dve.wait_ge(gfin_in, 16)
            for t in range(T):
                dve.scalar_tensor_tensor(res[:, t, :], h[:, t, :], rstd[:, t:t + 1], gfin, ALU.mult, ALU.mult).then_inc(dve_final, 1)

        @block.tensor
        def _(pe):
            mm = nc.tensor.matmul

            def transposes(src, n_ready, ready, done):
                pe.wait_ge(ready, n_ready)
                for b in range(4):
                    for k in (2 * b, 2 * b + 1):
                        for t in range(T):
                            last = nc.tensor.transpose(bank[b][:, (k % 2) * S + t * P:(k % 2) * S + (t + 1) * P],
                                                       src[:, t, k, :], ident)
                    last.then_inc(done, 1)

            def rows(n, xt, b, last=True):
                w = unit(n)
                arrived(pe, n)
                for t in range(T):
                    for k in range(KT):
                        ins = mm(bank[b][:, t * UC:(t + 1) * UC], xt[:, k, t * P:(t + 1) * P], w[:, k, :],
                                 start=(k == 0), stop=(k == KT - 1))
                ins.then_inc(unit_used, 1)

            pe.wait_ge(small_in, 16 * N_SMALL)
            transposes(xs, 2, xs_ready, xt_done)
            pe.wait_ge(xt_ready, 4)
            for t in range(T):
                for k in range(KT):
                    ins = mm(bank[0][:, t * NGATE:(t + 1) * NGATE], xT[0][:, k, t * P:(t + 1) * P], w_mgate[:, k, :],
                             start=(k == 0), stop=(k == KT - 1))
            ins.then_inc(mgate_done, 1)
            for u in range(4):
                arrived(pe, u)
                w = unit(u)
                for j in range(2):
                    for k in range(KT):
                        ins = mm(bank[4 + u][:, j * S:(j + 1) * S], w[:, k, j * P:(j + 1) * P], xT[0][:, k, :],
                                 start=(k == 0), stop=(k == KT - 1))
                ins.then_inc(unit_used, 1)
                if u == 0:
                    pe.wait_ge(mgate_ready, 1)
                    for i in range(2):
                        for t in range(T):
                            nc.tensor.transpose(bank[1][0:MH, i * S + t * P:i * S + (t + 1) * P],
                                                gpre[:, t, i * MH:(i + 1) * MH], ident).then_inc(mgateT_done, 1)
            for u in range(4, 12):
                pe.wait_ge(projA_read, u - 3)
                rows(u, xT[0], 4 + u % 4)
            pe.wait_ge(am_ready, 1)
            for i, g in enumerate((gA[5], gA[7])):
                for t in range(T):
                    ins = nc.tensor.transpose(bank[3][:, 8 * i + MH * t:8 * i + MH * (t + 1)], g[:, t * P:(t + 1) * P],
                                              ident[0:MH, 0:MH])
            ins.then_inc(col_done, 1)
            pe.wait_ge(const_ready, 3)
            sel = c("sel").rearrange("p (h m) -> p h m", h=MH)

            def exponents(hd):
                if hd >= 2:
                    pe.wait_ge(eA_ready, 2 * (hd - 1))
                b = bank[hd % 2]
                mm(b[:, 0:S], sel[0:MH, hd, :], gA[6][:, 0:S], start=True, stop=True)
                mm(b[:, 0:P], ident_b[:, :], mask_kb[:, :], start=False, stop=True, skip_group_check=True)
                mm(b[:, S:S + P], sel[0:MH, hd, :], gA[6][:, P:S], start=True, stop=True)
                mm(b[:, S:S + P], ident_b[:, :], mask_kb[:, :], start=False, stop=True, skip_group_check=True).then_inc(eA_done, 1)

            exponents(0)
            pe.wait_ge(col_ready, 2)
            pe.wait_ge(og_ready, 4)
            pe.wait_ge(projA_read, 8)
            for hd in range(MH):
                if hd + 1 < MH:
                    exponents(hd + 1)
                if hd:
                    pe.wait_ge(pA_ready, hd)
                mm(bank[2][:, 0:S], qkT[:, MH + hd, 0:P], qkT[:, hd, :], start=True, stop=True)
                mm(bank[2][:, S:S + P], qkT[:, MH + hd, P:S], qkT[:, hd, P:S], start=True, stop=True).then_inc(sA_done, 1)
                pe.wait_ge(pA_ready, hd + 1)
                p = PA[:, hd % 2, :]
                for t, tiles in ((0, [(0, 0)]), (1, [(P, 0), (S, 1)])):
                    for n, (at, s) in enumerate(tiles):
                        mm(bank[4 + hd][:, t * MDV:(t + 1) * MDV], p[:, at:at + P], vA[:, s, hd, :],
                           start=(n == 0), stop=(n == t))
                    for n, (at, s) in enumerate(tiles):
                        ins = mm(bank[3][:, 16 + t * MH + hd:17 + t * MH + hd], p[:, at:at + P], ones[:, 0:1],
                                 start=(n == 0), stop=(n == t))
                ins.then_inc(numA_done, 1)
            transposes(hsA, T * MH, hsA_ready, hsT_done)
            pe.wait_ge(hsT_ready, 4)
            for u in range(4):
                rows(U_AOUT + u, xT[0], 4 + u)

            def moe(layer):
                g = G_MOE + layer
                transposes(xs, 2 * (2 * layer + 2), xs_ready, xt_done)
                pe.wait_ge(xt_ready, (8, 20)[layer])
                for t in range(T):
                    for k in range(KT):
                        ins = mm(bank[4][:, t * 64:t * 64 + NR], xT[0][:, k, t * P:(t + 1) * P], w_route[:, layer, k, :],
                                 start=(k == 0), stop=(k == KT - 1))
                ins.then_inc(route_done, 1)
                pe.wait_ge(hot_ready, layer + 1)
                before = c("before")
                mm(bank[5][:, 0:NE], before, hot[2][:, 0, :], start=True, stop=True)
                mm(bank[5][:, NE:2 * NE], ones, hot[2][:, 0, :], start=True, stop=False)
                mm(bank[5][:, NE:2 * NE], before, hot[2][:, 1, :], start=False, stop=True)
                mm(bank[5][:, 2 * NE:3 * NE], ones, hot[2][:, 0, :], start=True, stop=False)
                mm(bank[5][:, 2 * NE:3 * NE], ones, hot[2][:, 1, :], start=False, stop=True).then_inc(rank_done, 1)
                pe.wait_ge(sel_ready, 2 * (layer + 1))
                for k in range(KT):
                    if k >= 4:
                        pe.wait_ge(*((gather_a, 4 * layer + (k - 4) // 2 + 1) if k % 2 else (gather_v, 4 * layer + (k - 4) // 2 + 1)))
                    for t in range(T):
                        ins = mm(bank[k % 4][:, :], xs[:, t, k, :], Sel[:, t, :], start=(t == 0), stop=(t == T - 1))
                    ins.then_inc(gather_done, 1)
                pe.wait_ge(g_ready, 2 * (layer + 1))
                for b in range(2):
                    for s in (2 * b, 2 * b + 1):
                        for t in range(T):
                            ins = nc.tensor.transpose(bank[6 + b][:, (s % 2) * S + t * P:(s % 2) * S + (t + 1) * P],
                                                      Gm[:, t, s * P:(s + 1) * P], ident)
                    ins.then_inc(gT_done, 1)
                pe.wait_ge(gather_v, 4 * (layer + 1))
                pe.wait_ge(gather_a, 4 * (layer + 1))
                base, e0 = U_MOE[layer], NE * layer

                def up(w, b, xw):
                    for f in range(FT):
                        for k in range(KT):
                            ins = mm(bank[b][:, f * WIN:(f + 1) * WIN], w[:, k, f * P:(f + 1) * P], xw[:, k, :],
                                     start=(k == 0), stop=(k == KT - 1))
                    return ins

                def down(w, b, hd):
                    for m in range(KT):
                        for f in range(FT):
                            ins = mm(bank[b][:, m * WIN:(m + 1) * WIN], w[:, f, m * P:(m + 1) * P], hd[:, f, :],
                                     start=(f == 0), stop=(f == FT - 1))
                    return ins

                def gate_up(i, j, firsts):
                    pe.wait_ge(win_ready, e0 + j + 1 + GROUP * i)
                    if j >= 2 or not firsts:
                        pe.wait_ge(silu_ready, e0 + j - 1 + GROUP * i)
                    arrived(pe, base + GPOS[j], i)
                    up(unit(base + GPOS[j]), j % 2, xwin[:, j % 2, :, :]).then_inc(unit_used, 1)
                    if j >= 2 or not firsts:
                        pe.wait_ge(hid_ready, e0 + j - 1 + GROUP * i)
                    arrived(pe, base + UPOS[j], i)
                    up(unit(base + UPOS[j]), 2 + j % 2, xwin[:, j % 2, :, :]).then_inc(unit_used, 1)

                def downs(i, j, firsts):
                    pe.wait_ge(hid_ready, e0 + j + 1 + GROUP * i)
                    if j >= 2 or not firsts:
                        pe.wait_ge(y_stored, e0 + j - 1 + GROUP * i)
                    arrived(pe, base + DPOS[j], i)
                    w = ring[:, (base + DPOS[j]) % RING, :].rearrange("p (f d) -> p f d", f=FT)
                    down(w, 4 + j % 2, hid[:, j % 2, :, :]).then_inc(unit_used, 1)

                def group(i, firsts=False):
                    for j in range(GROUP):
                        gate_up(i, j, firsts)
                        if j:
                            downs(i, j - 1, firsts)
                    downs(i, GROUP - 1, firsts)

                group(0, True)
                with pe.Fori(1, WINDOWS) as i:
                    group(i)
                q = extra[layer]
                pe.wait_ge(table_ready, layer + 1)
                n_top = pe.value_load(table[0:1, T_COUNT:T_COUNT + 1], min_val=0, max_val=S)
                with pe.If(n_top > WIN):
                    def again(j):
                        pe.wait_ge(q["w"], 48 * j + 48)
                        pe.wait_ge(q["win"], j + 1)
                        up(unit(0), 0, xwin[:, 0, :, :])
                        up(unit(1), 2, xwin[:, 0, :, :]).then_inc(q["up"], 1)
                        pe.wait_ge(q["hid"], j + 1)
                        pe.wait_ge(q["stored"], XSTEPS + j)
                        down(ring[:, 2, :].rearrange("p (f d) -> p f d", f=FT), 4, hid[:, 0, :, :]).then_inc(q["down"], 1)

                    pe.wait_ge(y_stored, NE * (layer + 1))
                    again(0)
                    with pe.Fori(1, MAX_EXTRA) as j:
                        again(j)
                    pe.wait_ge(q["stored"], XSTEPS + MAX_EXTRA)
                pe.wait_ge(y_stored, NE * (layer + 1))
                pe.wait_ge(gT_ready, 2 * (layer + 1))
                for gi in range(2 * ST):
                    b = (0, 1, 6, 7)[gi % 4]
                    if gi >= 4:
                        pe.wait_ge(*((yT_a, ST * layer + (gi - 4) // 2 + 1) if gi % 2 else (yT_v, ST * layer + (gi - 4) // 2 + 1)))
                    for m in range(4):
                        k = 4 * (gi % 2) + m
                        ins = nc.tensor.transpose(bank[b][:, m * P:(m + 1) * P], Ys[:, k, (gi // 2) * P:(gi // 2 + 1) * P], ident)
                    ins.then_inc(yT_done, 1)
                pe.wait_ge(yT_v, ST * (layer + 1))
                pe.wait_ge(yT_a, ST * (layer + 1))
                for t in range(T):
                    for b in range(2):
                        for s in range(ST):
                            ins = mm(bank[2 + 2 * t + b][:, :], GT[:, s, t * P:(t + 1) * P], Yn[:, s, b * 512:(b + 1) * 512],
                                     start=(s == 0), stop=(s == ST - 1))
                        ins.then_inc(comb_done, 1)

            moe(0)
            transposes(xs, 6, xs_ready, xt_done)
            pe.wait_ge(xt_ready, 16)
            for u in range(2):
                rows(U_N + u, xT[0], 4 + u)
            pe.wait_ge(projN_read, 2)
            for b in range(2):
                for half in range(2):
                    for g in (2 * half, 2 * half + 1):
                        for t in range(T):
                            ins = nc.tensor.transpose(bank[2 * b + half][0:DH, (g % 2) * S + t * P:(g % 2) * S + (t + 1) * P],
                                                      KV[:, t, b, g * DH:(g + 1) * DH], ident)
                    ins.then_inc(cT_done, 1)
            for b in range(2):
                ins = nc.tensor.transpose(bank[6][0:DH, b * CB:(b + 1) * CB], pe_in[:, b, :], ident[0:CB, 0:CB])
            ins.then_inc(cT_done, 1)
            pe.wait_ge(cT_ready, 5)
            for b in range(2):
                n = U_N + 2 + b
                arrived(pe, n)
                w = ring[0:DH, n % RING, :].rearrange("d (l f) -> d l f", l=CB)
                for l in range(CB):
                    ins = mm(bank[4 + b][0:DH, 0:(NG + 1) * NCMP].rearrange("p (g n) -> p g n", g=NG + 1), w[:, l, :],
                             cT[:, b, :, l:l + CS * (NCMP - 1) + 1:CS], start=(l == 0), stop=(l == CB - 1))
                ins.then_inc(unit_used, 1)
            for u in range(2, 6):
                if u >= 4:
                    pe.wait_ge(projN_read, u - 1)
                    pe.wait_ge(c1_ready, u - 3)
                rows(U_N + 2 + u, xT[0], 4 + u % 4)
                if u >= 4:
                    b = u - 4
                    pe.wait_ge(c1s_ready, b + 1)
                    for g in range(NG):
                        ins = mm(bank[b][0:NCMP, g * DH:(g + 1) * DH], c1s[b][:, g * NCMP:(g + 1) * NCMP], w_cmp2[:, b, :],
                                 start=True, stop=True)
                    ins.then_inc(c2_done, 1)
            pe.wait_ge(c2_ready, 2)
            for a in range(2):
                ins = nc.tensor.transpose(bank[2][:, a * NCMP:(a + 1) * NCMP],
                                          kcn[:, 2 * a:2 * a + 2, :].rearrange("p g d -> p (g d)"), ident[0:NCMP, 0:NCMP])
            ins.then_inc(kcT_done, 1)
            for t in range(T):
                for k in range(KT):
                    ins = mm(bank[0][:, t * 64:t * 64 + NBR * NH], xT[1][:, k, t * P:(t + 1) * P], w_ngate[:, k, :],
                             start=(k == 0), stop=(k == KT - 1))
            ins.then_inc(ngate_done, 1)
            for u in range(4):
                pe.wait_ge(projN_read, u + 3)
                rows(U_N + 8 + u, xT[1], 4 + (u + 6) % 4)
            pe.wait_ge(kcT_ready, 1)
            pe.wait_ge(ngate_exp, 1)
            for i in range(6):
                if i >= 4:
                    pe.wait_ge(qkT_ready, i - 3)
                if i == 2:
                    pe.wait_ge(projN_read, 10)
                for m in range(2):
                    for t in range(T):
                        if i < 2:
                            src = KV[:, t, 2 + 2 * i, m * P:(m + 1) * P]
                        else:
                            a, j = (i - 2) // 2, 2 * (i % 2) + m
                            src = QN[:, t, a, j, :, :].rearrange("p r d -> p (r d)")
                        ins = nc.tensor.transpose(bank[i % 4][:, m * S + t * P:m * S + (t + 1) * P], src, ident)
                ins.then_inc(qkT_done, 1)
            pe.wait_ge(qkT_ready, 6)

            def q_of(hd, t):
                g, j = hd // HG, hd % HG
                lo = DH * (g % 2)
                return QT[lo:lo + DH, g // 2, j, t * P:(t + 1) * P], lo, g

            for t in range(T):
                for hd in range(NH):
                    q, lo, g = q_of(hd, t)
                    at = ((g // 2) * HG + hd % HG) * 16
                    ins = mm(bank[4 + 2 * t + g % 2][:, at:at + NCMP], q, kcT[lo:lo + DH, g // 2, :], start=True, stop=True)
                ins.then_inc(sc_done, 1)
            for i in range(8):
                t = i // 4
                pe.wait_ge(pc_ready, t + 1)
                if i >= 4:
                    pe.wait_ge(pcT_ready, i - 3)
                for m in range(4):
                    ins = nc.tensor.transpose(bank[i % 4][0:NCMP, m * P:(m + 1) * P], Pc[:, t, 4 * (i % 4) + m, 0:NCMP], ident)
                ins.then_inc(pcT_done, 1)
            pe.wait_ge(pcT_ready, 8)

            def scores(u):
                t, hd = u // NH, u % NH
                n = P * (t + 1)
                if u >= 2:
                    pe.wait_ge(eN_ready, 2 * (u - 1))
                q, lo, g = q_of(hd, t)
                for b in range(2):
                    mm(bank[u % 2][:, b * n:(b + 1) * n], q, KTn[lo:lo + DH, b, g // 2, 0:n], start=True, stop=True)
                    ins = mm(bank[u % 2][:, b * n + t * P:b * n + n], ident_b[:, :], mask_qb[:, :], start=False, stop=True,
                             skip_group_check=True)
                ins.then_inc(sN_done, 1)

            def turned(u):
                n = 2 * (u // NH + 1)
                pe.wait_ge(pN_ready, 2 * (u + 1))
                if u >= 2:
                    pe.wait_ge(ptN_a, u - 1)
                for m in range(n):
                    ins = nc.tensor.transpose(bank[2 + u % 2][:, m * P:(m + 1) * P], PN[:, u % 2, m * P:(m + 1) * P], ident)
                ins.then_inc(ptN_done, 1)

            def outputs(u):
                t, hd = u // NH, u % NH
                g = hd // HG
                o = bank[4 + u // 8][:, (hd % 8) * DH:(hd % 8 + 1) * DH]
                pe.wait_ge(ptN_a, u + 1)
                mm(o, PcT[:, hd, t * P:(t + 1) * P], vcn[:, g, :], start=True, stop=False)
                n = 2 * (t + 1)
                for m in range(n):
                    b, s = m // (t + 1), m % (t + 1)
                    ins = mm(o, PTn[:, u % 2, m * P:(m + 1) * P], KV[:, s, 3 + 2 * b, g * DH:(g + 1) * DH], start=False, stop=(m == n - 1))
                ins.then_inc(oN_done, 1)

            scores(0)
            for u in range(T * NH):
                if u + 1 < T * NH:
                    scores(u + 1)
                if u:
                    outputs(u - 1)
                turned(u)
            outputs(T * NH - 1)
            transposes(on, 4, oN_read, hsT_done)
            pe.wait_ge(hsT_ready, 8)
            for u in range(4):
                rows(U_NOUT + u, xT[0], 4 + u)
            moe(1)


N_SMALL = 22
XSTEPS = 27
_INS = ['x', 'mlstm_norm', 'mlstm_w_in', 'mlstm_gate_bias', 'mlstm_head_norm', 'mlstm_w_out', 'kv_norm', 'kv_w',
        'cmp_pe_k', 'cmp_w1_k', 'cmp_w2_k', 'cmp_pe_v', 'cmp_w1_v', 'cmp_w2_v', 'nsa_norm', 'nsa_w_q', 'nsa_w_out',
        'moe_norm', 'moe_w_group', 'moe_b_group', 'moe_w_router', 'moe_b_router', 'moe_w_gate', 'moe_w_up',
        'moe_w_down', 'final_norm']


def kernel(**inputs):
    import concourse.bacc as bacc
    from concourse.bass_utils import run_bass_kernel_spmd as run

    nc = bacc.Bacc("TRN2", target_bir_lowering=False, num_devices=1,
                   dynamic_dma_scratch_size=1024)
    arrays, args = {}, []
    for name in _INS:
        a = np.ascontiguousarray(inputs[name])
        arrays[f"in_{name}"] = a
        args.append(nc.dram_tensor(f"in_{name}", a.shape, mybir.dt.from_np(a.dtype), kind="ExternalInput").ap())
    consts, place = constants()
    arrays["in_consts"] = consts
    args.append(nc.dram_tensor("in_consts", consts.shape, mybir.dt.float32, kind="ExternalInput").ap())
    args.append(nc.dram_tensor("out_h", (1, S, D), mybir.dt.float32, kind="ExternalOutput").ap())
    build(nc, *args, place, consts.shape[1])
    r = run(nc, [arrays], core_ids=[0])
    return r.results[0]["out_h"]
```

```python
from contextlib import ExitStack

import numpy as np
import concourse.bass as bass
from concourse import mybir

P = 128
D = 1024
S = 256
T = S // P
KT = D // P
EPS = 1e-6
NEG = -1e30
MH, MDK, MDV = 4, 128, 256
SOFTCAP = 15.0
NGATE = 2 * MH
O_GATES = 2 * MH * MDK + 2 * MH * MDV
NH, DH, NG = 16, 64, 4
HG = NH // NG
ROPE = DH // 4
HALF = ROPE // 2
THETA = 500000.0
CB, CS = 32, 16
NCMP = (S - CB) // CS + 1
NBR = 3
MG, ME = 4, 8
NE = MG * ME
F = D // 4
FT = F // P
NR = MG + NE
SLOTS = 2 * S
ST = SLOTS // P
WIN = 64
MAX_EXTRA = (SLOTS - 1) // WIN
PADDED = SLOTS + WIN
LC = 512
LOAD = KT * LC
RING = 6
L_A, L_AOUT = 0, 6
L_MOE = (8, 64)
L_KV0, L_CMP, L_KV1, L_Q, L_NOUT = 56, 57, 58, 60, 62
N_LOADS = 112
PAIRS = NE // 2
TURN = 2
TURNS = PAIRS // TURN
KEY = S
LANDED, _count = [], [0] * RING
for _n in range(N_LOADS):
    _count[_n % RING] += 2 if _n == L_CMP else 1
    LANDED.append(_count[_n % RING])


def constants():
    f32 = np.float32
    row, col = np.arange(P)[:, None], np.arange(P)[None, :]
    inv = np.power(f32(THETA), -np.arange(HALF, dtype=f32) * f32(2.0 / ROPE)).astype(f32)

    def rope(pos):
        ang = (pos.astype(f32)[:, None] * inv[None, :]).astype(f32)
        c, s = np.cos(ang).astype(f32), np.sin(ang).astype(f32)
        return np.concatenate([c, c], 1), np.concatenate([-s, s], 1)

    c, s = rope(np.arange(S))
    tok = lambda a: a.reshape(T, P, -1).transpose(1, 0, 2).reshape(P, -1)
    cc, cs = rope(np.arange(NCMP) * CS + CB - 1)
    pad = lambda a: np.concatenate([a, np.zeros((P - a.shape[0], a.shape[1]), f32)])
    sel = np.zeros((P, MH, P), f32)
    for h in range(MH):
        sel[h, h] = 1
    ends = np.arange(NCMP) * CS + CB - 1
    ok = ends[None, :] <= np.arange(S)[:, None]
    parts = {
        "ident": np.eye(P), "mask_q": np.where(col > row, NEG, 0), "mask_k": np.where(col < row, NEG, 0),
        "before": row < col, "ones": np.ones((P, P)), "iota": np.tile(np.arange(SLOTS), (P, 1)),
        "cos": tok(c), "sin": tok(s), "ccos": pad(cc), "csin": pad(cs),
        "cmask": tok(np.where(ok, 0, NEG)), "cvalid": tok(ok.any(1)[:, None]),
        "sel": sel.reshape(P, -1), "slot_key": KEY * (2 * np.arange(PAIRS)[None, :] + row // WIN) + row % WIN, "lane": row % WIN,
        "key_e": np.tile(KEY * np.arange(NE), (P, 1)),
        "ones_s": np.ones((P, S)), "desc": np.tile(np.arange(ME, 0, -1), (P, 1)),
    }
    at, place = 0, {}
    for name, a in parts.items():
        place[name] = (at, at + a.shape[1])
        at += a.shape[1]
    return np.ascontiguousarray(np.concatenate([np.asarray(a, f32) for a in parts.values()], 1)), place


def build(nc, x, mlstm_norm, mlstm_w_in, mlstm_gate_bias, mlstm_head_norm, mlstm_w_out, kv_norm, kv_w,
          cmp_pe_k, cmp_w1_k, cmp_w2_k, cmp_pe_v, cmp_w1_v, cmp_w2_v, nsa_norm, nsa_w_q, nsa_w_out,
          moe_norm, moe_w_group, moe_b_group, moe_w_router, moe_b_router, moe_w_gate, moe_w_up,
          moe_w_down, final_norm, consts, out, place, n_const):
    fp32, bf16, i32 = mybir.dt.float32, mybir.dt.bfloat16, mybir.dt.int32
    ALU, ACT, AX = mybir.AluOpType, mybir.ActivationFunctionType, mybir.AxisListType
    ds = bass.ds
    ctx = ExitStack()
    with ctx:
        def sb(name, shape, dt=fp32):
            return ctx.enter_context(nc.sbuf_tensor(name, shape, dt))

        def sem(name):
            return ctx.enter_context(nc.semaphore(name))

        const = sb("const", [P, n_const])
        ring = sb("ring", [P, RING, LOAD])
        h = sb("h", [P, T, D])
        xs = sb("xs", [P, T, KT, P])
        xT = [sb(f"xT{i}", [P, KT, S]) for i in range(2)]
        area = sb("area", [P, 16384])
        bank = [ctx.enter_context(nc.psum_tensor(f"bank{i}", [P, 512], fp32)) for i in range(8)]

        def c(name):
            return const[:, place[name][0]:place[name][1]]

        ident, ones, iota = c("ident"), c("ones"), c("iota")
        ident_b = sb("ident_b", [P, P], bf16)
        mask_qb = sb("mask_qb", [P, P], bf16)
        mask_kb = sb("mask_kb", [P, P], bf16)
        gains = sb("gains", [P, 6, KT])
        G_A, G_HEAD, G_KV, G_Q, G_MOE = 0, 1, 2, 3, 4
        w_mgate = sb("w_mgate", [P, KT, NGATE])
        b_mgate = sb("b_mgate", [P, NGATE])
        w_ngate = sb("w_ngate", [P, KT, NBR * NH])
        w_route = sb("w_route", [P, 2, KT, NR])
        b_route = sb("b_route", [P, 2, NR])
        pe_in = sb("pe_in", [CB, 2, DH])
        w_cmp2 = sb("w_cmp2", [DH, 2, DH])
        sq = sb("sq", [P, T])
        ms = sb("ms", [P, T])
        rstd = sb("rstd", [P, T])
        slot_key = c("slot_key")
        neghalf = sb("neghalf", [P, 8])

        def cut(a, b, shape=None, parts=P):
            v = area[0:parts, a:b]
            if shape:
                v = v.rearrange(shape[0], **shape[1])
            return v

        qkT = cut(0, 2048, ("p (u t) -> p u t", {"t": S}))
        vA = cut(2048, 4096, ("p (t h v) -> p t h v", {"t": T, "h": MH}))
        og = cut(4096, 6144, ("p (t h v) -> p t h v", {"t": T, "h": MH}))
        EA = cut(6144, 6912, ("p (b n) -> p b n", {"b": 2}))
        PA = cut(6912, 7680, ("p (b n) -> p b n", {"b": 2}))
        gA = [cut(7680 + i * S, 7680 + (i + 1) * S, parts=MH) for i in range(8)]
        hsA = cut(9728, 11776, ("p (t k q) -> p t k q", {"t": T, "k": KT}))
        tmpA = cut(11776, 13824, ("p (t h v) -> p t h v", {"t": T, "h": MH}))
        gpre = sb("gpre", [P, T, NGATE])
        a_col = sb("a_col", [P, T, MH])
        em_col = sb("em_col", [P, T, MH])
        ssA = sb("ssA", [P, T, MH])
        rA = sb("rA", [P, T, MH])
        uA = sb("uA", [P, T, MH])
        cA = sb("cA", [P, T, MH])
        KV = cut(0, 3072, ("p (t u n) -> p t u n", {"t": T, "u": 6}))
        QT = cut(3072, 5120, ("p (a j t) -> p a j t", {"a": 2, "j": HG}))
        KTn = cut(5120, 6144, ("p (b a t) -> p b a t", {"b": 2, "a": 2}))
        PN = cut(6144, 7168, ("p (b n) -> p b n", {"b": 2}))
        PTn = cut(7168, 8192, ("p (b n) -> p b n", {"b": 2}))
        QN = cut(8192, 10240, ("p (t a j r d) -> p t a j r d", {"t": T, "a": 2, "j": HG, "r": 2}))
        cT = cut(10240, 12800, ("p (b g t) -> p b g t", {"b": 2, "g": NG + 1}), parts=DH)
        PcT = cut(8192, 12288, ("p (h t) -> p h t", {"h": NH}), parts=NCMP)
        on = cut(12800, 14848, ("p (t k q) -> p t k q", {"t": T, "k": KT}))
        Pc = cut(14848, 15360, ("p (t h n) -> p t h n", {"t": T, "h": NH}))
        ngate = sb("ngate", [P, T, NH, NBR])
        rope_a = sb("rope_a", [P, 4, ROPE])
        rope_b = sb("rope_b", [P, 4, ROPE])
        c1 = sb("c1", [DH, NG * NCMP])
        c1e = sb("c1e", [DH, NG * NCMP])
        cbias = sb("cbias", [DH, 1])
        c1s = [sb(f"c1s{i}", [DH, NG * NCMP]) for i in range(2)]
        kcn = sb("kcn", [NCMP, NG, DH])
        vcn = sb("vcn", [NCMP, NG, DH])
        kcT = sb("kcT", [P, 2, NCMP])
        ccoef = sb("ccoef", [P, NH])
        nmax = sb("nmax", [P, 2, 2])
        lsum = sb("lsum", [P, 2, 2])
        ncoef = sb("ncoef", [P, 2, 2])
        Xs = cut(0, 4608, ("p (k n) -> p k n", {"k": KT}))
        Sel = cut(4608, 5632, ("p (t n) -> p t n", {"t": T}))
        Y = cut(5632, 7680, ("p (b n) -> p b n", {"b": 2}))
        GT = cut(7680, 8192, ("p (b n) -> p b n", {"b": 2}))
        sg = cut(8192, 8448)
        hid = cut(8448, 8704)
        hidT = cut(8704, 8960, ("p (f n) -> p f n", {"f": FT}))
        g1, g2 = cut(8960, 9216), cut(9216, 9472)
        diag = cut(9472, 10496, ("p (t i n) -> p t i n", {"t": T, "i": 4}))
        bcast = cut(10496, 11520, ("p (i n) -> p i n", {"i": 4}))
        xwin = xT[1][:, :, :].rearrange("p k t -> p (k t)").rearrange("p (b r k n) -> p b r k n", b=2, r=2, k=KT)
        keys = sb("keys", [P, T, NE])
        lg = sb("lg", [P, T, NR])
        r4 = [sb(f"r4_{i}", [P, T, MG]) for i in range(2)]
        r8 = [sb(f"r8_{i}", [P, T, ME]) for i in range(4)]
        r32 = sb("r32", [P, T, ME, MG])
        hot = [sb(f"hot{i}", [P, T, NE]) for i in range(3)]
        place32 = sb("place32", [P, T, NE])
        prod32 = sb("prod32", [P, T, NE])
        cum = sb("cum", [P, NE])
        first = sb("first", [P, NE])
        one = [sb(f"one{i}", [P, T]) for i in range(12)]
        gexp = sb("gexp", [P, T, MG])
        table = sb("table", [1, 64], i32)
        T_COUNT, T_XFIRST, T_XID = 32, 40, 48
        n_max = sb("n_max", [1, 1])
        ex = [sb(f"ex{i}", [P, NE]) for i in range(4)]
        ex7 = [cut(11520 + 256 * i, 11520 + 256 * i + MAX_EXTRA * NE, ("p (x e) -> p x e", {"e": NE})) for i in range(3)]
        exr = [sb(f"exr{i}", [P, MAX_EXTRA]) for i in range(5)]
        gfin = cut(0, 1024)
        res = cut(1024, 3072, ("p (t n) -> p t n", {"t": T}))

        load_in = [sem(f"load_in{i}") for i in range(RING)]
        used = sem("used")
        x_in = sem("x_in")
        small_in = sem("small_in")
        gfin_in = sem("gfin_in")
        out_done = sem("out_done")
        h_ready = sem("h_ready")
        sq_ready = sem("sq_ready")
        ms_ready = sem("ms_ready")
        rstd_ready = sem("rstd_ready")
        xs_ready = sem("xs_ready")
        xt_done = sem("xt_done")
        xt_ready = sem("xt_ready")
        dve_step = sem("dve_step")
        act_step = sem("act_step")
        const_ready = sem("const_ready")
        dve_final = sem("dve_final")
        terms = sem("terms")
        neghalf_ready = sem("neghalf_ready")
        mgate_done, mgate_ready, mgateT_done, tanh_ready = map(sem, ("mgate_done", "mgate_ready", "mgateT_done", "tanh_ready"))
        logf_ready, am_ready, col_done, col_ready = map(sem, ("logf_ready", "am_ready", "col_done", "col_ready"))
        em_ready = sem("em_ready")
        projA_read = sem("projA_read")
        og_ready = sem("og_ready")
        eA_done, eA_ready, sA_done, pA_ready, numA_done = map(sem, ("eA_done", "eA_ready", "sA_done", "pA_ready", "numA_done"))
        ssA_ready, uA_ready, powA_ready, hsA_ready, hsT_done, hsT_ready = map(sem, (
            "ssA_ready", "uA_ready", "powA_ready", "hsA_ready", "hsT_done", "hsT_ready"))
        projN_read = sem("projN_read")
        ngate_done, ngate_exp, ngate_read = map(sem, ("ngate_done", "ngate_exp", "ngate_read"))
        cT_done, cT_ready, c1_ready, c1_exp, c1s_ready, c2_done, c2_ready, kcT_done, kcT_ready = map(sem, (
            "cT_done", "cT_ready", "c1_ready", "c1_exp", "c1s_ready", "c2_done", "c2_ready", "kcT_done", "kcT_ready"))
        qkT_done, qkT_ready = sem("qkT_done"), sem("qkT_ready")
        sc_done, sc_ready, pc_exp, pc_ready, pcT_done, pcT_ready = map(sem, (
            "sc_done", "sc_ready", "pc_exp", "pc_ready", "pcT_done", "pcT_ready"))
        sN_done, mN_ready, eN_ready, pN_ready, ptN_done, ptN_v, ptN_a, oN_done, oN_read = map(sem, (
            "sN_done", "mN_ready", "eN_ready", "pN_ready", "ptN_done", "ptN_v", "ptN_a", "oN_done", "oN_read"))
        route_done, route_sub, route_exp, route_sub2, route_exp2, hot_ready, rank_done = map(sem, (
            "route_done", "route_sub", "route_exp", "route_sub2", "route_exp2", "hot_ready", "rank_done"))
        sel_ready, diag_ready, bcast_done, bcast_ready, table_ready = map(sem, (
            "sel_ready", "diag_ready", "bcast_done", "bcast_ready", "table_ready"))
        gather_done, gather_v, gather_a, pad_ready = map(sem, ("gather_done", "gather_v", "gather_a", "pad_ready"))
        win_ready, silu_ready, hid_ready, hT_done, hT_ready, y_v, y_a, gt_ready, comb_done = map(sem, (
            "win_ready", "silu_ready", "hid_ready", "hT_done", "hT_ready", "y_v", "y_a", "gt_ready", "comb_done"))
        extra = [{n: sem(f"x_{n}{layer}") for n in ("step", "table", "w", "win", "up", "silu", "hid", "hT_done",
                                                     "hT", "down", "y", "gt", "comb")} for layer in range(2)]

        kpc = lambda w: w.rearrange("(p k) c -> p k c", k=KT)
        w_in, w_mout, w_kv, w_nq, w_nout = map(kpc, (mlstm_w_in[0], mlstm_w_out[0], kv_w, nsa_w_q[0], nsa_w_out[0]))
        pk = lambda g: g.rearrange("(p k) -> p k", k=KT)

        def columns(n):
            return ring[:, n % RING, :].rearrange("p (k c) -> p k c", k=KT)

        def pair_up(n):
            return ring[:, n % RING, :].rearrange("p (r k f) -> p r k f", r=2, k=KT)

        def pair_down(n):
            return ring[:, n % RING, :].rearrange("p (r f d) -> p r f d", r=2, f=FT)

        def arrived(eng, n, turn=0):
            eng.wait_ge(load_in[n % RING], 16 * LANDED[n] + 16 * turn)

        block = ctx.enter_context(nc.Block())

        @block.sync
        def _(sp):
            sp.dma_start(h[:, 0, :], x[0, 0:P, :]).then_inc(x_in, 16)
            sp.dma_start(h[:, 1, :], x[0, P:S, :]).then_inc(x_in, 16)

            def load(n, src):
                if n >= RING:
                    sp.wait_ge(used, 2 * (n - RING + 1))
                sp.dma_start(columns(n), src).then_inc(load_in[n % RING], 16)

            def load_moe(layer):
                base = L_MOE[layer]

                def turn(i):
                    for j in range(TURN):
                        e = (i * TURN + j) * 2
                        for m, w in enumerate((moe_w_gate, moe_w_up, moe_w_down)):
                            n = base + 3 * j + m
                            sp.wait_ge(used, 2 * (n - RING + 1) + 2 * RING * i)
                            if m == 2:
                                src = w[layer, ds(e, 2)].rearrange("r (f p) d -> p r f d", p=P)
                                sp.dma_start(pair_down(n), src).then_inc(load_in[n % RING], 16)
                            else:
                                src = w[layer, ds(e, 2)].rearrange("r (p k) f -> p r (k f)", k=KT)
                                sp.dma_start(ring[:, n % RING, :].rearrange("p (r c) -> p r c", r=2), src).then_inc(load_in[n % RING], 16)

                with sp.Fori(0, TURNS) as i:
                    turn(i)
                sp.wait_ge(table_ready, layer + 1)
                n_top = sp.value_load(table[0:1, T_COUNT:T_COUNT + 1], min_val=0, max_val=S)
                q = extra[layer]
                with sp.If(n_top > WIN):
                    sp.wait_ge(used, 2 * (base + 3 * PAIRS))
                    sp.wait_ge(q["table"], 1)

                    def again(j):
                        e = sp.value_load(table[0:1, ds(j + T_XID, 1)], min_val=0, max_val=NE - 1)
                        for m, w in enumerate((moe_w_gate, moe_w_up)):
                            sp.dma_start(ring[:, m, 0:LOAD // 2], w[layer, ds(e, 1)].rearrange("o (p k) f -> p (o k f)", k=KT)).then_inc(q["w"], 16)
                        sp.dma_start(pair_down(2)[:, 0, :, :], moe_w_down[layer, ds(e, 1)].rearrange("o (f p) d -> p (o f) d", p=P)).then_inc(q["w"], 16)

                    again(0)
                    with sp.Fori(1, MAX_EXTRA) as j:
                        sp.wait_ge(q["down"], j)
                        again(j)
                    sp.wait_ge(q["down"], MAX_EXTRA)

            for u in range(6):
                load(L_A + u, w_in[:, :, u * LC:(u + 1) * LC])
            for u in range(2):
                load(L_AOUT + u, w_mout[:, :, u * LC:(u + 1) * LC])
            load_moe(0)
            load(L_KV0, w_kv[:, :, 0:LC])
            sp.wait_ge(used, 2 * (L_CMP - RING + 1))
            for b, w in enumerate((cmp_w1_k, cmp_w1_v)):
                sp.dma_start(ring[0:DH, L_CMP % RING, b * 2048:(b + 1) * 2048].rearrange("d (l f) -> d l f", l=CB),
                             w.rearrange("(l d) f -> d l f", d=DH)).then_inc(load_in[L_CMP % RING], 16)
            for u in range(2):
                load(L_KV1 + u, w_kv[:, :, (u + 1) * LC:(u + 2) * LC])
            for u in range(2):
                load(L_Q + u, w_nq[:, :, u * LC:(u + 1) * LC])
            for u in range(2):
                load(L_NOUT + u, w_nout[:, :, u * LC:(u + 1) * LC])
            load_moe(1)
            sp.wait_ge(h_ready, 16)
            sp.dma_start(gfin, final_norm.rearrange("(a n) -> a n", a=1).to_broadcast([P, D])).then_inc(gfin_in, 16)
            for t in range(T):
                sp.wait_ge(dve_final, t + 1)
                sp.dma_start(out[0, t * P:(t + 1) * P, :], res[:, t, :]).then_inc(out_done, 16)
            sp.wait_ge(out_done, 32)

        @block.gpsimd
        def _(pool):
            pool.memset(neghalf[:, :], -0.5).then_inc(neghalf_ready, 1)
            pool.wait_ge(neghalf_ready, 1)

            def rms(n):
                pool.wait_ge(ms_ready, n + 1)
                pool.tensor_tensor(rstd[:, :], ms[:, :], neghalf[:, 0:T], ALU.pow).then_inc(rstd_ready, 1)

            rms(0)
            pool.wait_ge(uA_ready, 1)
            pool.tensor_tensor(cA[:, :, :].rearrange("p t h -> p (t h)"), uA[:, :, :].rearrange("p t h -> p (t h)"),
                               neghalf[:, :], ALU.pow).then_inc(powA_ready, 1)
            for n in range(1, 5):
                rms(n)

        @block.scalar
        def _(act):
            smalls = [
                (gains[:, G_A, :], pk(mlstm_norm[0])), (gains[:, G_HEAD, :], pk(mlstm_head_norm[0])),
                (gains[:, G_KV, :], pk(kv_norm)), (gains[:, G_Q, :], pk(nsa_norm[0])),
                (gains[:, G_MOE, :], pk(moe_norm[0])), (gains[:, G_MOE + 1, :], pk(moe_norm[1])),
                (w_mgate[:, :, :], w_in[:, :, O_GATES:O_GATES + NGATE]),
                (b_mgate[:, :], mlstm_gate_bias[0:1, :].to_broadcast([P, NGATE])),
                (w_ngate[:, :, :], w_nq[:, :, NH * DH:NH * DH + NBR * NH]),
                (pe_in[:, 0, :], cmp_pe_k), (pe_in[:, 1, :], cmp_pe_v),
                (w_cmp2[:, 0, :], cmp_w2_k), (w_cmp2[:, 1, :], cmp_w2_v),
            ]
            for i in range(2):
                smalls += [
                    (w_route[:, i, :, 0:MG], kpc(moe_w_group[i])), (w_route[:, i, :, MG:NR], kpc(moe_w_router[i])),
                    (b_route[:, i, 0:MG], moe_b_group[i:i + 1, :].to_broadcast([P, MG])),
                    (b_route[:, i, MG:NR], moe_b_router[i:i + 1, :].to_broadcast([P, NE])),
                ]
            assert len(smalls) == N_SMALL - 1
            act.dma_start(const[:, :], consts).then_inc(small_in, 16)
            for dst, src in smalls:
                act.dma_start(dst, src).then_inc(small_in, 16)

            def squares(n):
                for t in range(T):
                    if n == 0:
                        act.wait_ge(x_in, 32)
                    else:
                        act.wait_ge(h_ready, 4 * n)
                    act.activation(xs[:, t, :, :].rearrange("p k q -> p (k q)"), h[:, t, :], ACT.Square,
                                   accum_out=sq[:, t:t + 1]).then_inc(sq_ready, 1)

            squares(0)
            act.wait_ge(mgateT_done, 4)
            act.activation(gA[0], bank[1][0:MH, 0:S], ACT.Tanh, scale=1.0 / SOFTCAP).then_inc(act_step, 1)
            act.activation(gA[1], bank[1][0:MH, S:2 * S], ACT.Tanh, scale=1.0 / SOFTCAP).then_inc(act_step, 1)
            act.wait_ge(act_step, 2)
            act.activation(gA[2], gA[1], ACT.Exp, scale=-SOFTCAP).then_inc(act_step, 1)
            act.wait_ge(act_step, 3)
            act.activation(gA[3], gA[2], ACT.Ln, bias=1.0).then_inc(logf_ready, 1)
            for n in range(4):
                act.wait_ge(used, 2 * 4 + n + 1)
                act.activation(og[:, n % 2, n // 2 * 2:n // 2 * 2 + 2, :], bank[4 + n][:, :].rearrange("p (h v) -> p h v", h=2),
                               ACT.Tanh, scale=0.5).then_inc(og_ready, 1)
            act.wait_ge(col_ready, 2)
            act.activation(em_col[:, :, :], em_col[:, :, :], ACT.Exp, scale=-1.0).then_inc(em_ready, 1)
            for hd in range(MH):
                act.wait_ge(eA_done, hd + 1)
                if hd >= 2:
                    act.wait_ge(pA_ready, hd - 1)
                act.activation(EA[:, hd % 2, 0:S], bank[hd % 2][:, 0:S], ACT.Exp, bias=a_col[:, 0, hd:hd + 1]).then_inc(eA_ready, 1)
                act.activation(EA[:, hd % 2, S:S + P], bank[hd % 2][:, S:S + P], ACT.Exp, bias=a_col[:, 1, hd:hd + 1]).then_inc(eA_ready, 1)
            for hd in range(MH):
                for t in range(T):
                    act.wait_ge(numA_done, hd + 1)
                    act.activation(tmpA[:, t, hd, :], bank[4 + hd][:, t * MDV:(t + 1) * MDV], ACT.Square,
                                   accum_out=ssA[:, t, hd:hd + 1]).then_inc(ssA_ready, 1)

            def moe(layer):
                squares(2 * layer + 1)
                act.wait_ge(route_sub, layer + 1)
                act.activation(gexp[:, :, :], gexp[:, :, :], ACT.Exp).then_inc(route_exp, 1)
                act.wait_ge(route_sub2, layer + 1)
                act.activation(one[5][:, :], one[4][:, :], ACT.Exp).then_inc(route_exp2, 1)
                for k in range(1, KT, 2):
                    act.wait_ge(gather_done, KT * layer + k + 1)
                    act.activation(Xs[:, k, 0:SLOTS], bank[k % 4][:, :], ACT.Copy,
                                   scale=gains[:, G_MOE + layer, k:k + 1]).then_inc(gather_a, 1)
                base, p0 = 2 * L_MOE[layer], PAIRS * layer
                act.wait_ge(gather_v, 4 * (layer + 1))
                act.wait_ge(gather_a, 4 * (layer + 1))
                act.wait_ge(pad_ready, layer + 1)
                act.wait_ge(table_ready, layer + 1)

                def window(i, j, first):
                    if not first:
                        act.wait_ge(used, base + 6 * (j - 2) + 4 + 6 * TURN * i)
                    for r in range(2):
                        start = act.value_load(table[0:1, ds((i * TURN + j) * 2 + r, 1)], min_val=0, max_val=SLOTS)
                        act.activation(xwin[:, j % 2, r, :, :], Xs[:, :, ds(start, WIN)], ACT.Copy).then_inc(win_ready, 1)

                def turn(i, first=False, last=False):
                    for j in range(TURN):
                        if not (last and j == TURN - 1):
                            window(i, j + 1, first and j + 1 < 2)
                        at = base + 6 * j + 6 * TURN * i
                        act.wait_ge(used, at + 4)
                        act.activation(sg, bank[4][:, 0:F], ACT.Silu).then_inc(silu_ready, 1)
                        act.wait_ge(hT_done, p0 + j + 1 + TURN * i)
                        act.activation(hidT[:, :, :].rearrange("p f n -> p (f n)"), bank[7][:, 0:FT * P], ACT.Copy).then_inc(hT_ready, 1)
                        act.wait_ge(used, at + 6)
                        if not (first or j >= 2):
                            act.wait_ge(comb_done, p0 + j - 1 + TURN * i)
                        act.activation(Y[:, j % 2, 512:1024], bank[6][:, :], ACT.Copy).then_inc(y_a, 1)

                window(0, 0, True)
                turn(0, first=True)
                with act.Fori(1, TURNS - 1) as i:
                    turn(i)
                turn(TURNS - 1, last=True)
                q = extra[layer]
                n_top = act.value_load(table[0:1, T_COUNT:T_COUNT + 1], min_val=0, max_val=S)
                with act.If(n_top > WIN):
                    act.wait_ge(q["table"], 1)
                    act.wait_ge(comb_done, p0 + PAIRS)

                    def again(j):
                        start = act.value_load(table[0:1, ds(j + T_XFIRST, 1)], min_val=0, max_val=SLOTS)
                        act.activation(xwin[:, 0, 0, :, :], Xs[:, :, ds(start, WIN)], ACT.Copy).then_inc(q["win"], 1)
                        act.wait_ge(q["up"], j + 1)
                        act.activation(sg[0:WIN, :], bank[4][0:WIN, 0:F], ACT.Silu).then_inc(q["silu"], 1)
                        act.wait_ge(q["hT_done"], j + 1)
                        act.activation(hidT[:, :, 0:WIN], bank[7][:, 0:FT * P].rearrange("p (f n) -> p f n", f=FT)[:, :, 0:WIN], ACT.Copy).then_inc(q["hT"], 1)

                    again(0)
                    with act.Fori(1, MAX_EXTRA) as j:
                        again(j)

            moe(0)
            squares(2)
            act.wait_ge(c1_ready, 1)
            act.activation(c1e[:, :], c1[:, :], ACT.Exp, scale=-1.0).then_inc(c1_exp, 1)
            act.wait_ge(c1_ready, 2)
            act.activation(c1e[:, :], c1[:, :], ACT.Exp, scale=-1.0).then_inc(c1_exp, 1)
            act.wait_ge(ngate_done, 1)
            act.activation(ngate[:, :, :, :].rearrange("p t h b -> p t (h b)"),
                           bank[0][:, 0:2 * 64].rearrange("p (t n) -> p t n", t=T)[:, :, 0:NBR * NH],
                           ACT.Exp, scale=-1.0).then_inc(ngate_exp, 1)
            for t in range(T):
                act.wait_ge(sc_ready, t + 1)
                act.activation(Pc[:, t, :, 0:NCMP], Pc[:, t, :, 0:NCMP], ACT.Exp).then_inc(pc_exp, 1)

            def exps(u):
                n = P * (u // NH + 1)
                act.wait_ge(mN_ready, u + 1)
                if u >= 2:
                    act.wait_ge(ptN_done, u - 1)
                for b in range(2):
                    act.activation(PN[:, u % 2, b * n:(b + 1) * n], bank[u % 2][:, b * n:(b + 1) * n], ACT.Exp,
                                   bias=nmax[:, u % 2, b:b + 1], accum_out=lsum[:, u % 2, b:b + 1]).then_inc(eN_ready, 1)

            def evac(u):
                n = 2 * P * (u // NH + 1)
                act.wait_ge(ptN_done, u + 1)
                if u >= 2:
                    act.wait_ge(oN_done, u - 1)
                act.activation(PTn[:, u % 2, 0:n], bank[2 + u % 2][:, 0:n], ACT.Copy).then_inc(ptN_a, 1)

            exps(0)
            for u in range(1, T * NH):
                exps(u)
                evac(u - 1)
            evac(T * NH - 1)
            moe(1)
            squares(4)

        @block.vector
        def _(dve):
            steps = [0]

            def step(ins):
                steps[0] += 1
                ins.then_inc(dve_step, 1)
                dve.wait_ge(dve_step, steps[0])

            dve.wait_ge(small_in, 16 * N_SMALL)
            dve.tensor_copy(ident_b[:, :], ident).then_inc(const_ready, 1)
            dve.tensor_copy(mask_qb[:, :], c("mask_q")).then_inc(const_ready, 1)
            dve.tensor_copy(mask_kb[:, :], c("mask_k")).then_inc(const_ready, 1)

            def scale_rows(n):
                dve.wait_ge(sq_ready, T * (n + 1))
                dve.tensor_scalar(ms[:, :], sq[:, :], 1.0 / D, EPS, ALU.mult, ALU.add).then_inc(ms_ready, 1)
                dve.wait_ge(rstd_ready, n + 1)
                if n < 4:
                    for t in range(T):
                        dve.tensor_scalar(xs[:, t, :, :], h[:, t, :].rearrange("p (q k) -> p k q", k=KT),
                                          rstd[:, t:t + 1], None, ALU.mult).then_inc(xs_ready, 1)

            def evac_xT(done, gain_of, order):
                for b in range(4):
                    dve.wait_ge(xt_done, done + b + 1)
                    for i, g in enumerate(gain_of):
                        dve.tensor_tensor(xT[i][:, 2 * b:2 * b + 2, :], bank[b][:, :].rearrange("p (k t) -> p k t", k=2),
                                          gains[:, g, 2 * b:2 * b + 2].rearrange("p (k o) -> p k o", o=1).to_broadcast([P, 2, S]),
                                          ALU.mult).then_inc(xt_ready, 1)

            scale_rows(0)
            evac_xT(0, [G_A], None)
            dve.wait_ge(mgate_done, 1)
            dve.tensor_tensor(gpre[:, :, :], bank[0][:, 0:T * NGATE].rearrange("p (t n) -> p t n", t=T),
                              b_mgate[:, :].rearrange("p (o n) -> p o n", o=1).to_broadcast([P, T, NGATE]),
                              ALU.add).then_inc(mgate_ready, 1)

            def evac_projA(u):
                dve.wait_ge(used, u + 1)
                src = bank[4 + u % 4][:, :].rearrange("p (a n) -> p a n", a=2)
                if u < 2:
                    ins = dve.tensor_copy(qkT[:, 2 * u:2 * u + 2, :], src)
                elif u < 4:
                    ins = dve.tensor_scalar(qkT[:, 2 * u:2 * u + 2, :], src, float(MDK) ** -0.5, None, ALU.mult)
                else:
                    ins = dve.tensor_copy(vA[:, u % 2, 2 * (u // 2 - 2):2 * (u // 2 - 2) + 2, :], src)
                ins.then_inc(projA_read, 1)

            for u in range(4):
                evac_projA(u)
            ones_row = c("ones_s")[0:MH, :]
            dve.wait_ge(logf_ready, 1)
            step(dve.tensor_scalar(gA[3], gA[3], -1.0, None, ALU.mult))
            step(dve.tensor_tensor_scan(gA[4], ones_row, gA[3], 0.0, ALU.mult, ALU.add))
            step(dve.scalar_tensor_tensor(gA[5], gA[0], SOFTCAP, gA[4], ALU.mult, ALU.subtract))
            step(dve.tensor_tensor_scan(gA[6], ones_row, gA[5], 0.0, ALU.mult, ALU.max))
            step(dve.tensor_tensor(gA[7], gA[4], gA[6], ALU.add))
            dve.tensor_scalar(gA[6], gA[6], -1.0, None, ALU.mult).then_inc(am_ready, 1)
            for u in range(4, 8):
                evac_projA(u)
            dve.wait_ge(col_done, 1)
            dve.tensor_copy(a_col[:, :, :], bank[3][:, 0:8].rearrange("p (t h) -> p t h", t=T)).then_inc(col_ready, 1)
            dve.tensor_copy(em_col[:, :, :], bank[3][:, 8:16].rearrange("p (t h) -> p t h", t=T)).then_inc(col_ready, 1)
            for hd in range(MH):
                dve.wait_ge(eA_ready, 2 * hd + 2)
                dve.wait_ge(sA_done, hd + 1)
                if hd >= 2:
                    dve.wait_ge(numA_done, hd - 1)
                dve.tensor_tensor(PA[:, hd % 2, :], bank[2][:, 0:S + P], EA[:, hd % 2, :], ALU.mult).then_inc(pA_ready, 1)
            dve.wait_ge(og_ready, 4)
            dve.wait_ge(em_ready, 1)
            dve.wait_ge(numA_done, MH)
            den = bank[3][:, 16:24].rearrange("p (t h) -> p t h", t=T)
            step(dve.tensor_scalar(rA[:, :, :], den, -1.0, None, ALU.mult))
            step(dve.tensor_tensor(rA[:, :, :], den, rA[:, :, :], ALU.max))
            step(dve.tensor_tensor(rA[:, :, :], rA[:, :, :], em_col[:, :, :], ALU.max))
            step(dve.reciprocal(rA[:, :, :], rA[:, :, :]))
            dve.wait_ge(ssA_ready, T * MH)
            step(dve.tensor_tensor(uA[:, :, :], ssA[:, :, :], rA[:, :, :], ALU.mult))
            step(dve.tensor_tensor(uA[:, :, :], uA[:, :, :], rA[:, :, :], ALU.mult))
            step(dve.tensor_scalar(uA[:, :, :], uA[:, :, :], 1.0 / MDV, EPS, ALU.mult, ALU.add))
            dve.tensor_scalar(rA[:, :, :], rA[:, :, :], 0.5, None, ALU.mult).then_inc(uA_ready, 1)
            dve.wait_ge(uA_ready, 1)
            dve.wait_ge(powA_ready, 1)
            step(dve.tensor_tensor(cA[:, :, :], cA[:, :, :], rA[:, :, :], ALU.mult))
            for t in range(T):
                for hd in range(MH):
                    step(dve.scalar_tensor_tensor(tmpA[:, t, hd, :], og[:, t, hd, :], 1.0,
                                                  bank[4 + hd][:, t * MDV:(t + 1) * MDV], ALU.add, ALU.mult))
                    q = MDV // KT
                    dve.tensor_scalar(hsA[:, t, :, hd * q:(hd + 1) * q], tmpA[:, t, hd, :].rearrange("p (q k) -> p k q", k=KT),
                                      cA[:, t, hd:hd + 1], None, ALU.mult).then_inc(hsA_ready, 1)

            def evac_eT(first, gain):
                for b in range(4):
                    dve.wait_ge(hsT_done, first + b + 1)
                    src = bank[b][:, :].rearrange("p (k t) -> p k t", k=2)
                    if gain is None:
                        ins = dve.tensor_copy(xT[0][:, 2 * b:2 * b + 2, :], src)
                    else:
                        ins = dve.tensor_tensor(xT[0][:, 2 * b:2 * b + 2, :], src,
                                                gains[:, gain, 2 * b:2 * b + 2].rearrange("p (k o) -> p k o", o=1).to_broadcast([P, 2, S]),
                                                ALU.mult)
                    ins.then_inc(hsT_ready, 1)

            def add_out(first):
                for u in range(4):
                    dve.wait_ge(used, 2 * first + u + 1)
                    rows = h[:, u % 2, u // 2 * LC:(u // 2 + 1) * LC]
                    dve.tensor_tensor(rows, bank[4 + u][:, :], rows, ALU.add).then_inc(h_ready, 1)

            evac_eT(0, G_HEAD)
            add_out(L_AOUT)

            def first_max(vals, top, onehot, key, n):
                step(dve.tensor_reduce(top, vals, AX.X, ALU.max))
                step(dve.tensor_tensor(key, vals, top.rearrange("p (t o) -> p t o", o=1).to_broadcast([P, T, n]), ALU.is_ge))
                step(dve.tensor_tensor(key, key, c("desc")[:, 0:n].rearrange("p (o n) -> p o n", o=1).to_broadcast([P, T, n]), ALU.mult))
                step(dve.tensor_reduce(one[9][:, :], key, AX.X, ALU.max))
                step(dve.tensor_tensor(onehot, key, one[9][:, :].rearrange("p (t o) -> p t o", o=1).to_broadcast([P, T, n]), ALU.is_ge))

            def moe(layer):
                scale_rows(2 * layer + 1)
                evac_xT((4, 12)[layer], [G_MOE + layer], None)
                dve.wait_ge(route_done, layer + 1)
                step(dve.tensor_tensor(lg[:, :, :], bank[4][:, 0:128].rearrange("p (t n) -> p t n", t=T)[:, :, 0:NR],
                                       b_route[:, layer:layer + 1, :].to_broadcast([P, T, NR]), ALU.add))
                first_max(lg[:, :, 0:MG], one[0][:, :], r4[0][:, :, :], r4[1][:, :, :], MG)
                dve.tensor_tensor(gexp[:, :, :], lg[:, :, 0:MG], one[0][:, :].rearrange("p (t o) -> p t o", o=1).to_broadcast([P, T, MG]),
                                  ALU.subtract).then_inc(route_sub, 1)
                for t in range(T):
                    dve.tensor_tensor(r32[:, t, :, :], lg[:, t, MG:NR].rearrange("p (g e) -> p e g", g=MG),
                                      r4[0][:, t:t + 1, :].to_broadcast([P, ME, MG]), ALU.mult).then_inc(dve_step, 1)
                steps[0] += T
                dve.wait_ge(dve_step, steps[0])
                step(dve.tensor_reduce(r8[0][:, :, :], r32[:, :, :, :], AX.X, ALU.add))
                first_max(r8[0][:, :, :], one[1][:, :], r8[1][:, :, :], r8[3][:, :, :], ME)
                step(dve.scalar_tensor_tensor(r8[2][:, :, :], r8[1][:, :, :], -3e38, r8[0][:, :, :], ALU.mult, ALU.add))
                first_max(r8[2][:, :, :], one[2][:, :], r8[0][:, :, :], r8[3][:, :, :], ME)
                dve.tensor_tensor(one[4][:, :], one[2][:, :], one[1][:, :], ALU.subtract).then_inc(route_sub2, 1)
                for t in range(T):
                    for i, r in ((0, r8[1]), (1, r8[0])):
                        dve.tensor_tensor(hot[i][:, t, :].rearrange("p (g e) -> p g e", g=MG),
                                          r4[0][:, t, :].rearrange("p (g o) -> p g o", o=1).to_broadcast([P, MG, ME]),
                                          r[:, t:t + 1, :].to_broadcast([P, MG, ME]), ALU.mult).then_inc(dve_step, 1)
                steps[0] += 2 * T
                dve.wait_ge(dve_step, steps[0])
                dve.tensor_tensor(hot[2][:, :, :], hot[0][:, :, :], hot[1][:, :, :], ALU.add).then_inc(hot_ready, 1)
                dve.wait_ge(route_exp, layer + 1)
                step(dve.tensor_reduce(one[3][:, :], gexp[:, :, :], AX.X, ALU.add))
                dve.wait_ge(route_exp2, layer + 1)
                step(dve.scalar_tensor_tensor(one[6][:, :], one[5][:, :], 1.0, one[3][:, :], ALU.add, ALU.mult))
                step(dve.reciprocal(one[6][:, :], one[6][:, :]))
                step(dve.tensor_tensor(one[7][:, :], one[6][:, :], one[5][:, :], ALU.mult))
                dve.wait_ge(rank_done, layer + 1)
                count = bank[5][:, 64:96]
                step(dve.tensor_copy(first[:, :], count))
                step(dve.tensor_tensor_scan(cum[:, :], ones[:, 0:NE], first[:, :], 0.0, ALU.mult, ALU.add))
                step(dve.tensor_reduce(n_max[:, :], first[0:1, :], AX.X, ALU.max))
                step(dve.tensor_tensor(first[:, :], cum[:, :], first[:, :], ALU.subtract))
                step(dve.tensor_copy(table[0:1, 0:NE], first[0:1, :]))
                dve.tensor_copy(table[0:1, T_COUNT:T_COUNT + 1], n_max[:, :]).then_inc(table_ready, 1)
                step(dve.tensor_tensor(place32[:, :, :], bank[5][:, 0:64].rearrange("p (t e) -> p t e", t=T),
                                       first[:, :].rearrange("p (o e) -> p o e", o=1).to_broadcast([P, T, NE]), ALU.add))
                step(dve.tensor_tensor(keys[:, :, :], bank[5][:, 0:64].rearrange("p (t e) -> p t e", t=T),
                                       c("key_e").rearrange("p (o e) -> p o e", o=1).to_broadcast([P, T, NE]), ALU.add))
                for i in range(2):
                    step(dve.tensor_tensor(prod32[:, :, :], hot[i][:, :, :], place32[:, :, :], ALU.mult))
                    step(dve.tensor_reduce(one[i][:, :], prod32[:, :, :], AX.X, ALU.add))
                for t in range(T):
                    step(dve.tensor_scalar(Sel[:, t, :], iota, one[0][:, t:t + 1], None, ALU.is_equal))
                    dve.scalar_tensor_tensor(Sel[:, t, :], iota, one[1][:, t:t + 1], Sel[:, t, :], ALU.is_equal, ALU.add).then_inc(sel_ready, 1)
                for i in range(2):
                    step(dve.tensor_tensor(prod32[:, :, :], hot[i][:, :, :], keys[:, :, :], ALU.mult))
                    step(dve.tensor_reduce(one[10 + i][:, :], prod32[:, :, :], AX.X, ALU.add))
                for t in range(T):
                    for i, v in enumerate((10, 11, 6, 7)):
                        dve.tensor_scalar(diag[:, t, i, :], ident, one[v][:, t:t + 1], None, ALU.mult).then_inc(diag_ready, 1)
                dve.memset(Xs[:, :, SLOTS:PADDED], 0.0).then_inc(pad_ready, 1)
                for k in range(0, KT, 2):
                    dve.wait_ge(gather_done, KT * layer + k + 1)
                    dve.tensor_scalar(Xs[:, k, 0:SLOTS], bank[k % 4][:, :], gains[:, G_MOE + layer, k:k + 1], None,
                                      ALU.mult).then_inc(gather_v, 1)
                for t in range(T):
                    dve.wait_ge(bcast_done, T * layer + t + 1)
                    dve.tensor_copy(bcast[:, :, t * P:(t + 1) * P], bank[6 + t][:, :].rearrange("p (i n) -> p i n", i=4)).then_inc(bcast_ready, 1)
                dve.wait_ge(bcast_ready, T * (layer + 1))
                base, p0 = 2 * L_MOE[layer], PAIRS * layer

                def weights_of(dst, key, parts, inc):
                    for g, m in ((g1, 0), (g2, 1)):
                        inc(dve.scalar_tensor_tensor(g[0:parts, :], bcast[0:parts, m, :], key, bcast[0:parts, 2 + m, :],
                                                     ALU.is_equal, ALU.mult))
                    return dve.tensor_tensor(dst, g1[0:parts, :], g2[0:parts, :], ALU.add)

                def turn(i, first=False):
                    for j in range(TURN):
                        if not (first or j >= 2):
                            dve.wait_ge(comb_done, p0 + j - 1 + TURN * i)
                        halves = []

                        def inc(ins):
                            halves.append(0)
                            ins.then_inc(terms, 1)
                            dve.wait_ge(terms, 2 * p0 + 2 * j + len(halves) + 2 * TURN * i)

                        weights_of(GT[:, j % 2, :], slot_key[:, ds(i * TURN + j, 1)], P, inc).then_inc(gt_ready, 1)
                        dve.wait_ge(silu_ready, p0 + j + 1 + TURN * i)
                        dve.tensor_tensor(hid, bank[4][:, F:2 * F], sg, ALU.mult).then_inc(hid_ready, 1)
                        dve.wait_ge(used, base + 6 * j + 5 + 6 * TURN * i)
                        dve.tensor_copy(Y[:, j % 2, 0:512], bank[5][:, :]).then_inc(y_v, 1)

                turn(0, first=True)
                with dve.Fori(1, TURNS) as i:
                    turn(i)
                q = extra[layer]
                n_top = dve.value_load(table[0:1, T_COUNT:T_COUNT + 1], min_val=0, max_val=S)
                with dve.If(n_top > WIN):
                    extras(layer, q, weights_of)
                dve.wait_ge(comb_done, PAIRS * (layer + 1))
                for t in range(T):
                    for b in range(2):
                        dve.tensor_tensor(h[:, t, b * 512:(b + 1) * 512], bank[2 * t + b][:, :],
                                          h[:, t, b * 512:(b + 1) * 512], ALU.add).then_inc(h_ready, 1)

            def extras(layer, q, weights_of):
                cnt, extra_of, before, upto = (e[:, :] for e in ex)
                n = [0]

                def xstep(ins):
                    n[0] += 1
                    ins.then_inc(q["step"], 1)
                    dve.wait_ge(q["step"], n[0])

                bc = lambda v: v.rearrange("p (o e) -> p o e", o=1).to_broadcast([P, MAX_EXTRA, NE])
                col = lambda v: v.rearrange("p (x o) -> p x o", o=1).to_broadcast([P, MAX_EXTRA, NE])
                xstep(dve.tensor_tensor(cnt, cum[:, :], first[:, :], ALU.subtract))
                xstep(dve.tensor_scalar(extra_of, cnt, float(WIN), None, ALU.is_gt))
                for m in range(2, S // WIN):
                    xstep(dve.scalar_tensor_tensor(extra_of, cnt, float(m * WIN), extra_of, ALU.is_gt, ALU.add))
                xstep(dve.tensor_tensor_scan(upto, ones[:, 0:NE], extra_of, 0.0, ALU.mult, ALU.add))
                xstep(dve.tensor_tensor(before, upto, extra_of, ALU.subtract))
                idx = iota[:, 0:MAX_EXTRA]
                mine, t0, t1 = ex7
                xstep(dve.tensor_tensor(mine, bc(before), col(idx), ALU.is_le))
                xstep(dve.tensor_tensor(t0, bc(upto), col(idx), ALU.is_gt))
                xstep(dve.tensor_tensor(mine, mine, t0, ALU.mult))
                eid, start, nth, any_, key = (e[:, :] for e in exr)
                for dst, src in ((eid, iota[:, 0:NE]), (start, first[:, :]), (nth, before)):
                    xstep(dve.tensor_tensor(t1, mine, bc(src), ALU.mult))
                    xstep(dve.tensor_reduce(dst, t1, AX.X, ALU.add))
                xstep(dve.tensor_reduce(any_, mine, AX.X, ALU.add))
                xstep(dve.tensor_tensor(nth, idx, nth, ALU.subtract))
                xstep(dve.tensor_scalar(nth, nth, 1.0, float(WIN), ALU.add, ALU.mult))
                xstep(dve.tensor_tensor(nth, nth, any_, ALU.mult))
                xstep(dve.tensor_tensor(start, start, nth, ALU.add))
                xstep(dve.tensor_scalar(any_, any_, -1.0, float(-KEY * NE), ALU.add, ALU.mult))
                xstep(dve.scalar_tensor_tensor(key, eid, float(KEY), nth, ALU.mult, ALU.add))
                xstep(dve.tensor_tensor(key, key, any_, ALU.add))
                xstep(dve.tensor_scalar(key, key, c("lane"), None, ALU.add))
                xstep(dve.tensor_copy(table[0:1, T_XFIRST:T_XFIRST + MAX_EXTRA], start[0:1, :]))
                dve.tensor_copy(table[0:1, T_XID:T_XID + MAX_EXTRA], eid[0:1, :]).then_inc(q["table"], 1)
                made = n[0]

                def again(j):
                    at = [0]

                    def inc(ins):
                        at[0] += 1
                        ins.then_inc(q["step"], 1)
                        dve.wait_ge(q["step"], made + at[0] + 2 * j)

                    weights_of(GT[0:WIN, 0, :], key[0:WIN, ds(j, 1)], WIN, inc).then_inc(q["gt"], 1)
                    dve.wait_ge(q["silu"], j + 1)
                    dve.tensor_tensor(hid[0:WIN, :], bank[4][0:WIN, F:2 * F], sg[0:WIN, :], ALU.mult).then_inc(q["hid"], 1)
                    dve.wait_ge(q["down"], j + 1)
                    for b in range(2):
                        dve.tensor_copy(Y[0:WIN, 0, b * 512:(b + 1) * 512], bank[5 + b][0:WIN, :]).then_inc(q["y"], 1)

                dve.wait_ge(comb_done, PAIRS * (layer + 1))
                again(0)
                with dve.Fori(1, MAX_EXTRA) as j:
                    dve.wait_ge(q["comb"], j)
                    again(j)
                dve.wait_ge(q["comb"], MAX_EXTRA)

            moe(0)
            scale_rows(2)
            evac_xT(8, [G_KV, G_Q], None)
            dve.memset(cT[:, :, NG, :], 0.0).then_inc(dve_step, 1)
            steps[0] += 1

            def evac_kv(m, t):
                n = (L_KV0, L_KV1, L_KV1 + 1)[m]
                dve.wait_ge(used, 2 * n + t + 1)
                ins = dve.tensor_copy(KV[:, t, 2 * m:2 * m + 2, :], bank[(4, 4, 6)[m] + t][:, :].rearrange("p (u n) -> p u n", u=2))
                if m:
                    step(ins)
                    rotate(KV[:, t, 2 * m, :].rearrange("p (g d) -> p g d", g=NG), t)
                else:
                    ins.then_inc(projN_read, 1)

            def rotate(x4, t):
                m = x4.shape[1]
                lead = c("cos")[:, t * ROPE:(t + 1) * ROPE], c("sin")[:, t * ROPE:(t + 1) * ROPE]
                cos, sin = (v.rearrange("p (o n) -> p o n", o=1).to_broadcast([P, m, ROPE]) for v in lead)
                ra, rb = rope_a[:, 0:m, :], rope_b[:, 0:m, :]
                dve.tensor_tensor(ra, x4[:, :, 0:ROPE], cos, ALU.mult).then_inc(dve_step, 1)
                dve.tensor_tensor(rb[:, :, 0:HALF], x4[:, :, HALF:ROPE], sin[:, :, 0:HALF], ALU.mult).then_inc(dve_step, 1)
                dve.tensor_tensor(rb[:, :, HALF:ROPE], x4[:, :, 0:HALF], sin[:, :, HALF:ROPE], ALU.mult).then_inc(dve_step, 1)
                steps[0] += 3
                dve.wait_ge(dve_step, steps[0])
                dve.tensor_tensor(x4[:, :, 0:ROPE], ra, rb, ALU.add).then_inc(projN_read, 1)

            for t in range(T):
                evac_kv(0, t)
            dve.wait_ge(dve_step, steps[0])
            for b in range(2):
                for half in range(2):
                    dve.wait_ge(cT_done, 2 * b + half + 1)
                    dve.tensor_copy(cT[:, b, 2 * half:2 * half + 2, :],
                                    bank[2 * b + half][0:DH, :].rearrange("p (g t) -> p g t", g=2)).then_inc(cT_ready, 1)
            dve.wait_ge(cT_done, 5)
            dve.tensor_copy(cT[:, :, NG, 0:CB], bank[6][0:DH, 0:2 * CB].rearrange("p (b l) -> p b l", b=2)).then_inc(cT_ready, 1)
            for b in range(2):
                dve.wait_ge(used, 2 * L_CMP + b + 1)
                if b:
                    dve.wait_ge(c1s_ready, 1)
                step(dve.tensor_copy(cbias[:, :], bank[6 + b][0:DH, NG * NCMP:NG * NCMP + 1]))
                dve.tensor_scalar(c1[:, :], bank[6 + b][0:DH, 0:NG * NCMP], cbias[:, 0:1], None, ALU.add).then_inc(c1_ready, 1)
                dve.wait_ge(c1_exp, b + 1)
                step(dve.tensor_scalar(c1e[:, :], c1e[:, :], 1.0, None, ALU.add))
                step(dve.reciprocal(c1e[:, :], c1e[:, :]))
                dve.tensor_tensor(c1s[b][:, :], c1[:, :], c1e[:, :], ALU.mult).then_inc(c1s_ready, 1)
            for m in (1, 2):
                for t in range(T):
                    evac_kv(m, t)
            dve.wait_ge(c2_done, 1)
            step(dve.tensor_copy(kcn[:, :, :], bank[0][0:NCMP, 0:NG * DH].rearrange("p (g d) -> p g d", g=NG)))
            bc = lambda name: c(name)[0:NCMP, :].rearrange("p (o n) -> p o n", o=1).to_broadcast([NCMP, NG, ROPE])
            ra, rb = rope_a[0:NCMP, :, :], rope_b[0:NCMP, :, :]
            dve.wait_ge(projN_read, 6)
            step(dve.tensor_tensor(ra, kcn[:, :, 0:ROPE], bc("ccos"), ALU.mult))
            step(dve.tensor_tensor(rb[:, :, 0:HALF], kcn[:, :, HALF:ROPE], bc("csin")[:, :, 0:HALF], ALU.mult))
            step(dve.tensor_tensor(rb[:, :, HALF:ROPE], kcn[:, :, 0:HALF], bc("csin")[:, :, HALF:ROPE], ALU.mult))
            dve.tensor_tensor(kcn[:, :, 0:ROPE], ra, rb, ALU.add).then_inc(c2_ready, 1)
            dve.wait_ge(c2_done, 2)
            dve.tensor_copy(vcn[:, :, :], bank[1][0:NCMP, 0:NG * DH].rearrange("p (g d) -> p g d", g=NG)).then_inc(c2_ready, 1)
            dve.wait_ge(kcT_done, 1)
            dve.tensor_copy(kcT[:, :, :], bank[2][:, 0:2 * NCMP].rearrange("p (a n) -> p a n", a=2)).then_inc(kcT_ready, 1)
            dve.wait_ge(c2_ready, 1)
            for u in range(2):
                for t in range(T):
                    dve.wait_ge(used, 2 * (L_Q + u) + t + 1)
                    src = bank[4 + 2 * u + t][:, :].rearrange("p (r j d) -> p r j d", r=2, j=HG)
                    for r in range(2):
                        x4 = QN[:, t, u, :, r, :]
                        step(dve.tensor_scalar(x4, src[:, r, :, :], float(DH) ** -0.5, None, ALU.mult))
                        rotate(x4, t)
                if u == 0:
                    dve.wait_ge(ngate_exp, 1)
                    g = ngate[:, :, :, :].rearrange("p t h b -> p (t h b)")
                    step(dve.tensor_scalar(g, g, 1.0, None, ALU.add))
                    step(dve.reciprocal(g, g))
            for i in range(6):
                dve.wait_ge(qkT_done, i + 1)
                if i < 2:
                    dst = KTn[:, i, :, :]
                else:
                    dst = QT[:, (i - 2) // 2, 2 * (i % 2):2 * (i % 2) + 2, :]
                dve.tensor_copy(dst, bank[i % 4][:, :].rearrange("p (a t) -> p a t", a=2)).then_inc(qkT_ready, 1)
            for t in range(T):
                dve.wait_ge(sc_done, t + 1)
                pc = Pc[:, t, :, 0:NCMP]
                for r in range(2):
                    step(dve.tensor_tensor(Pc[:, t, :, :].rearrange("p (a r j) n -> p r a j n", a=2, r=2)[:, r, :, :, 0:NCMP],
                                           bank[4 + 2 * t + r][:, 0:NH * 8].rearrange("p (a j n) -> p a j n", a=2, j=HG)[:, :, :, 0:NCMP],
                                           c("cmask")[:, t * NCMP:(t + 1) * NCMP].rearrange("p (o q n) -> p o q n", o=1, q=1)
                                           .to_broadcast([P, 2, HG, NCMP]), ALU.add))
                step(dve.tensor_reduce(ccoef[:, :], pc, AX.X, ALU.max))
                bcc = ccoef[:, :].rearrange("p (h o) -> p h o", o=1).to_broadcast([P, NH, NCMP])
                dve.tensor_tensor(pc, pc, bcc, ALU.subtract).then_inc(sc_ready, 1)
                dve.wait_ge(pc_exp, t + 1)
                step(dve.tensor_reduce(ccoef[:, :], pc, AX.X, ALU.add))
                step(dve.reciprocal(ccoef[:, :], ccoef[:, :]))
                step(dve.scalar_tensor_tensor(ccoef[:, :], ccoef[:, :], c("cvalid")[:, t:t + 1], ngate[:, t, :, 0], ALU.mult, ALU.mult))
                dve.tensor_tensor(pc, pc, bcc, ALU.mult).then_inc(pc_ready, 1)
                dve.wait_ge(pc_ready, t + 1)
            for i in range(8):
                dve.wait_ge(pcT_done, i + 1)
                dve.tensor_copy(PcT[:, 4 * (i % 4):4 * (i % 4) + 4, (i // 4) * P:(i // 4 + 1) * P],
                                bank[i % 4][0:NCMP, :].rearrange("p (h t) -> p h t", h=4)).then_inc(pcT_ready, 1)

            def maxima(u):
                n = P * (u // NH + 1)
                dve.wait_ge(sN_done, u + 1)
                if u >= 2:
                    dve.wait_ge(eN_ready, 2 * (u - 1))
                dve.tensor_reduce(nmax[:, u % 2, :], bank[u % 2][:, 0:2 * n].rearrange("p (b n) -> p b n", b=2), AX.X, ALU.max,
                                  negate=True).then_inc(mN_ready, 1)

            def normalise(u):
                t, hd = u // NH, u % NH
                n = P * (t + 1)
                dve.wait_ge(eN_ready, 2 * (u + 1))
                step(dve.reciprocal(ncoef[:, u % 2, :], lsum[:, u % 2, :]))
                step(dve.tensor_tensor(ncoef[:, u % 2, :], ncoef[:, u % 2, :], ngate[:, t, hd, 1:3], ALU.mult))
                for b in range(2):
                    dve.tensor_scalar(PN[:, u % 2, b * n:(b + 1) * n], PN[:, u % 2, b * n:(b + 1) * n],
                                      ncoef[:, u % 2, b:b + 1], None, ALU.mult).then_inc(pN_ready, 1)

            maxima(0)
            for u in range(T * NH):
                if u + 1 < T * NH:
                    maxima(u + 1)
                normalise(u)
                if u % 8 == 7:
                    b = u // 8
                    dve.wait_ge(oN_done, u + 1)
                    dve.tensor_copy(on[:, b // 2, :, 64 * (b % 2):64 * (b % 2) + 64],
                                    bank[4 + b][:, :].rearrange("p (q k) -> p k q", k=KT)).then_inc(oN_read, 1)
            evac_eT(4, None)
            add_out(L_NOUT)
            moe(1)
            scale_rows(4)
            dve.wait_ge(gfin_in, 16)
            for t in range(T):
                dve.scalar_tensor_tensor(res[:, t, :], h[:, t, :], rstd[:, t:t + 1], gfin, ALU.mult, ALU.mult).then_inc(dve_final, 1)

        @block.tensor
        def _(pe):
            mm = nc.tensor.matmul

            def transposes(src, n_ready, ready, done):
                pe.wait_ge(ready, n_ready)
                for b in range(4):
                    for k in (2 * b, 2 * b + 1):
                        for t in range(T):
                            last = nc.tensor.transpose(bank[b][:, (k % 2) * S + t * P:(k % 2) * S + (t + 1) * P],
                                                       src[:, t, k, :], ident)
                    last.then_inc(done, 1)

            def rows(n, xt, b, free=None):
                w = columns(n)
                arrived(pe, n)
                for t in range(T):
                    if free:
                        free(t)
                    for k in range(KT):
                        ins = mm(bank[b + t][:, :], xt[:, k, t * P:(t + 1) * P], w[:, k, :], start=(k == 0), stop=(k == KT - 1))
                    ins.then_inc(used, 1)

            pe.wait_ge(small_in, 16 * N_SMALL)
            transposes(xs, 2, xs_ready, xt_done)
            pe.wait_ge(xt_ready, 4)
            for t in range(T):
                for k in range(KT):
                    ins = mm(bank[0][:, t * NGATE:(t + 1) * NGATE], xT[0][:, k, t * P:(t + 1) * P], w_mgate[:, k, :],
                             start=(k == 0), stop=(k == KT - 1))
            ins.then_inc(mgate_done, 1)
            for u in range(2):
                arrived(pe, u)
                w = columns(u)
                for hd in range(MH):
                    for k in range(KT):
                        ins = mm(bank[4 + 2 * u + hd // 2][:, (hd % 2) * S:(hd % 2 + 1) * S], w[:, k, hd * P:(hd + 1) * P], xT[0][:, k, :],
                                 start=(k == 0), stop=(k == KT - 1))
                    if hd % 2:
                        ins.then_inc(used, 1)
                if u == 0:
                    pe.wait_ge(mgate_ready, 1)
                    for i in range(2):
                        for t in range(T):
                            nc.tensor.transpose(bank[1][0:MH, i * S + t * P:i * S + (t + 1) * P],
                                                gpre[:, t, i * MH:(i + 1) * MH], ident).then_inc(mgateT_done, 1)
            for u in range(2, 6):
                rows(u, xT[0], 4 + 2 * (u % 2), lambda t: pe.wait_ge(projA_read, 2 * (u - 2) + t + 1))
            pe.wait_ge(am_ready, 1)
            for i, g in enumerate((gA[5], gA[7])):
                for t in range(T):
                    ins = nc.tensor.transpose(bank[3][:, 8 * i + MH * t:8 * i + MH * (t + 1)], g[:, t * P:(t + 1) * P],
                                              ident[0:MH, 0:MH])
            ins.then_inc(col_done, 1)
            pe.wait_ge(const_ready, 3)
            sel = c("sel").rearrange("p (h m) -> p h m", h=MH)

            def exponents(hd):
                if hd >= 2:
                    pe.wait_ge(eA_ready, 2 * (hd - 1))
                b = bank[hd % 2]
                mm(b[:, 0:S], sel[0:MH, hd, :], gA[6][:, 0:S], start=True, stop=True)
                mm(b[:, 0:P], ident_b[:, :], mask_kb[:, :], start=False, stop=True, skip_group_check=True)
                mm(b[:, S:S + P], sel[0:MH, hd, :], gA[6][:, P:S], start=True, stop=True)
                mm(b[:, S:S + P], ident_b[:, :], mask_kb[:, :], start=False, stop=True, skip_group_check=True).then_inc(eA_done, 1)

            exponents(0)
            pe.wait_ge(col_ready, 2)
            pe.wait_ge(og_ready, 4)
            pe.wait_ge(projA_read, 8)
            for hd in range(MH):
                if hd + 1 < MH:
                    exponents(hd + 1)
                if hd:
                    pe.wait_ge(pA_ready, hd)
                mm(bank[2][:, 0:S], qkT[:, MH + hd, 0:P], qkT[:, hd, :], start=True, stop=True)
                mm(bank[2][:, S:S + P], qkT[:, MH + hd, P:S], qkT[:, hd, P:S], start=True, stop=True).then_inc(sA_done, 1)
                pe.wait_ge(pA_ready, hd + 1)
                p = PA[:, hd % 2, :]
                for t, tiles in ((0, [(0, 0)]), (1, [(P, 0), (S, 1)])):
                    for n, (at, s) in enumerate(tiles):
                        mm(bank[4 + hd][:, t * MDV:(t + 1) * MDV], p[:, at:at + P], vA[:, s, hd, :],
                           start=(n == 0), stop=(n == t))
                    for n, (at, s) in enumerate(tiles):
                        ins = mm(bank[3][:, 16 + t * MH + hd:17 + t * MH + hd], p[:, at:at + P], ones[:, 0:1],
                                 start=(n == 0), stop=(n == t))
                ins.then_inc(numA_done, 1)
            transposes(hsA, T * MH, hsA_ready, hsT_done)
            pe.wait_ge(hsT_ready, 4)
            for u in range(2):
                rows(L_AOUT + u, xT[0], 4 + 2 * u)

            def moe(layer):
                g = G_MOE + layer
                transposes(xs, 2 * (2 * layer + 2), xs_ready, xt_done)
                pe.wait_ge(xt_ready, (8, 20)[layer])
                for t in range(T):
                    for k in range(KT):
                        ins = mm(bank[4][:, t * 64:t * 64 + NR], xT[0][:, k, t * P:(t + 1) * P], w_route[:, layer, k, :],
                                 start=(k == 0), stop=(k == KT - 1))
                ins.then_inc(route_done, 1)
                pe.wait_ge(hot_ready, layer + 1)
                before = c("before")
                mm(bank[5][:, 0:NE], before, hot[2][:, 0, :], start=True, stop=True)
                mm(bank[5][:, NE:2 * NE], ones, hot[2][:, 0, :], start=True, stop=False)
                mm(bank[5][:, NE:2 * NE], before, hot[2][:, 1, :], start=False, stop=True)
                mm(bank[5][:, 2 * NE:3 * NE], ones, hot[2][:, 0, :], start=True, stop=False)
                mm(bank[5][:, 2 * NE:3 * NE], ones, hot[2][:, 1, :], start=False, stop=True).then_inc(rank_done, 1)
                pe.wait_ge(sel_ready, 2 * (layer + 1))
                for k in range(KT):
                    if k >= 4:
                        pe.wait_ge(*((gather_a, 4 * layer + (k - 4) // 2 + 1) if k % 2 else (gather_v, 4 * layer + (k - 4) // 2 + 1)))
                    for t in range(T):
                        ins = mm(bank[k % 4][:, :], xs[:, t, k, :], Sel[:, t, :], start=(t == 0), stop=(t == T - 1))
                    ins.then_inc(gather_done, 1)
                pe.wait_ge(diag_ready, 4 * T * (layer + 1))
                for t in range(T):
                    mm(bank[6 + t][:, :], ones, diag[:, t, :, :].rearrange("p i n -> p (i n)"), start=True, stop=True).then_inc(bcast_done, 1)
                pe.wait_ge(gather_v, 4 * (layer + 1))
                pe.wait_ge(gather_a, 4 * (layer + 1))
                pe.wait_ge(bcast_ready, T * (layer + 1))
                base, p0 = L_MOE[layer], PAIRS * layer

                def combine(i, j, start=False, stop=False):
                    pe.wait_ge(y_v, p0 + j + 1 + TURN * i)
                    pe.wait_ge(y_a, p0 + j + 1 + TURN * i)
                    pe.wait_ge(gt_ready, p0 + j + 1 + TURN * i)
                    for t in range(T):
                        for b in range(2):
                            ins = mm(bank[2 * t + b][:, :], GT[:, j % 2, t * P:(t + 1) * P], Y[:, j % 2, b * 512:(b + 1) * 512],
                                     start=start, stop=stop)
                    ins.then_inc(comb_done, 1)

                def turn(i, first=False):
                    for j in range(TURN):
                        pe.wait_ge(win_ready, 2 * (p0 + j + 1) + 2 * TURN * i)
                        if not first or j:
                            pe.wait_ge(hid_ready, p0 + j + TURN * i)
                        for m in range(2):
                            n = base + 3 * j + m
                            arrived(pe, n, i)
                            w = pair_up(n)
                            for k in range(KT):
                                for r in range(2):
                                    ins = mm(bank[4][r * WIN:(r + 1) * WIN, m * F:(m + 1) * F], xwin[:, j % 2, r, k, :], w[:, r, k, :],
                                             start=(k == 0), stop=(k == KT - 1))
                                if k % 4 == 3:
                                    ins.then_inc(used, 1)
                        if not first or j:
                            combine(i, j - 1, start=(first and j == 1))
                        pe.wait_ge(hid_ready, p0 + j + 1 + TURN * i)
                        if not first or j:
                            pe.wait_ge(hT_ready, p0 + j + TURN * i)
                        for f in range(FT):
                            ins = nc.tensor.transpose(bank[7][:, f * P:(f + 1) * P], hid[:, f * P:(f + 1) * P], ident)
                        ins.then_inc(hT_done, 1)
                        pe.wait_ge(hT_ready, p0 + j + 1 + TURN * i)
                        n = base + 3 * j + 2
                        arrived(pe, n, i)
                        w = pair_down(n)
                        for b in range(2):
                            for f in range(FT):
                                for r in range(2):
                                    ins = mm(bank[5 + b][r * WIN:(r + 1) * WIN, :], hidT[:, f, r * WIN:(r + 1) * WIN],
                                             w[:, r, f, b * 512:(b + 1) * 512], start=(f == 0), stop=(f == FT - 1))
                            ins.then_inc(used, 1)

                turn(0, first=True)
                with pe.Fori(1, TURNS) as i:
                    turn(i)
                combine(TURNS, -1, stop=True)
                q = extra[layer]
                n_top = pe.value_load(table[0:1, T_COUNT:T_COUNT + 1], min_val=0, max_val=S)
                with pe.If(n_top > WIN):
                    def again(j):
                        pe.wait_ge(q["w"], 48 * j + 48)
                        pe.wait_ge(q["win"], j + 1)
                        for m in range(2):
                            w = pair_up(m)
                            for k in range(KT):
                                ins = mm(bank[4][0:WIN, m * F:(m + 1) * F], xwin[:, 0, 0, k, :], w[:, 0, k, :],
                                         start=(k == 0), stop=(k == KT - 1))
                        ins.then_inc(q["up"], 1)
                        pe.wait_ge(q["hid"], j + 1)
                        for f in range(FT):
                            ins = nc.tensor.transpose(bank[7][:, f * P:(f + 1) * P], hid[:, f * P:(f + 1) * P], ident)
                        ins.then_inc(q["hT_done"], 1)
                        pe.wait_ge(q["hT"], j + 1)
                        for b in range(2):
                            for f in range(FT):
                                ins = mm(bank[5 + b][0:WIN, :], hidT[:, f, 0:WIN], pair_down(2)[:, 0, f, b * 512:(b + 1) * 512],
                                         start=(f == 0), stop=(f == FT - 1))
                        ins.then_inc(q["down"], 1)
                        pe.wait_ge(q["gt"], j + 1)
                        pe.wait_ge(q["y"], 2 * j + 2)
                        for t in range(T):
                            for b in range(2):
                                ins = mm(bank[2 * t + b][:, :], GT[0:WIN, 0, t * P:(t + 1) * P], Y[0:WIN, 0, b * 512:(b + 1) * 512],
                                         start=False, stop=True, skip_group_check=True)
                        ins.then_inc(q["comb"], 1)

                    again(0)
                    with pe.Fori(1, MAX_EXTRA) as j:
                        again(j)

            moe(0)
            transposes(xs, 6, xs_ready, xt_done)
            pe.wait_ge(xt_ready, 16)
            rows(L_KV0, xT[0], 4)
            pe.wait_ge(projN_read, 2)
            for b in range(2):
                for half in range(2):
                    for g in (2 * half, 2 * half + 1):
                        for t in range(T):
                            ins = nc.tensor.transpose(bank[2 * b + half][0:DH, (g % 2) * S + t * P:(g % 2) * S + (t + 1) * P],
                                                      KV[:, t, b, g * DH:(g + 1) * DH], ident)
                    ins.then_inc(cT_done, 1)
            for b in range(2):
                ins = nc.tensor.transpose(bank[6][0:DH, b * CB:(b + 1) * CB], pe_in[:, b, :], ident[0:CB, 0:CB])
            ins.then_inc(cT_done, 1)
            pe.wait_ge(cT_ready, 5)
            arrived(pe, L_CMP)
            for b in range(2):
                w = ring[0:DH, L_CMP % RING, b * 2048:(b + 1) * 2048].rearrange("d (l f) -> d l f", l=CB)
                for l in range(CB):
                    ins = mm(bank[6 + b][0:DH, 0:(NG + 1) * NCMP].rearrange("p (g n) -> p g n", g=NG + 1), w[:, l, :],
                             cT[:, b, :, l:l + CS * (NCMP - 1) + 1:CS], start=(l == 0), stop=(l == CB - 1))
                ins.then_inc(used, 1)
            rows(L_KV1, xT[0], 4)
            for b in range(2):
                pe.wait_ge(c1s_ready, b + 1)
                for g in range(NG):
                    ins = mm(bank[b][0:NCMP, g * DH:(g + 1) * DH], c1s[b][:, g * NCMP:(g + 1) * NCMP], w_cmp2[:, b, :],
                             start=True, stop=True)
                ins.then_inc(c2_done, 1)
            rows(L_KV1 + 1, xT[0], 6)
            pe.wait_ge(c2_ready, 2)
            for a in range(2):
                ins = nc.tensor.transpose(bank[2][:, a * NCMP:(a + 1) * NCMP],
                                          kcn[:, 2 * a:2 * a + 2, :].rearrange("p g d -> p (g d)"), ident[0:NCMP, 0:NCMP])
            ins.then_inc(kcT_done, 1)
            for t in range(T):
                for k in range(KT):
                    ins = mm(bank[0][:, t * 64:t * 64 + NBR * NH], xT[1][:, k, t * P:(t + 1) * P], w_ngate[:, k, :],
                             start=(k == 0), stop=(k == KT - 1))
            ins.then_inc(ngate_done, 1)
            for u in range(2):
                rows(L_Q + u, xT[1], 4 + 2 * u, lambda t: pe.wait_ge(projN_read, 2 * u + t + 3))
            pe.wait_ge(kcT_ready, 1)
            pe.wait_ge(ngate_exp, 1)
            for i in range(6):
                if i >= 4:
                    pe.wait_ge(qkT_ready, i - 3)
                if i == 2:
                    pe.wait_ge(projN_read, 14)
                for m in range(2):
                    for t in range(T):
                        if i < 2:
                            src = KV[:, t, 2 + 2 * i, m * P:(m + 1) * P]
                        else:
                            a, j = (i - 2) // 2, 2 * (i % 2) + m
                            src = QN[:, t, a, j, :, :].rearrange("p r d -> p (r d)")
                        ins = nc.tensor.transpose(bank[i % 4][:, m * S + t * P:m * S + (t + 1) * P], src, ident)
                ins.then_inc(qkT_done, 1)
            pe.wait_ge(qkT_ready, 6)

            def q_of(hd, t):
                g, j = hd // HG, hd % HG
                lo = DH * (g % 2)
                return QT[lo:lo + DH, g // 2, j, t * P:(t + 1) * P], lo, g

            for t in range(T):
                for hd in range(NH):
                    q, lo, g = q_of(hd, t)
                    at = ((g // 2) * HG + hd % HG) * 16
                    ins = mm(bank[4 + 2 * t + g % 2][:, at:at + NCMP], q, kcT[lo:lo + DH, g // 2, :], start=True, stop=True)
                ins.then_inc(sc_done, 1)
            for i in range(8):
                t = i // 4
                pe.wait_ge(pc_ready, t + 1)
                if i >= 4:
                    pe.wait_ge(pcT_ready, i - 3)
                for m in range(4):
                    ins = nc.tensor.transpose(bank[i % 4][0:NCMP, m * P:(m + 1) * P], Pc[:, t, 4 * (i % 4) + m, 0:NCMP], ident)
                ins.then_inc(pcT_done, 1)
            pe.wait_ge(pcT_ready, 8)

            def scores(u):
                t, hd = u // NH, u % NH
                n = P * (t + 1)
                if u >= 2:
                    pe.wait_ge(eN_ready, 2 * (u - 1))
                q, lo, g = q_of(hd, t)
                for b in range(2):
                    mm(bank[u % 2][:, b * n:(b + 1) * n], q, KTn[lo:lo + DH, b, g // 2, 0:n], start=True, stop=True)
                    ins = mm(bank[u % 2][:, b * n + t * P:b * n + n], ident_b[:, :], mask_qb[:, :], start=False, stop=True,
                             skip_group_check=True)
                ins.then_inc(sN_done, 1)

            def turned(u):
                n = 2 * (u // NH + 1)
                pe.wait_ge(pN_ready, 2 * (u + 1))
                if u >= 2:
                    pe.wait_ge(ptN_a, u - 1)
                for m in range(n):
                    ins = nc.tensor.transpose(bank[2 + u % 2][:, m * P:(m + 1) * P], PN[:, u % 2, m * P:(m + 1) * P], ident)
                ins.then_inc(ptN_done, 1)

            def outputs(u):
                t, hd = u // NH, u % NH
                g = hd // HG
                o = bank[4 + u // 8][:, (hd % 8) * DH:(hd % 8 + 1) * DH]
                pe.wait_ge(ptN_a, u + 1)
                mm(o, PcT[:, hd, t * P:(t + 1) * P], vcn[:, g, :], start=True, stop=False)
                n = 2 * (t + 1)
                for m in range(n):
                    b, s = m // (t + 1), m % (t + 1)
                    ins = mm(o, PTn[:, u % 2, m * P:(m + 1) * P], KV[:, s, 3 + 2 * b, g * DH:(g + 1) * DH], start=False, stop=(m == n - 1))
                ins.then_inc(oN_done, 1)

            scores(0)
            for u in range(T * NH):
                if u + 1 < T * NH:
                    scores(u + 1)
                if u:
                    outputs(u - 1)
                turned(u)
            outputs(T * NH - 1)
            transposes(on, 4, oN_read, hsT_done)
            pe.wait_ge(hsT_ready, 8)
            for u in range(2):
                rows(L_NOUT + u, xT[0], 4 + 2 * u)
            moe(1)


N_SMALL = 22
_INS = ['x', 'mlstm_norm', 'mlstm_w_in', 'mlstm_gate_bias', 'mlstm_head_norm', 'mlstm_w_out', 'kv_norm', 'kv_w',
        'cmp_pe_k', 'cmp_w1_k', 'cmp_w2_k', 'cmp_pe_v', 'cmp_w1_v', 'cmp_w2_v', 'nsa_norm', 'nsa_w_q', 'nsa_w_out',
        'moe_norm', 'moe_w_group', 'moe_b_group', 'moe_w_router', 'moe_b_router', 'moe_w_gate', 'moe_w_up',
        'moe_w_down', 'final_norm']


def kernel(**inputs):
    import concourse.bacc as bacc
    from concourse.bass_utils import run_bass_kernel_spmd as run

    nc = bacc.Bacc("TRN2", target_bir_lowering=False, num_devices=1,
                   dynamic_dma_scratch_size=1024)
    arrays, args = {}, []
    for name in _INS:
        a = np.ascontiguousarray(inputs[name])
        arrays[f"in_{name}"] = a
        args.append(nc.dram_tensor(f"in_{name}", a.shape, mybir.dt.from_np(a.dtype), kind="ExternalInput").ap())
    consts, place = constants()
    arrays["in_consts"] = consts
    args.append(nc.dram_tensor("in_consts", consts.shape, mybir.dt.float32, kind="ExternalInput").ap())
    args.append(nc.dram_tensor("out_h", (1, S, D), mybir.dt.float32, kind="ExternalOutput").ap())
    build(nc, *args, place, consts.shape[1])
    r = run(nc, [arrays], core_ids=[0])
    return r.results[0]["out_h"]
```

```python
from contextlib import ExitStack

import numpy as np
import concourse.bass as bass
from concourse import mybir

P = 128
D = 1024
S = 256
T = S // P
KT = D // P
EPS = 1e-6
NEG = -1e30
MH, MDK, MDV = 4, 128, 256
SOFTCAP = 15.0
NGATE = 2 * MH
O_GATES = 2 * MH * MDK + 2 * MH * MDV
NH, DH, NG = 16, 64, 4
HG = NH // NG
ROPE = DH // 4
HALF = ROPE // 2
THETA = 500000.0
CB, CS = 32, 16
NBUF = 3
NCMP = (S - CB) // CS + 1
NBR = 3
MG, ME = 4, 8
NE = MG * ME
F = D // 4
FT = F // P
NR = MG + NE
SLOTS = 2 * S
ST = SLOTS // P
WIN = 64
MAX_EXTRA = (SLOTS - 1) // WIN
PADDED = SLOTS + WIN
LC = 512
LOAD = KT * LC
RING = 6
L_A, L_AOUT = 0, 6
L_MOE = (8, 62)
SPARES = (4, 5)
L_KV0, L_CMP, L_KV1, L_Q, L_NOUT = 54, 55, 56, 58, 60
N_LOADS = 108
PAIRS = NE // 2
TURN = 2
TURNS = PAIRS // TURN
AREA = 16384
KEY = S
SPLIT = list(range(L_A, L_AOUT + 2)) + [L_KV0, L_KV1, L_KV1 + 1, L_Q, L_Q + 1, L_NOUT, L_NOUT + 1]
X_A, X_AOUT, X_KV, X_Q, X_NOUT = range(5)
QUARTERS = 4
LANDED, _count = [], [0] * RING
for _n in range(N_LOADS):
    _count[_n % RING] += 2 if _n == L_CMP else 1
    LANDED.append(_count[_n % RING])


def constants():
    f32 = np.float32
    row, col = np.arange(P)[:, None], np.arange(P)[None, :]
    inv = np.power(f32(THETA), -np.arange(HALF, dtype=f32) * f32(2.0 / ROPE)).astype(f32)

    def rope(pos):
        ang = (pos.astype(f32)[:, None] * inv[None, :]).astype(f32)
        c, s = np.cos(ang).astype(f32), np.sin(ang).astype(f32)
        return np.concatenate([c, c], 1), np.concatenate([-s, s], 1)

    c, s = rope(np.arange(S))
    tok = lambda a: a.reshape(T, P, -1).transpose(1, 0, 2).reshape(P, -1)
    cc, cs = rope(np.arange(NCMP) * CS + CB - 1)
    pad = lambda a: np.concatenate([a, np.zeros((P - a.shape[0], a.shape[1]), f32)])
    sel = np.zeros((P, MH, P), f32)
    for h in range(MH):
        sel[h, h] = 1
    ends = np.arange(NCMP) * CS + CB - 1
    ok = ends[None, :] <= np.arange(S)[:, None]
    parts = {
        "ident": np.eye(P), "mask_q": np.where(col > row, NEG, 0), "mask_k": np.where(col < row, NEG, 0),
        "before": row < col, "ones": np.ones((P, P)), "iota": np.tile(np.arange(SLOTS), (P, 1)),
        "cos": tok(c), "sin": tok(s), "ccos": pad(cc), "csin": pad(cs),
        "cmask": tok(np.where(ok, 0, NEG)), "cvalid": tok(ok.any(1)[:, None]),
        "sel": sel.reshape(P, -1), "slot_key": KEY * (2 * np.arange(PAIRS)[None, :] + row // WIN) + row % WIN, "lane": row % WIN,
        "key_e": np.tile(KEY * np.arange(NE), (P, 1)),
        "ones_s": np.ones((P, S)), "desc": np.tile(np.arange(ME, 0, -1), (P, 1)),
    }
    at, place = 0, {}
    for name, a in parts.items():
        place[name] = (at, at + a.shape[1])
        at += a.shape[1]
    return np.ascontiguousarray(np.concatenate([np.asarray(a, f32) for a in parts.values()], 1)), place


def build(nc, x, mlstm_norm, mlstm_w_in, mlstm_gate_bias, mlstm_head_norm, mlstm_w_out, kv_norm, kv_w,
          cmp_pe_k, cmp_w1_k, cmp_w2_k, cmp_pe_v, cmp_w1_v, cmp_w2_v, nsa_norm, nsa_w_q, nsa_w_out,
          moe_norm, moe_w_group, moe_b_group, moe_w_router, moe_b_router, moe_w_gate, moe_w_up,
          moe_w_down, final_norm, consts, out, place, n_const):
    fp32, bf16, i32, fp32r = mybir.dt.float32, mybir.dt.bfloat16, mybir.dt.int32, mybir.dt.float32r
    ALU, ACT, AX = mybir.AluOpType, mybir.ActivationFunctionType, mybir.AxisListType
    ds = bass.ds
    ctx = ExitStack()
    with ctx:
        def sb(name, shape, dt=fp32):
            return ctx.enter_context(nc.sbuf_tensor(name, shape, dt))

        def sem(name):
            return ctx.enter_context(nc.semaphore(name))

        def twin(name, at, shape):
            with ExitStack() as around:
                if at:
                    around.enter_context(nc.sbuf_tensor(f"before_{name}", [P, at], fp32))
                return around.enter_context(nc.sbuf_tensor(name, [P] + shape, fp32r))

        XS_AT = RING * LOAD
        AREA_AT = XS_AT + T * D
        ring_r = [twin(f"ring_r{i}", i * LOAD, [KT, LC]) for i in range(RING)]
        xs_r = twin("xs_r", XS_AT, [T, KT, P])
        hi_A, hi_N = twin("hi_A", AREA_AT + 11776, [KT, LC]), twin("hi_N", AREA_AT + 3072, [KT, LC])
        xs_wide = twin("xs_wide", XS_AT, [KT, S])
        x_lo_A, x_lo_kv = twin("x_lo_A", AREA_AT + 9728, [KT, S]), twin("x_lo_kv", AREA_AT + 14336, [KT, S])
        x_hi_q, x_lo_q = twin("x_hi_q", AREA_AT + 10240, [KT, S]), twin("x_lo_q", AREA_AT + 12288, [KT, S])
        x_hi, x_lo = (xs_wide, xs_wide, xs_wide, x_hi_q, xs_wide), (x_lo_A, x_lo_A, x_lo_kv, x_lo_q, x_lo_kv)
        xg_hi = twin("xg_hi", AREA_AT + 5632, [T, KT, P])
        Sel = twin("Sel", AREA_AT + 4608, [T, SLOTS])
        ring = sb("ring", [P, RING, LOAD])
        xs = sb("xs", [P, T, KT, P])
        area = sb("area", [P, AREA])
        const = sb("const", [P, n_const])
        h = sb("h", [P, T, D])
        xT = [sb(f"xT{i}", [P, KT, S]) for i in range(2)]
        bank = [ctx.enter_context(nc.psum_tensor(f"bank{i}", [P, 512], fp32)) for i in range(8)]

        A_BANK = (4, 0, 4, 0, 2, 4)
        C_BANK = (2, 3, 7)
        S_BANK = (0, 1, 6)

        def c(name):
            return const[:, place[name][0]:place[name][1]]

        ident, ones, iota = c("ident"), c("ones"), c("iota")
        ident_b = sb("ident_b", [P, P], bf16)
        mask_qb = sb("mask_qb", [P, P], bf16)
        mask_kb = sb("mask_kb", [P, P], bf16)
        gains = sb("gains", [P, 6, KT])
        G_A, G_HEAD, G_KV, G_Q, G_MOE = 0, 1, 2, 3, 4
        w_mgate = sb("w_mgate", [P, KT, NGATE])
        b_mgate = sb("b_mgate", [P, NGATE])
        w_ngate = sb("w_ngate", [P, KT, NBR * NH])
        w_route = sb("w_route", [P, 2, KT, NR])
        b_route = sb("b_route", [P, 2, NR])
        pe_in = sb("pe_in", [CB, 2, DH])
        w_cmp2 = sb("w_cmp2", [DH, 2, DH])
        sq = sb("sq", [P, T])
        ms = sb("ms", [P, T])
        rstd = sb("rstd", [P, T])
        q_scale, g_scale = sb("q_scale", [P, T]), sb("g_scale", [P, T])
        slot_key = c("slot_key")
        neghalf = sb("neghalf", [P, 8])

        def cut(a, b, shape=None, parts=P):
            v = area[0:parts, a:b]
            if shape:
                v = v.rearrange(shape[0], **shape[1])
            return v

        qkT = cut(0, 2048, ("p (u t) -> p u t", {"t": S}))
        vA = cut(2048, 4096, ("p (t h v) -> p t h v", {"t": T, "h": MH}))
        og = cut(4096, 6144, ("p (t h v) -> p t h v", {"t": T, "h": MH}))
        EA = cut(6144, 6912, ("p (b n) -> p b n", {"b": 2}))
        PA = cut(6912, 7680, ("p (b n) -> p b n", {"b": 2}))
        gA = [cut(7680 + i * S, 7680 + (i + 1) * S, parts=MH) for i in range(8)]
        tmpA = cut(9728, 11776, ("p (t h v) -> p t h v", {"t": T, "h": MH}))
        gpre = sb("gpre", [P, T, NGATE])
        a_col = sb("a_col", [P, T, MH])
        em_col = sb("em_col", [P, T, MH])
        ssA = sb("ssA", [P, T, MH])
        rA = sb("rA", [P, T, MH])
        uA = sb("uA", [P, T, MH])
        cA = sb("cA", [P, T, MH])
        KV = cut(0, 3072, ("p (t u n) -> p t u n", {"t": T, "u": 6}))
        QT = cut(3072, 7168, ("p (a r j t) -> p a r j t", {"a": 2, "r": 2, "j": HG}))
        KTn = cut(7168, 8192, ("p (b a t) -> p b a t", {"b": 2, "a": 2}))
        QN = cut(8192, 10240, ("p (t a j r d) -> p t a j r d", {"t": T, "a": 2, "j": HG, "r": 2}))
        cT = cut(10240, 12800, ("p (b g t) -> p b g t", {"b": 2, "g": NG + 1}), parts=DH)
        PN = cut(8192, 9728, ("p (b n) -> p b n", {"b": NBUF}))
        Pc = cut(9728, 10240, ("p (t h n) -> p t h n", {"t": T, "h": NH}))
        PcT = cut(10240, 14336, ("p (h t) -> p h t", {"h": NH}))
        PTn = cut(14336, 16384, ("p (b n) -> p b n", {"b": 4}))
        ngate = sb("ngate", [P, T, NH, NBR])
        rope_a = sb("rope_a", [P, 8, ROPE])
        rope_b = sb("rope_b", [P, 8, ROPE])
        c1 = sb("c1", [DH, NG * NCMP])
        c1e = sb("c1e", [DH, NG * NCMP])
        cbias = sb("cbias", [DH, 1])
        c1s = [sb(f"c1s{i}", [DH, NG * NCMP]) for i in range(2)]
        kcn = sb("kcn", [NCMP, NG, DH])
        vcn = sb("vcn", [P, NG, DH])
        kcT = sb("kcT", [P, 2, NCMP])
        ccoef = sb("ccoef", [P, NH])
        nmax = sb("nmax", [P, NBUF, 2])
        lsum = sb("lsum", [P, NBUF, 2])
        ncoef = sb("ncoef", [P, NBUF, 2])
        Xs = cut(0, 4608, ("p (k n) -> p k n", {"k": KT}))
        Y = cut(5632, 7680, ("p (b n) -> p b n", {"b": 2}))
        GT = cut(7680, 8192, ("p (b n) -> p b n", {"b": 2}))
        sg = cut(8192, 8448)
        hid = cut(8448, 8704)
        hidT = cut(8704, 8960, ("p (f n) -> p f n", {"f": FT}))
        g1, g2 = cut(8960, 9216), cut(9216, 9472)
        diag = cut(9472, 10496, ("p (t i n) -> p t i n", {"t": T, "i": 4}))
        bcast = cut(10496, 11520, ("p (i n) -> p i n", {"i": 4}))
        spare = cut(12288, 16384)
        spare_up = [v.rearrange("p a b -> p (a b)") for v in (xT[0][:, :, :], xs[:, :, :, :].rearrange("p t k q -> p t (k q)"))]
        xwin = xT[1][:, :, :].rearrange("p k t -> p (k t)").rearrange("p (b r k n) -> p b r k n", b=2, r=2, k=KT)
        keys = sb("keys", [P, T, NE])
        lg = sb("lg", [P, T, NR])
        r4 = [sb(f"r4_{i}", [P, T, MG]) for i in range(2)]
        r8 = [sb(f"r8_{i}", [P, T, ME]) for i in range(4)]
        r32 = sb("r32", [P, T, ME, MG])
        hot = [sb(f"hot{i}", [P, T, NE]) for i in range(3)]
        place32 = sb("place32", [P, T, NE])
        prod32 = sb("prod32", [P, 2, T, NE])
        first_slot = sb("first_slot", [P, NE])
        cum = sb("cum", [P, NE])
        counts = sb("counts", [P, NE])
        one = [sb(f"one{i}", [P, T]) for i in range(12)]
        gexp = sb("gexp", [P, T, MG])
        table = sb("table", [1, 64], i32)
        T_COUNT, T_XFIRST, T_XID = 32, 40, 48
        n_max = sb("n_max", [1, 1])
        ex = [sb(f"ex{i}", [P, NE]) for i in range(4)]
        ex7 = [cut(11520 + 256 * i, 11520 + 256 * i + MAX_EXTRA * NE, ("p (x e) -> p x e", {"e": NE})) for i in range(3)]
        exr = [sb(f"exr{i}", [P, MAX_EXTRA]) for i in range(5)]
        gfin = cut(0, 1024)
        res = cut(1024, 3072, ("p (t n) -> p t n", {"t": T}))

        load_in = [sem(f"load_in{i}") for i in range(RING)]
        used = sem("used")
        spare_in, spare_up_in, spare_used = sem("spare_in"), sem("spare_up_in"), sem("spare_used")
        hi_ready, parts_ready, mid_used, xh_ready, xl_ready, xg_ready, xgl_ready = map(sem, (
            "hi_ready", "parts_ready", "mid_used", "xh_ready", "xl_ready", "xg_ready", "xgl_ready"))
        x_in = [sem(f"x_in{t}") for t in range(T)]
        early_in = sem("early_in")
        const_in = sem("const_in")
        small_in = sem("small_in")
        gfin_in = sem("gfin_in")
        out_done = sem("out_done")
        h_ready = sem("h_ready")
        sq_ready = sem("sq_ready")
        ms_ready = sem("ms_ready")
        rstd_ready = sem("rstd_ready")
        xs_ready = sem("xs_ready")
        xt_done = sem("xt_done")
        xt_ready = sem("xt_ready")
        dve_step = sem("dve_step")
        act_step = sem("act_step")
        const_ready = sem("const_ready")
        dve_final = sem("dve_final")
        terms = sem("terms")
        neghalf_ready = sem("neghalf_ready")
        mgate_done, mgate_ready, mgateT_done = map(sem, ("mgate_done", "mgate_ready", "mgateT_done"))
        logf_ready, am_ready, col_done, col_ready = map(sem, ("logf_ready", "am_ready", "col_done", "col_ready"))
        em_ready = sem("em_ready")
        projA_read = sem("projA_read")
        og_ready = sem("og_ready")
        eA_done, eA_ready, sA_done, pA_ready, numA_done = map(sem, ("eA_done", "eA_ready", "sA_done", "pA_ready", "numA_done"))
        ssA_ready, uA_ready, powA_ready, hsA_ready, hsT_done, hsT_ready = map(sem, (
            "ssA_ready", "uA_ready", "powA_ready", "hsA_ready", "hsT_done", "hsT_ready"))
        projN_read = sem("projN_read")
        scale_ready = sem("scale_ready")
        q_ready = sem("q_ready")
        ngate_done, ngate_exp = map(sem, ("ngate_done", "ngate_exp"))
        cT_done, cT_ready, c1_ready, c1_exp, c1s_ready, c2_done, c2_ready, kcT_done, kcT_ready = map(sem, (
            "cT_done", "cT_ready", "c1_ready", "c1_exp", "c1s_ready", "c2_done", "c2_ready", "kcT_done", "kcT_ready"))
        qkT_done, qkT_v, qkT_a, qpad_ready, cpad_ready = map(sem, ("qkT_done", "qkT_v", "qkT_a", "qpad_ready", "cpad_ready"))
        sc_done, sc_ready, pc_exp, pc_ready, pcT_done, pcT_ready = map(sem, (
            "sc_done", "sc_ready", "pc_exp", "pc_ready", "pcT_done", "pcT_ready"))
        sN_done, mN_ready, eN_ready, pN_ready, ptN_done, ptN_a, oN_done, oN_read = map(sem, (
            "sN_done", "mN_ready", "eN_ready", "pN_ready", "ptN_done", "ptN_a", "oN_done", "oN_read"))
        route_done, route_sub, route_exp, route_sub2, route_exp2, hot_ready, rank_done = map(sem, (
            "route_done", "route_sub", "route_exp", "route_sub2", "route_exp2", "hot_ready", "rank_done"))
        sel_ready, diag_ready, bcast_done, bcast_ready, table_ready = map(sem, (
            "sel_ready", "diag_ready", "bcast_done", "bcast_ready", "table_ready"))
        gather_done, gather_v, gather_a, pad_ready = map(sem, ("gather_done", "gather_v", "gather_a", "pad_ready"))
        win_ready, silu_ready, hid_ready, hT_done, hT_ready, y_v, y_a, gt_ready, comb_done = map(sem, (
            "win_ready", "silu_ready", "hid_ready", "hT_done", "hT_ready", "y_v", "y_a", "gt_ready", "comb_done"))
        extra = [{n: sem(f"x_{n}{layer}") for n in ("step", "table", "w", "win", "up", "silu", "hid", "hT_done",
                                                     "hT", "down", "y", "gt", "comb")} for layer in range(2)]

        kpc = lambda w: w.rearrange("(p k) c -> p k c", k=KT)
        w_in, w_mout, w_kv, w_nq = map(kpc, (mlstm_w_in[0], mlstm_w_out[0], kv_w, nsa_w_q[0]))
        w_nout = nsa_w_out[0].rearrange("(k p) c -> p k c", p=P)
        pk = lambda g: g.rearrange("(p k) -> p k", k=KT)

        def columns(n):
            return ring[:, n % RING, :].rearrange("p (k c) -> p k c", k=KT)

        def pair_up(n):
            return ring[:, n % RING, :].rearrange("p (r k f) -> p r k f", r=2, k=KT)

        def pair_down_of(place):
            return place.rearrange("p (r f d) -> p r f d", r=2, f=FT)

        def pair_down(n):
            return pair_down_of(ring[:, n % RING, :])

        def arrived(eng, n, turn=0):
            eng.wait_ge(load_in[n % RING], 16 * LANDED[n] + 16 * turn)

        def moe_load(layer, j, m, first):
            return L_MOE[layer] + 3 * j + m - (0 if first else len(SPARES))

        def gates_used(layer, i, j, first):
            if first and 3 * j + 1 in SPARES:
                return spare_used, 3 * layer + 1
            return used, 2 * moe_load(layer, j, 1, first) + 2 + 2 * RING * i

        def down_used(layer, i, j, first, half):
            signal, value = gates_used(layer, i, j, first)
            return signal, value + half

        def hi_of(i):
            n = SPLIT[i]
            return (hi_A if n < L_AOUT + 2 else hi_N), ring_r[n % RING]

        KQ = KT // QUARTERS

        def hi_quarter(act, i, q):
            ks, n = slice(q * KQ, (q + 1) * KQ), SPLIT[i]
            arrived(act, n)
            if i and q % 2:
                act.wait_ge(used, 2 * SPLIT[i - 1] + q // 2 + 1)
            elif i:
                act.wait_ge(mid_used, 2 * (i - 1) + q // 2 + 1)
            act.activation(hi_of(i)[0][:, ks, :], columns(n)[:, ks, :], ACT.Copy).then_inc(hi_ready, 1)

        def lo_quarter(dve, i, q):
            ks, n = slice(q * KQ, (q + 1) * KQ), SPLIT[i]
            dve.wait_ge(hi_ready, QUARTERS * i + q + 1)
            dve.tensor_tensor(hi_of(i)[1][:, ks, :], columns(n)[:, ks, :], hi_of(i)[0][:, ks, :],
                              ALU.subtract).then_inc(parts_ready, 1)

        def x_quarter(eng, i, xt, lo, q, wait=None):
            ks = slice(q * KQ, (q + 1) * KQ)
            if lo:
                eng.wait_ge(xh_ready, QUARTERS * i + q + 1)
                eng.tensor_tensor(x_lo[i][:, ks, :], xt[:, ks, :], x_hi[i][:, ks, :], ALU.subtract).then_inc(xl_ready, 1)
            else:
                eng.wait_ge(*wait(q))
                eng.activation(x_hi[i][:, ks, :], xt[:, ks, :], ACT.Copy).then_inc(xh_ready, 1)

        def x_quarters(eng, i, xt, lo, wait):
            for q in range(QUARTERS):
                x_quarter(eng, i, xt, lo, q, wait)

        block = ctx.enter_context(nc.Block())

        @block.sync
        def _(sp):
            for t in range(T):
                sp.dma_start(h[:, t, :], x[0, t * P:(t + 1) * P, :]).then_inc(x_in[t], 16)
            sp.dma_start(ident, consts[:, 0:P]).then_inc(early_in, 16)
            sp.dma_start(gains[:, G_A, :], pk(mlstm_norm[0])).then_inc(early_in, 16)
            sp.dma_start(w_mgate[:, :, :], w_in[:, :, O_GATES:O_GATES + NGATE]).then_inc(early_in, 16)
            sp.dma_start(b_mgate[:, :], mlstm_gate_bias[0:1, :].to_broadcast([P, NGATE])).then_inc(early_in, 16)

            smalls = [
                (gains[:, G_HEAD, :], pk(mlstm_head_norm[0])),
                (gains[:, G_KV, :], pk(kv_norm)), (gains[:, G_Q, :], pk(nsa_norm[0])),
                (gains[:, G_MOE, :], pk(moe_norm[0])), (gains[:, G_MOE + 1, :], pk(moe_norm[1])),
                (w_ngate[:, :, :], w_nq[:, :, NH * DH:NH * DH + NBR * NH]),
                (pe_in[:, 0, :], cmp_pe_k), (pe_in[:, 1, :], cmp_pe_v),
                (w_cmp2[:, 0, :], cmp_w2_k), (w_cmp2[:, 1, :], cmp_w2_v),
            ]
            for i in range(2):
                smalls += [
                    (w_route[:, i, :, 0:MG], kpc(moe_w_group[i])), (w_route[:, i, :, MG:NR], kpc(moe_w_router[i])),
                    (b_route[:, i, 0:MG], moe_b_group[i:i + 1, :].to_broadcast([P, MG])),
                    (b_route[:, i, MG:NR], moe_b_router[i:i + 1, :].to_broadcast([P, NE])),
                ]
            assert len(smalls) == N_SMALL

            def load(n, src):
                if n >= RING:
                    sp.wait_ge(used, 2 * (n - RING + 1))
                sp.dma_start(columns(n), src).then_inc(load_in[n % RING], 16)

            def load_moe(layer):
                base = L_MOE[layer]

                def turn(i, first=False):
                    for j in range(TURN):
                        e = (i * TURN + j) * 2
                        for m, w in enumerate((moe_w_gate, moe_w_up, moe_w_down)):
                            if first and 3 * j + m in SPARES:
                                continue
                            n = moe_load(layer, j, m, first)
                            sp.wait_ge(used, 2 * (n - RING + 1) + 2 * RING * i)
                            if m == 2:
                                src = w[layer, ds(e, 2)].rearrange("r (f p) d -> p r f d", p=P)
                                sp.dma_start(pair_down(n), src).then_inc(load_in[n % RING], 16)
                            else:
                                src = w[layer, ds(e, 2)].rearrange("r (p k) f -> p r (k f)", k=KT)
                                sp.dma_start(ring[:, n % RING, :].rearrange("p (r c) -> p r c", r=2), src).then_inc(load_in[n % RING], 16)

                turn(0, first=True)
                with sp.Fori(1, TURNS) as i:
                    turn(i)
                sp.wait_ge(table_ready, layer + 1)
                n_top = sp.value_load(table[0:1, T_COUNT:T_COUNT + 1], min_val=0, max_val=S)
                q = extra[layer]
                with sp.If(n_top > WIN):
                    sp.wait_ge(used, 2 * (base + 3 * PAIRS - len(SPARES)))
                    sp.wait_ge(q["table"], 1)

                    def again(j):
                        e = sp.value_load(table[0:1, ds(j + T_XID, 1)], min_val=0, max_val=NE - 1)
                        for m, w in enumerate((moe_w_gate, moe_w_up)):
                            sp.dma_start(ring[:, m, 0:LOAD // 2], w[layer, ds(e, 1)].rearrange("o (p k) f -> p (o k f)", k=KT)).then_inc(q["w"], 16)
                        sp.dma_start(pair_down(2)[:, 0, :, :], moe_w_down[layer, ds(e, 1)].rearrange("o (f p) d -> p (o f) d", p=P)).then_inc(q["w"], 16)

                    again(0)
                    with sp.Fori(1, MAX_EXTRA) as j:
                        sp.wait_ge(q["down"], j)
                        again(j)
                    sp.wait_ge(q["down"], MAX_EXTRA)

            for u in range(6):
                load(L_A + u, w_in[:, :, u * LC:(u + 1) * LC])
                if u == 1:
                    sp.dma_start(const[:, P:n_const], consts[:, P:n_const]).then_inc(const_in, 16)
            for dst, src in smalls:
                sp.dma_start(dst, src).then_inc(small_in, 16)
            for u in range(2):
                load(L_AOUT + u, w_mout[:, :, u * LC:(u + 1) * LC])
            load_moe(0)
            load(L_KV0, w_kv[:, :, 0:LC])
            sp.wait_ge(used, 2 * (L_CMP - RING + 1))
            for b, w in enumerate((cmp_w1_k, cmp_w1_v)):
                sp.dma_start(ring[0:DH, L_CMP % RING, b * 2048:(b + 1) * 2048].rearrange("d (l f) -> d l f", l=CB),
                             w.rearrange("(l d) f -> d l f", d=DH)).then_inc(load_in[L_CMP % RING], 16)
            for u in range(2):
                load(L_KV1 + u, w_kv[:, :, (u + 1) * LC:(u + 2) * LC])
            for u in range(2):
                load(L_Q + u, w_nq[:, :, u * LC:(u + 1) * LC])
            for u in range(2):
                load(L_NOUT + u, w_nout[:, :, u * LC:(u + 1) * LC])
            load_moe(1)
            sp.wait_ge(h_ready, 16)
            sp.dma_start(gfin, final_norm.rearrange("(a n) -> a n", a=1).to_broadcast([P, D])).then_inc(gfin_in, 16)
            for t in range(T):
                sp.wait_ge(dve_final, t + 1)
                sp.dma_start(out[0, t * P:(t + 1) * P, :], res[:, t, :]).then_inc(out_done, 16)
            sp.wait_ge(out_done, 32)

        @block.gpsimd
        def _(pool):
            pool.memset(neghalf[:, :], -0.5).then_inc(neghalf_ready, 1)
            pool.wait_ge(neghalf_ready, 1)

            def rms(n):
                pool.wait_ge(ms_ready, n + 1)
                pool.tensor_tensor(rstd[:, :], ms[:, :], neghalf[:, 0:T], ALU.pow).then_inc(rstd_ready, 1)

            pool.memset(vcn[:, :, :], 0.0).then_inc(cpad_ready, 1)
            pool.wait_ge(cpad_ready, 1)
            def gather_lo(layer):
                for t in range(T):
                    pool.wait_ge(xg_ready, T * layer + t + 1)
                    if t:
                        pool.wait_ge(xgl_ready, T * layer + t)
                    pool.tensor_tensor(xs_r[:, t, :, :], xs[:, t, :, :], xg_hi[:, t, :, :], ALU.subtract).then_inc(xgl_ready, 1)
                pool.wait_ge(xgl_ready, T * (layer + 1))

            rms(0)
            pool.wait_ge(uA_ready, 1)
            pool.tensor_tensor(cA[:, :, :].rearrange("p t h -> p (t h)"), uA[:, :, :].rearrange("p t h -> p (t h)"),
                               neghalf[:, :], ALU.pow).then_inc(powA_ready, 1)
            rms(1)
            gather_lo(0)
            rms(2)
            pool.wait_ge(rstd_ready, 3)
            pool.wait_ge(used, 2 * (L_Q + 2))
            pool.memset(QT[DH:P, :, 0, :, :], 0.0).then_inc(qpad_ready, 1)
            pool.wait_ge(qpad_ready, 1)
            pool.memset(QT[0:DH, :, 1, :, :], 0.0).then_inc(qpad_ready, 1)
            pool.wait_ge(qpad_ready, 2)
            pool.memset(PcT[:, :, :], 0.0).then_inc(cpad_ready, 1)
            pool.wait_ge(cpad_ready, 2)
            rms(3)
            gather_lo(1)
            rms(4)

        @block.scalar
        def _(act):
            def squares(n, junk=None):
                for t in range(T):
                    if n == 0:
                        act.wait_ge(x_in[t], 16)
                    else:
                        act.wait_ge(h_ready, 4 * n - (0 if t else 1 if n % 2 else 2))
                    act.activation((xs[:, :, :, :].rearrange("p t k q -> p t (k q)") if junk is None else junk)[:, t, :], h[:, t, :], ACT.Square,
                                   accum_out=sq[:, t:t + 1]).then_inc(sq_ready, 1)

            def hi_all(i):
                for q in range(QUARTERS):
                    hi_quarter(act, i, q)

            squares(0)
            act.wait_ge(xt_done, 4)
            for q in range(QUARTERS):
                x_quarter(act, X_A, xT[0], False, q, lambda q: (xt_ready, q + 1))
                hi_quarter(act, 0, q)
            hi_all(1)
            hi_all(2)
            act.wait_ge(mgateT_done, 4)
            act.activation(gA[0], bank[7][0:MH, 0:S], ACT.Tanh, scale=1.0 / SOFTCAP).then_inc(act_step, 1)
            act.activation(gA[1], bank[7][0:MH, S:2 * S], ACT.Tanh, scale=1.0 / SOFTCAP).then_inc(act_step, 1)
            act.wait_ge(act_step, 2)
            act.activation(gA[2], gA[1], ACT.Exp, scale=-SOFTCAP).then_inc(act_step, 1)
            act.wait_ge(act_step, 3)
            act.activation(gA[3], gA[2], ACT.Ln, bias=1.0).then_inc(logf_ready, 1)
            for i in range(3, 6):
                hi_all(i)
            for n in range(4):
                act.wait_ge(used, 2 * (5 + n // 2))
                act.activation(og[:, n % 2, n // 2 * 2:n // 2 * 2 + 2, :], bank[A_BANK[4 + n // 2] + n % 2][:, :].rearrange("p (h v) -> p h v", h=2),
                               ACT.Tanh, scale=0.5).then_inc(og_ready, 1)
            act.wait_ge(col_ready, 2)
            act.activation(em_col[:, :, :], em_col[:, :, :], ACT.Exp, scale=-1.0).then_inc(em_ready, 1)
            for hd in range(MH):
                act.wait_ge(eA_done, hd + 1)
                if hd >= 2:
                    act.wait_ge(pA_ready, hd - 1)
                act.activation(EA[:, hd % 2, 0:S], bank[hd % 2][:, 0:S], ACT.Exp, bias=a_col[:, 0, hd:hd + 1]).then_inc(eA_ready, 1)
                act.activation(EA[:, hd % 2, S:S + P], bank[hd % 2][:, S:S + P], ACT.Exp, bias=a_col[:, 1, hd:hd + 1]).then_inc(eA_ready, 1)
            for hd in range(MH):
                for t in range(T):
                    act.wait_ge(numA_done, hd + 1)
                    act.activation(xs[:, t, 2 * hd:2 * hd + 2, :].rearrange("p k q -> p (k q)"), bank[4 + hd][:, t * MDV:(t + 1) * MDV], ACT.Square,
                                   accum_out=ssA[:, t, hd:hd + 1]).then_inc(ssA_ready, 1)
            hi_quarter(act, 6, 0)
            hi_quarter(act, 6, 1)
            act.wait_ge(hsT_done, 4)
            for q in range(QUARTERS):
                x_quarter(act, X_AOUT, xT[0], False, q, lambda q: (hsT_ready, q + 1))
                if q >= 2:
                    hi_quarter(act, 6, q)
            hi_all(7)

            def load_spare_up(layer, r):
                act.dma_start(spare_up[r], moe_w_up[layer, 2 + r].rearrange("(p k) f -> p (k f)", k=KT)).then_inc(spare_up_in, 16)

            def moe(layer):
                squares(2 * layer + 1)
                act.dma_start(pair_down_of(spare), moe_w_down[layer, 2:4].rearrange("r (f p) d -> p r f d", p=P)).then_inc(spare_in, 16)
                for t in range(T):
                    act.wait_ge(xs_ready, T * (layer + 1) + t + 1)
                    act.activation(xg_hi[:, t, :, :], xs[:, t, :, :], ACT.Copy).then_inc(xg_ready, 1)
                act.wait_ge(route_done, layer + 1)
                load_spare_up(layer, 0)
                act.wait_ge(route_sub, layer + 1)
                act.activation(gexp[:, :, :], gexp[:, :, :], ACT.Exp).then_inc(route_exp, 1)
                act.wait_ge(route_sub2, layer + 1)
                act.activation(one[5][:, :], one[4][:, :], ACT.Exp).then_inc(route_exp2, 1)
                for k in range(1, KT, 2):
                    act.wait_ge(gather_done, KT * layer + k + 1)
                    act.activation(Xs[:, k, 0:SLOTS], bank[k % 4][:, :], ACT.Copy,
                                   scale=gains[:, G_MOE + layer, k:k + 1]).then_inc(gather_a, 1)
                p0 = PAIRS * layer
                act.wait_ge(gather_v, 4 * (layer + 1))
                act.wait_ge(gather_a, 4 * (layer + 1))
                act.wait_ge(pad_ready, layer + 1)
                act.wait_ge(table_ready, layer + 1)

                def window(i, j, first):
                    if not first:
                        act.wait_ge(hT_done, p0 + j - 1 + TURN * i)
                    for r in range(2):
                        start = act.value_load(table[0:1, ds((i * TURN + j) * 2 + r, 1)], min_val=0, max_val=SLOTS)
                        act.activation(xwin[:, j % 2, r, :, :], Xs[:, :, ds(start, WIN)], ACT.Copy).then_inc(win_ready, 1)

                def turn(i, first=False, last=False):
                    for j in range(TURN):
                        if not (last and j == TURN - 1):
                            window(i, j + 1, first and j + 1 < 2)
                        if first and j == 0:
                            load_spare_up(layer, 1)
                        act.wait_ge(*gates_used(layer, i, j, first))
                        act.activation(sg, bank[4][:, 0:F], ACT.Silu).then_inc(silu_ready, 1)
                        act.wait_ge(hT_done, p0 + j + 1 + TURN * i)
                        act.activation(hidT[:, :, :].rearrange("p f n -> p (f n)"), bank[7][:, 0:FT * P], ACT.Copy).then_inc(hT_ready, 1)
                        act.wait_ge(*down_used(layer, i, j, first, 2))
                        if not (first or j >= 2):
                            act.wait_ge(comb_done, p0 + j - 1 + TURN * i)
                        act.activation(Y[:, j % 2, 512:1024], bank[6][:, :], ACT.Copy).then_inc(y_a, 1)

                window(0, 0, True)
                turn(0, first=True)
                with act.Fori(1, TURNS - 1) as i:
                    turn(i)
                turn(TURNS - 1, last=True)
                q = extra[layer]
                n_top = act.value_load(table[0:1, T_COUNT:T_COUNT + 1], min_val=0, max_val=S)
                with act.If(n_top > WIN):
                    act.wait_ge(q["table"], 1)
                    act.wait_ge(comb_done, p0 + PAIRS)

                    def again(j):
                        start = act.value_load(table[0:1, ds(j + T_XFIRST, 1)], min_val=0, max_val=SLOTS)
                        act.activation(xwin[:, 0, 0, :, :], Xs[:, :, ds(start, WIN)], ACT.Copy).then_inc(q["win"], 1)
                        act.wait_ge(q["up"], j + 1)
                        act.activation(sg[0:WIN, :], bank[4][0:WIN, 0:F], ACT.Silu).then_inc(q["silu"], 1)
                        act.wait_ge(q["hT_done"], j + 1)
                        act.activation(hidT[:, :, 0:WIN], bank[7][:, 0:FT * P].rearrange("p (f n) -> p f n", f=FT)[:, :, 0:WIN], ACT.Copy).then_inc(q["hT"], 1)

                    again(0)
                    with act.Fori(1, MAX_EXTRA) as j:
                        again(j)

            moe(0)
            act.wait_ge(h_ready, 8)
            for q in range(QUARTERS):
                hi_quarter(act, 8, q)
                x_quarter(act, X_KV, xT[0], False, q, lambda q: (xt_ready, 8 + q + 1))
            squares(2, area[:, 12288:14336].rearrange("p (t n) -> p t n", t=T))
            hi_all(9)
            act.wait_ge(c1_ready, 1)
            act.activation(c1e[:, :], c1[:, :], ACT.Exp, scale=-1.0).then_inc(c1_exp, 1)
            act.wait_ge(c1_ready, 2)
            act.activation(c1e[:, :], c1[:, :], ACT.Exp, scale=-1.0).then_inc(c1_exp, 1)
            hi_all(10)
            act.wait_ge(used, 2 * (L_CMP + 1))
            x_quarters(act, X_Q, xT[1], False, lambda q: (xt_ready, 12 + q + 1))
            hi_all(11)
            act.wait_ge(ngate_done, 1)
            act.wait_ge(scale_ready, 2)
            for t in range(T):
                act.activation(ngate[:, t, :, :].rearrange("p h b -> p (h b)"), bank[0][:, t * 64:t * 64 + NBR * NH],
                               ACT.Exp, scale=g_scale[:, t:t + 1]).then_inc(ngate_exp, 1)
            hi_all(12)
            for u in range(2):
                act.wait_ge(used, 2 * (L_Q + u) + 2)
                for t in range(T):
                    for r in range(2):
                        ins = act.activation(QN[:, t, u, :, r, :], bank[4 + 2 * u + t][:, r * S:(r + 1) * S].rearrange("p (j d) -> p j d", j=HG),
                                             ACT.Copy, scale=q_scale[:, t:t + 1])
                    ins.then_inc(q_ready, 1)
            for i in range(1, 6):
                act.wait_ge(qkT_done, i + 1)
                if i == 1:
                    dst, src = KTn[:, 1, :, :], bank[1][:, :]
                else:
                    dst, src = QT[DH:P, (i - 2) // 2, 1, 2 * (i % 2):2 * (i % 2) + 2, :], bank[i % 4][DH:P, :]
                act.activation(dst, src.rearrange("p (a t) -> p a t", a=2), ACT.Copy).then_inc(qkT_a, 1)
            for t in range(T):
                act.wait_ge(sc_ready, t + 1)
                act.activation(Pc[:, t, :, 0:NCMP], Pc[:, t, :, 0:NCMP], ACT.Exp).then_inc(pc_exp, 1)

            def exps(u):
                n = P * (u // NH + 1)
                act.wait_ge(mN_ready, u + 1)
                if u >= NBUF:
                    act.wait_ge(ptN_done, u - NBUF + 1)
                for b in range(2):
                    act.activation(PN[:, u % NBUF, b * n:(b + 1) * n], bank[S_BANK[u % NBUF]][:, b * n:(b + 1) * n], ACT.Exp,
                                   bias=nmax[:, u % NBUF, b:b + 1], accum_out=lsum[:, u % NBUF, b:b + 1]).then_inc(eN_ready, 1)

            def evac(u):
                n = 2 * P * (u // NH + 1)
                act.wait_ge(ptN_done, u + 1)
                if u >= 4:
                    act.wait_ge(oN_done, u // 2 - 1)
                act.activation(PTn[:, u % 4, 0:n], bank[2 + u % 2][:, 0:n], ACT.Copy).then_inc(ptN_a, 1)

            exps(0)
            exps(1)
            for u in range(T * NH):
                if u + 2 < T * NH:
                    exps(u + 2)
                evac(u)
            for q in (0, 1):
                hi_quarter(act, 13, q)
            for q in range(QUARTERS):
                x_quarter(act, X_NOUT, xT[0], False, q, lambda q: (oN_read, 3 + q // 2))
                if q in (1, 3):
                    hi_quarter(act, 13, 2 + q // 2)
            hi_all(14)
            moe(1)
            squares(4)

        @block.vector
        def _(dve):
            steps = [0]

            def step(ins):
                steps[0] += 1
                ins.then_inc(dve_step, 1)
                dve.wait_ge(dve_step, steps[0])

            def mean_square(n):
                dve.wait_ge(sq_ready, T * (n + 1))
                dve.tensor_scalar(ms[:, :], sq[:, :], 1.0 / D, EPS, ALU.mult, ALU.add).then_inc(ms_ready, 1)

            def scale_rows(n):
                dve.wait_ge(rstd_ready, n + 1)
                for t in range(T):
                    dve.tensor_scalar(xs[:, t, :, :], h[:, t, :].rearrange("p (q k) -> p k q", k=KT),
                                      rstd[:, t:t + 1], None, ALU.mult).then_inc(xs_ready, 1)

            def evac_xT(done, gain, b, xt=0):
                dve.wait_ge(xt_done, done + b + 1)
                dve.tensor_tensor(xT[xt][:, 2 * b:2 * b + 2, :], bank[b][:, :].rearrange("p (k t) -> p k t", k=2),
                                  gains[:, gain, 2 * b:2 * b + 2].rearrange("p (k o) -> p k o", o=1).to_broadcast([P, 2, S]),
                                  ALU.mult).then_inc(xt_ready, 1)

            def lo_all(i):
                for q in range(QUARTERS):
                    lo_quarter(dve, i, q)

            mean_square(0)
            scale_rows(0)
            dve.wait_ge(early_in, 16 * N_EARLY)
            for q in range(QUARTERS):
                evac_xT(0, G_A, q)
                x_quarter(dve, X_A, xT[0], True, q)
                lo_quarter(dve, 0, q)
            def evac_projA(u):
                dve.wait_ge(used, 2 * u + 2)
                for hd in range(MH if u < 2 else 0):
                    dst, src = qkT[:, MH * u + hd, :], bank[A_BANK[u] + hd][:, 0:S]
                    if u == 0:
                        ins = dve.tensor_copy(dst, src)
                    else:
                        ins = dve.tensor_scalar(dst, src, float(MDK) ** -0.5, None, ALU.mult)
                    ins.then_inc(projA_read, 1)
                for t in range(T if u >= 2 else 0):
                    dve.tensor_copy(vA[:, t, 2 * (u - 2):2 * (u - 2) + 2, :],
                                    bank[A_BANK[u] + t][:, :].rearrange("p (a n) -> p a n", a=2)).then_inc(projA_read, 1)

            lo_all(1)
            dve.wait_ge(mgate_done, 1)
            dve.tensor_tensor(gpre[:, :, :], bank[0][:, 0:T * NGATE].rearrange("p (t n) -> p t n", t=T),
                              b_mgate[:, :].rearrange("p (o n) -> p o n", o=1).to_broadcast([P, T, NGATE]),
                              ALU.add).then_inc(mgate_ready, 1)
            evac_projA(0)
            lo_all(2)
            evac_projA(1)
            dve.wait_ge(const_in, 16)
            dve.tensor_copy(ident_b[:, :], ident).then_inc(const_ready, 1)
            dve.tensor_copy(mask_qb[:, :], c("mask_q")).then_inc(const_ready, 1)
            dve.tensor_copy(mask_kb[:, :], c("mask_k")).then_inc(const_ready, 1)
            lo_all(3)
            ones_row = c("ones_s")[0:MH, :]
            dve.wait_ge(logf_ready, 1)
            step(dve.tensor_scalar(gA[3], gA[3], -1.0, None, ALU.mult))
            step(dve.tensor_tensor_scan(gA[4], ones_row, gA[3], 0.0, ALU.mult, ALU.add))
            step(dve.scalar_tensor_tensor(gA[5], gA[0], SOFTCAP, gA[4], ALU.mult, ALU.subtract))
            step(dve.tensor_tensor_scan(gA[6], ones_row, gA[5], 0.0, ALU.mult, ALU.max))
            step(dve.tensor_tensor(gA[7], gA[4], gA[6], ALU.add))
            dve.tensor_scalar(gA[6], gA[6], -1.0, None, ALU.mult).then_inc(am_ready, 1)
            evac_projA(2)
            lo_all(4)
            evac_projA(3)
            lo_all(5)
            dve.wait_ge(col_done, 1)
            dve.tensor_copy(a_col[:, :, :], bank[3][:, 0:8].rearrange("p (t h) -> p t h", t=T)).then_inc(col_ready, 1)
            dve.tensor_copy(em_col[:, :, :], bank[3][:, 8:16].rearrange("p (t h) -> p t h", t=T)).then_inc(col_ready, 1)
            for hd in range(MH):
                dve.wait_ge(eA_ready, 2 * hd + 2)
                dve.wait_ge(sA_done, hd + 1)
                if hd >= 2:
                    dve.wait_ge(numA_done, hd - 1)
                dve.tensor_tensor(PA[:, hd % 2, :], bank[4 + hd][:, 0:S + P], EA[:, hd % 2, :], ALU.mult).then_inc(pA_ready, 1)
            dve.wait_ge(og_ready, 4)
            for hd in range(MH):
                if hd == MH - 1:
                    dve.wait_ge(em_ready, 1)
                    dve.wait_ge(numA_done, MH)
                    den = bank[3][:, 16:24].rearrange("p (t h) -> p t h", t=T)
                    step(dve.tensor_scalar(rA[:, :, :], den, -1.0, None, ALU.mult))
                    step(dve.tensor_tensor(rA[:, :, :], den, rA[:, :, :], ALU.max))
                    step(dve.tensor_tensor(rA[:, :, :], rA[:, :, :], em_col[:, :, :], ALU.max))
                    step(dve.reciprocal(rA[:, :, :], rA[:, :, :]))
                    dve.wait_ge(ssA_ready, T * MH)
                    step(dve.tensor_tensor(uA[:, :, :], ssA[:, :, :], rA[:, :, :], ALU.mult))
                    step(dve.tensor_tensor(uA[:, :, :], uA[:, :, :], rA[:, :, :], ALU.mult))
                    dve.tensor_scalar(uA[:, :, :], uA[:, :, :], 1.0 / MDV, EPS, ALU.mult, ALU.add).then_inc(uA_ready, 1)
                    step(dve.tensor_scalar(rA[:, :, :], rA[:, :, :], 0.5, None, ALU.mult))
                dve.wait_ge(ssA_ready, T * (hd + 1))
                for t in range(T):
                    dve.scalar_tensor_tensor(tmpA[:, t, hd, :], og[:, t, hd, :], 1.0,
                                             bank[4 + hd][:, t * MDV:(t + 1) * MDV], ALU.add, ALU.mult).then_inc(dve_step, 1)
                    steps[0] += 1
            lo_quarter(dve, 6, 0)
            dve.wait_ge(powA_ready, 1)
            step(dve.tensor_tensor(cA[:, :, :], cA[:, :, :], rA[:, :, :], ALU.mult))
            for t in range(T):
                for hd in range(MH):
                    q = MDV // KT
                    dve.tensor_scalar(xs[:, t, :, hd * q:(hd + 1) * q], tmpA[:, t, hd, :].rearrange("p (q k) -> p k q", k=KT),
                                      cA[:, t, hd:hd + 1], None, ALU.mult).then_inc(hsA_ready, 1)

            dve.wait_ge(small_in, 16 * N_SMALL)
            for b in range(4):
                dve.wait_ge(hsT_done, b + 1)
                dve.tensor_tensor(xT[0][:, 2 * b:2 * b + 2, :], bank[b][:, :].rearrange("p (k t) -> p k t", k=2),
                                  gains[:, G_HEAD, 2 * b:2 * b + 2].rearrange("p (k o) -> p k o", o=1).to_broadcast([P, 2, S]),
                                  ALU.mult).then_inc(hsT_ready, 1)
                if b:
                    lo_quarter(dve, 6, b)
                x_quarter(dve, X_AOUT, xT[0], True, b)
            def add_out(first):
                for u in range(4):
                    dve.wait_ge(used, 2 * (first + u // 2) + 2)
                    rows = h[:, u % 2, u // 2 * LC:(u // 2 + 1) * LC]
                    dve.tensor_tensor(rows, bank[4 + u][:, :], rows, ALU.add).then_inc(h_ready, 1)

            lo_all(7)
            add_out(L_AOUT)

            def first_max(vals, top, onehot, key, n):
                step(dve.tensor_reduce(top, vals, AX.X, ALU.max))
                for t in range(T):
                    dve.scalar_tensor_tensor(key[:, t, :], vals[:, t, :], top[:, t:t + 1], c("desc")[:, 0:n], ALU.is_ge,
                                             ALU.mult).then_inc(dve_step, 1)
                steps[0] += T
                dve.wait_ge(dve_step, steps[0])
                step(dve.tensor_reduce(one[9][:, :], key, AX.X, ALU.max))
                step(dve.tensor_tensor(onehot, key, one[9][:, :].rearrange("p (t o) -> p t o", o=1).to_broadcast([P, T, n]), ALU.is_ge))

            def moe(layer):
                for b in range(QUARTERS):
                    evac_xT((4, 12)[layer], G_MOE + layer, b)
                mean_square(2 * layer + 1)
                scale_rows(2 * layer + 1)
                dve.wait_ge(route_done, layer + 1)
                for t in range(T):
                    dve.scalar_tensor_tensor(lg[:, t, :], bank[4][:, t * 64:t * 64 + NR], rstd[:, t:t + 1], b_route[:, layer, :],
                                             ALU.mult, ALU.add).then_inc(dve_step, 1)
                steps[0] += T
                dve.wait_ge(dve_step, steps[0])
                first_max(lg[:, :, 0:MG], one[0][:, :], r4[0][:, :, :], r4[1][:, :, :], MG)
                for t in range(T):
                    dve.tensor_tensor(r32[:, t, :, :], lg[:, t, MG:NR].rearrange("p (g e) -> p e g", g=MG),
                                      r4[0][:, t:t + 1, :].to_broadcast([P, ME, MG]), ALU.mult).then_inc(dve_step, 1)
                steps[0] += T
                dve.wait_ge(dve_step, steps[0])
                step(dve.tensor_reduce(r8[0][:, :, :], r32[:, :, :, :], AX.X, ALU.add))
                first_max(r8[0][:, :, :], one[1][:, :], r8[1][:, :, :], r8[3][:, :, :], ME)
                step(dve.scalar_tensor_tensor(r8[2][:, :, :], r8[1][:, :, :], -3e38, r8[0][:, :, :], ALU.mult, ALU.add))
                first_max(r8[2][:, :, :], one[2][:, :], r8[0][:, :, :], r8[3][:, :, :], ME)
                for t in range(T):
                    for i, r in ((0, r8[1]), (1, r8[0])):
                        dve.tensor_tensor(hot[i][:, t, :].rearrange("p (g e) -> p g e", g=MG),
                                          r4[0][:, t, :].rearrange("p (g o) -> p g o", o=1).to_broadcast([P, MG, ME]),
                                          r[:, t:t + 1, :].to_broadcast([P, MG, ME]), ALU.mult).then_inc(dve_step, 1)
                steps[0] += 2 * T
                dve.wait_ge(dve_step, steps[0])
                dve.tensor_tensor(hot[2][:, :, :], hot[0][:, :, :], hot[1][:, :, :], ALU.add).then_inc(hot_ready, 1)
                dve.tensor_tensor(gexp[:, :, :], lg[:, :, 0:MG], one[0][:, :].rearrange("p (t o) -> p t o", o=1).to_broadcast([P, T, MG]),
                                  ALU.subtract).then_inc(route_sub, 1)
                dve.tensor_tensor(one[4][:, :], one[2][:, :], one[1][:, :], ALU.subtract).then_inc(route_sub2, 1)
                dve.wait_ge(route_exp, layer + 1)
                step(dve.tensor_reduce(one[3][:, :], gexp[:, :, :], AX.X, ALU.add))
                dve.wait_ge(route_exp2, layer + 1)
                step(dve.scalar_tensor_tensor(one[6][:, :], one[5][:, :], 1.0, one[3][:, :], ALU.add, ALU.mult))
                step(dve.reciprocal(one[6][:, :], one[6][:, :]))
                step(dve.tensor_tensor(one[7][:, :], one[6][:, :], one[5][:, :], ALU.mult))
                dve.wait_ge(rank_done, layer + 1)
                count = bank[5][:, 64:96]
                step(dve.tensor_copy(counts[:, :], count))
                step(dve.tensor_tensor_scan(cum[:, :], ones[:, 0:NE], counts[:, :], 0.0, ALU.mult, ALU.add))
                dve.tensor_reduce(n_max[:, :], counts[0:1, :], AX.X, ALU.max).then_inc(dve_step, 1)
                steps[0] += 1
                step(dve.tensor_tensor(first_slot[:, :], cum[:, :], counts[:, :], ALU.subtract))
                step(dve.tensor_tensor(place32[:, :, :], bank[5][:, 0:64].rearrange("p (t e) -> p t e", t=T),
                                       first_slot[:, :].rearrange("p (o e) -> p o e", o=1).to_broadcast([P, T, NE]), ALU.add))
                for i in range(2):
                    dve.tensor_tensor(prod32[:, i, :, :], hot[i][:, :, :], place32[:, :, :], ALU.mult).then_inc(dve_step, 1)
                steps[0] += 2
                dve.wait_ge(dve_step, steps[0])
                for i in range(2):
                    dve.tensor_reduce(one[i][:, :], prod32[:, i, :, :], AX.X, ALU.add).then_inc(dve_step, 1)
                steps[0] += 2
                dve.wait_ge(dve_step, steps[0])
                for t in range(T):
                    dve.tensor_scalar(Sel[:, t, :], iota, one[0][:, t:t + 1], None, ALU.is_equal).then_inc(dve_step, 1)
                steps[0] += T
                dve.wait_ge(dve_step, steps[0])
                for t in range(T):
                    dve.scalar_tensor_tensor(Sel[:, t, :], iota, one[1][:, t:t + 1], Sel[:, t, :], ALU.is_equal, ALU.add).then_inc(sel_ready, 1)
                dve.tensor_copy(table[0:1, 0:NE], first_slot[0:1, :]).then_inc(dve_step, 1)
                steps[0] += 1
                dve.wait_ge(dve_step, steps[0])
                dve.tensor_copy(table[0:1, T_COUNT:T_COUNT + 1], n_max[:, :]).then_inc(table_ready, 1)
                step(dve.tensor_tensor(keys[:, :, :], bank[5][:, 0:64].rearrange("p (t e) -> p t e", t=T),
                                       c("key_e").rearrange("p (o e) -> p o e", o=1).to_broadcast([P, T, NE]), ALU.add))
                for i in range(2):
                    step(dve.tensor_tensor(prod32[:, i, :, :], hot[i][:, :, :], keys[:, :, :], ALU.mult))
                    step(dve.tensor_reduce(one[10 + i][:, :], prod32[:, i, :, :], AX.X, ALU.add))
                for t in range(T):
                    for i, v in enumerate((10, 11, 6, 7)):
                        dve.tensor_scalar(diag[:, t, i, :], ident, one[v][:, t:t + 1], None, ALU.mult).then_inc(diag_ready, 1)
                dve.memset(Xs[:, :, SLOTS:PADDED], 0.0).then_inc(pad_ready, 1)
                for k in range(0, KT, 2):
                    dve.wait_ge(gather_done, KT * layer + k + 1)
                    dve.tensor_scalar(Xs[:, k, 0:SLOTS], bank[k % 4][:, :], gains[:, G_MOE + layer, k:k + 1], None,
                                      ALU.mult).then_inc(gather_v, 1)
                for t in range(T):
                    dve.wait_ge(bcast_done, T * layer + t + 1)
                    dve.tensor_copy(bcast[:, :, t * P:(t + 1) * P], bank[6 + t][:, :].rearrange("p (i n) -> p i n", i=4)).then_inc(bcast_ready, 1)
                dve.wait_ge(bcast_ready, T * (layer + 1))
                p0 = PAIRS * layer

                def weights_of(dst, key, parts, inc):
                    for g, m in ((g1, 0), (g2, 1)):
                        inc(dve.scalar_tensor_tensor(g[0:parts, :], bcast[0:parts, m, :], key, bcast[0:parts, 2 + m, :],
                                                     ALU.is_equal, ALU.mult))
                    return dve.tensor_tensor(dst, g1[0:parts, :], g2[0:parts, :], ALU.add)

                def turn(i, first=False):
                    for j in range(TURN):
                        if not (first or j >= 2):
                            dve.wait_ge(comb_done, p0 + j - 1 + TURN * i)
                        halves = []

                        def inc(ins):
                            halves.append(0)
                            ins.then_inc(terms, 1)
                            dve.wait_ge(terms, 2 * p0 + 2 * j + len(halves) + 2 * TURN * i)

                        weights_of(GT[:, j % 2, :], slot_key[:, ds(i * TURN + j, 1)], P, inc).then_inc(gt_ready, 1)
                        dve.wait_ge(silu_ready, p0 + j + 1 + TURN * i)
                        dve.tensor_tensor(hid, bank[4][:, F:2 * F], sg, ALU.mult).then_inc(hid_ready, 1)
                        dve.wait_ge(*down_used(layer, i, j, first, 1))
                        dve.tensor_copy(Y[:, j % 2, 0:512], bank[5][:, :]).then_inc(y_v, 1)

                turn(0, first=True)
                with dve.Fori(1, TURNS) as i:
                    turn(i)
                q = extra[layer]
                n_top = dve.value_load(table[0:1, T_COUNT:T_COUNT + 1], min_val=0, max_val=S)
                with dve.If(n_top > WIN):
                    extras(layer, q, weights_of)
                dve.wait_ge(comb_done, PAIRS * (layer + 1))
                for t in range(T):
                    for b in range(2):
                        dve.tensor_tensor(h[:, t, b * 512:(b + 1) * 512], bank[2 * t + b][:, :],
                                          h[:, t, b * 512:(b + 1) * 512], ALU.add).then_inc(h_ready, 1)

            def extras(layer, q, weights_of):
                cnt, extra_of, before, upto = (e[:, :] for e in ex)
                n = [0]

                def xstep(ins):
                    n[0] += 1
                    ins.then_inc(q["step"], 1)
                    dve.wait_ge(q["step"], n[0])

                bc = lambda v: v.rearrange("p (o e) -> p o e", o=1).to_broadcast([P, MAX_EXTRA, NE])
                col = lambda v: v.rearrange("p (x o) -> p x o", o=1).to_broadcast([P, MAX_EXTRA, NE])
                xstep(dve.tensor_copy(cnt, counts[:, :]))
                xstep(dve.tensor_scalar(extra_of, cnt, float(WIN), None, ALU.is_gt))
                for m in range(2, S // WIN):
                    xstep(dve.scalar_tensor_tensor(extra_of, cnt, float(m * WIN), extra_of, ALU.is_gt, ALU.add))
                xstep(dve.tensor_tensor_scan(upto, ones[:, 0:NE], extra_of, 0.0, ALU.mult, ALU.add))
                xstep(dve.tensor_tensor(before, upto, extra_of, ALU.subtract))
                idx = iota[:, 0:MAX_EXTRA]
                mine, t0, t1 = ex7
                xstep(dve.tensor_tensor(mine, bc(before), col(idx), ALU.is_le))
                xstep(dve.tensor_tensor(t0, bc(upto), col(idx), ALU.is_gt))
                xstep(dve.tensor_tensor(mine, mine, t0, ALU.mult))
                eid, start, nth, any_, key = (e[:, :] for e in exr)
                for dst, src in ((eid, iota[:, 0:NE]), (start, first_slot[:, :]), (nth, before)):
                    xstep(dve.tensor_tensor(t1, mine, bc(src), ALU.mult))
                    xstep(dve.tensor_reduce(dst, t1, AX.X, ALU.add))
                xstep(dve.tensor_reduce(any_, mine, AX.X, ALU.add))
                xstep(dve.tensor_tensor(nth, idx, nth, ALU.subtract))
                xstep(dve.tensor_scalar(nth, nth, 1.0, float(WIN), ALU.add, ALU.mult))
                xstep(dve.tensor_tensor(nth, nth, any_, ALU.mult))
                xstep(dve.tensor_tensor(start, start, nth, ALU.add))
                xstep(dve.tensor_scalar(any_, any_, -1.0, float(-KEY * NE), ALU.add, ALU.mult))
                xstep(dve.scalar_tensor_tensor(key, eid, float(KEY), nth, ALU.mult, ALU.add))
                xstep(dve.tensor_tensor(key, key, any_, ALU.add))
                xstep(dve.tensor_scalar(key, key, c("lane"), None, ALU.add))
                xstep(dve.tensor_copy(table[0:1, T_XFIRST:T_XFIRST + MAX_EXTRA], start[0:1, :]))
                dve.tensor_copy(table[0:1, T_XID:T_XID + MAX_EXTRA], eid[0:1, :]).then_inc(q["table"], 1)
                made = n[0]

                def again(j):
                    at = [0]

                    def inc(ins):
                        at[0] += 1
                        ins.then_inc(q["step"], 1)
                        dve.wait_ge(q["step"], made + at[0] + 2 * j)

                    weights_of(GT[0:WIN, 0, :], key[0:WIN, ds(j, 1)], WIN, inc).then_inc(q["gt"], 1)
                    dve.wait_ge(q["silu"], j + 1)
                    dve.tensor_tensor(hid[0:WIN, :], bank[4][0:WIN, F:2 * F], sg[0:WIN, :], ALU.mult).then_inc(q["hid"], 1)
                    dve.wait_ge(q["down"], j + 1)
                    for b in range(2):
                        dve.tensor_copy(Y[0:WIN, 0, b * 512:(b + 1) * 512], bank[5 + b][0:WIN, :]).then_inc(q["y"], 1)

                dve.wait_ge(comb_done, PAIRS * (layer + 1))
                again(0)
                with dve.Fori(1, MAX_EXTRA) as j:
                    dve.wait_ge(q["comb"], j)
                    again(j)
                dve.wait_ge(q["comb"], MAX_EXTRA)

            moe(0)
            for q in range(QUARTERS):
                evac_xT(8, G_KV, q)
                lo_quarter(dve, 8, q)
                x_quarter(dve, X_KV, xT[0], True, q)
            mean_square(2)
            for q in range(QUARTERS):
                evac_xT(8, G_Q, q, 1)
            dve.memset(cT[:, :, NG, :], 0.0).then_inc(dve_step, 1)
            steps[0] += 1

            def evac_kv(m, t):
                n = (L_KV0, L_KV1, L_KV1 + 1)[m]
                dve.wait_ge(used, 2 * n + 2)
                ins = dve.tensor_scalar(KV[:, t, 2 * m:2 * m + 2, :], bank[(4, 4, 6)[m] + t][:, :].rearrange("p (u n) -> p u n", u=2),
                                        rstd[:, t:t + 1], None, ALU.mult)
                if m:
                    step(ins)
                    rotate(KV[:, t, 2 * m, :].rearrange("p (g d) -> p g d", g=NG), t)
                else:
                    ins.then_inc(projN_read, 1)

            def rotate(x4, t):
                m = x4.shape[1]
                lead = c("cos")[:, t * ROPE:(t + 1) * ROPE], c("sin")[:, t * ROPE:(t + 1) * ROPE]
                cos, sin = (v.rearrange("p (o n) -> p o n", o=1).to_broadcast([P, m, ROPE]) for v in lead)
                ra, rb = rope_a[:, 0:m, :], rope_b[:, 0:m, :]
                dve.tensor_tensor(ra, x4[:, :, 0:ROPE], cos, ALU.mult).then_inc(dve_step, 1)
                dve.tensor_tensor(rb[:, :, 0:HALF], x4[:, :, HALF:ROPE], sin[:, :, 0:HALF], ALU.mult).then_inc(dve_step, 1)
                dve.tensor_tensor(rb[:, :, HALF:ROPE], x4[:, :, 0:HALF], sin[:, :, HALF:ROPE], ALU.mult).then_inc(dve_step, 1)
                steps[0] += 3
                dve.wait_ge(dve_step, steps[0])
                dve.tensor_tensor(x4[:, :, 0:ROPE], ra, rb, ALU.add).then_inc(projN_read, 1)

            dve.wait_ge(rstd_ready, 3)
            dve.tensor_scalar(q_scale[:, :], rstd[:, :], float(DH) ** -0.5, None, ALU.mult).then_inc(scale_ready, 1)
            dve.tensor_scalar(g_scale[:, :], rstd[:, :], -1.0, None, ALU.mult).then_inc(scale_ready, 1)
            for t in range(T):
                evac_kv(0, t)
            dve.wait_ge(dve_step, steps[0])
            for b in range(2):
                for half in range(2):
                    dve.wait_ge(cT_done, 2 * b + half + 1)
                    dve.tensor_copy(cT[:, b, 2 * half:2 * half + 2, :],
                                    bank[2 * b + half][0:DH, :].rearrange("p (g t) -> p g t", g=2)).then_inc(cT_ready, 1)
            dve.wait_ge(cT_done, 5)
            dve.tensor_copy(cT[:, :, NG, 0:CB], bank[6][0:DH, 0:2 * CB].rearrange("p (b l) -> p b l", b=2)).then_inc(cT_ready, 1)
            lo_all(9)
            for b in range(2):
                dve.wait_ge(used, 2 * L_CMP + b + 1)
                if b:
                    dve.wait_ge(c1s_ready, 1)
                step(dve.tensor_copy(cbias[:, :], bank[6 + b][0:DH, NG * NCMP:NG * NCMP + 1]))
                dve.tensor_scalar(c1[:, :], bank[6 + b][0:DH, 0:NG * NCMP], cbias[:, 0:1], None, ALU.add).then_inc(c1_ready, 1)
                dve.wait_ge(c1_exp, b + 1)
                step(dve.tensor_scalar(c1e[:, :], c1e[:, :], 1.0, None, ALU.add))
                step(dve.reciprocal(c1e[:, :], c1e[:, :]))
                dve.tensor_tensor(c1s[b][:, :], c1[:, :], c1e[:, :], ALU.mult).then_inc(c1s_ready, 1)
            lo_all(10)
            for t in range(T):
                evac_kv(1, t)
            x_quarters(dve, X_Q, xT[1], True, None)
            dve.wait_ge(c2_done, 1)
            step(dve.tensor_copy(kcn[:, :, :], bank[0][0:NCMP, 0:NG * DH].rearrange("p (g d) -> p g d", g=NG)))
            bc = lambda name: c(name)[0:NCMP, :].rearrange("p (o n) -> p o n", o=1).to_broadcast([NCMP, NG, ROPE])
            ra, rb = rope_a[0:NCMP, 0:NG, :], rope_b[0:NCMP, 0:NG, :]
            dve.wait_ge(projN_read, 4)
            step(dve.tensor_tensor(ra, kcn[:, :, 0:ROPE], bc("ccos"), ALU.mult))
            step(dve.tensor_tensor(rb[:, :, 0:HALF], kcn[:, :, HALF:ROPE], bc("csin")[:, :, 0:HALF], ALU.mult))
            step(dve.tensor_tensor(rb[:, :, HALF:ROPE], kcn[:, :, 0:HALF], bc("csin")[:, :, HALF:ROPE], ALU.mult))
            dve.tensor_tensor(kcn[:, :, 0:ROPE], ra, rb, ALU.add).then_inc(c2_ready, 1)
            dve.wait_ge(c2_done, 2)
            dve.wait_ge(cpad_ready, 1)
            dve.tensor_copy(vcn[0:NCMP, :, :], bank[1][0:NCMP, 0:NG * DH].rearrange("p (g d) -> p g d", g=NG)).then_inc(c2_ready, 1)
            lo_all(11)
            dve.wait_ge(c2_ready, 1)
            for t in range(T):
                evac_kv(2, t)
            dve.wait_ge(kcT_done, 1)
            dve.tensor_copy(kcT[:, :, :], bank[2][:, 0:2 * NCMP].rearrange("p (a n) -> p a n", a=2)).then_inc(kcT_ready, 1)
            lo_all(12)
            for u in range(2):
                for t in range(T):
                    dve.wait_ge(q_ready, T * u + t + 1)
                    dve.wait_ge(projN_read, 6 + T * u + t)
                    rotate(QN[:, t, u, :, :, :].rearrange("p j r d -> p (j r) d"), t)
                if u == 0:
                    dve.wait_ge(ngate_exp, 2)
                    g = ngate[:, :, :, :].rearrange("p t h b -> p (t h b)")
                    step(dve.tensor_scalar(g, g, 1.0, None, ALU.add))
                    step(dve.reciprocal(g, g))
            for i in (0, 2, 3, 4, 5):
                dve.wait_ge(qkT_done, i + 1)
                if i == 0:
                    dst, src = KTn[:, 0, :, :], bank[0][:, :]
                else:
                    dst, src = QT[0:DH, (i - 2) // 2, 0, 2 * (i % 2):2 * (i % 2) + 2, :], bank[i % 4][0:DH, :]
                dve.tensor_copy(dst, src.rearrange("p (a t) -> p a t", a=2)).then_inc(qkT_v, 1)
            for t in range(T):
                dve.wait_ge(sc_done, t + 1)
                pc = Pc[:, t, :, 0:NCMP]
                step(dve.tensor_tensor(pc, bank[4 + t][:, 0:NH * 16].rearrange("p (h n) -> p h n", h=NH)[:, :, 0:NCMP],
                                       c("cmask")[:, t * NCMP:(t + 1) * NCMP].rearrange("p (o n) -> p o n", o=1)
                                       .to_broadcast([P, NH, NCMP]), ALU.add))
                step(dve.tensor_reduce(ccoef[:, :], pc, AX.X, ALU.max))
                bcc = ccoef[:, :].rearrange("p (h o) -> p h o", o=1).to_broadcast([P, NH, NCMP])
                dve.tensor_tensor(pc, pc, bcc, ALU.subtract).then_inc(sc_ready, 1)
                dve.wait_ge(pc_exp, t + 1)
                step(dve.tensor_reduce(ccoef[:, :], pc, AX.X, ALU.add))
                step(dve.reciprocal(ccoef[:, :], ccoef[:, :]))
                step(dve.scalar_tensor_tensor(ccoef[:, :], ccoef[:, :], c("cvalid")[:, t:t + 1], ngate[:, t, :, 0], ALU.mult, ALU.mult))
                dve.tensor_tensor(pc, pc, bcc, ALU.mult).then_inc(pc_ready, 1)
                dve.wait_ge(pc_ready, t + 1)
            def maxima(u):
                n = P * (u // NH + 1)
                dve.wait_ge(sN_done, u + 1)
                if u >= NBUF:
                    dve.wait_ge(eN_ready, 2 * (u - NBUF + 1))
                dve.tensor_reduce(nmax[:, u % NBUF, :], bank[S_BANK[u % NBUF]][:, 0:2 * n].rearrange("p (b n) -> p b n", b=2),
                                  AX.X, ALU.max, negate=True).then_inc(mN_ready, 1)

            def normalise(u):
                t, hd = u // NH, u % NH
                n = P * (t + 1)
                dve.wait_ge(eN_ready, 2 * (u + 1))
                step(dve.reciprocal(ncoef[:, u % NBUF, :], lsum[:, u % NBUF, :]))
                step(dve.tensor_tensor(ncoef[:, u % NBUF, :], ncoef[:, u % NBUF, :], ngate[:, t, hd, 1:3], ALU.mult))
                for b in range(2):
                    dve.tensor_scalar(PN[:, u % NBUF, b * n:(b + 1) * n], PN[:, u % NBUF, b * n:(b + 1) * n],
                                      ncoef[:, u % NBUF, b:b + 1], None, ALU.mult).then_inc(pN_ready, 1)

            def read_outputs(b):
                dve.wait_ge(oN_done, 4 * (b + 1))
                dve.tensor_copy(xT[0][:, 4 * (b % 2):4 * (b % 2) + 4, b // 2 * P:(b // 2 + 1) * P],
                                bank[4 + b % 2][:, :].rearrange("p (m t) -> p m t", m=4)).then_inc(oN_read, 1)

            maxima(0)
            maxima(1)
            dve.wait_ge(cpad_ready, 2)
            for i in range(8):
                dve.wait_ge(pcT_done, i + 1)
                dve.tensor_copy(PcT[0:NCMP, 4 * (i % 4):4 * (i % 4) + 4, (i // 4) * P:(i // 4 + 1) * P],
                                bank[C_BANK[i % 3]][0:NCMP, :].rearrange("p (h t) -> p h t", h=4)).then_inc(pcT_ready, 1)
            for u in range(T * NH):
                normalise(u)
                if u + 2 < T * NH:
                    maxima(u + 2)
                if u % 8 == 3 and u > 8:
                    read_outputs(u // 8 - 1)
            lo_quarter(dve, 13, 0)
            read_outputs(3)
            x_quarter(dve, X_NOUT, xT[0], True, 0)
            for q in range(1, QUARTERS):
                lo_quarter(dve, 13, q)
                x_quarter(dve, X_NOUT, xT[0], True, q)
            lo_all(14)
            add_out(L_NOUT)
            moe(1)
            mean_square(4)
            dve.wait_ge(rstd_ready, 5)
            dve.wait_ge(gfin_in, 16)
            for t in range(T):
                dve.scalar_tensor_tensor(res[:, t, :], h[:, t, :], rstd[:, t:t + 1], gfin, ALU.mult, ALU.mult).then_inc(dve_final, 1)

        @block.tensor
        def _(pe):
            mm = nc.tensor.matmul

            def transposes(src, n_ready, ready, done):
                pe.wait_ge(ready, n_ready)
                for b in range(4):
                    for k in (2 * b, 2 * b + 1):
                        for t in range(T):
                            last = nc.tensor.transpose(bank[b][:, (k % 2) * S + t * P:(k % 2) * S + (t + 1) * P],
                                                       src[:, t, k, :], ident)
                    last.then_inc(done, 1)

            def split_steps(i, x, each):
                for k in range(KT):
                    if k % KQ == 0:
                        pe.wait_ge(xl_ready, QUARTERS * x + k // KQ + 1)
                        pe.wait_ge(parts_ready, QUARTERS * i + k // KQ + 1)
                    ins = each(k)
                    if k % KQ == KQ - 1:
                        ins.then_inc(used if k // KQ % 2 else mid_used, 1)

            h_kp = h[:, :, :].rearrange("p t (q k) -> p t k q", k=KT)

            def rows(i, x, b, free=None, between=None):
                w_hi, w_lo = hi_of(i)

                def each(k):
                    if between:
                        between(k)
                    for t in range(T):
                        if free and k == 0:
                            free(t)
                        at = slice(t * P, (t + 1) * P)
                        for m, (xp, w) in enumerate(((x_hi[x], w_hi), (x_hi[x], w_lo), (x_lo[x], w_hi))):
                            ins = mm(bank[b + t][:, :], xp[:, k, at], w[:, k, :], start=(k == 0 and m == 0), stop=(k == KT - 1 and m == 2))
                    return ins

                split_steps(i, x, each)

            pe.wait_ge(early_in, 16 * N_EARLY)
            transposes(xs, 2, xs_ready, xt_done)
            for u in range(2):
                w_hi, w_lo = hi_of(u)

                def heads_step(k):
                    for hd in range(MH):
                        at = slice(hd * P, (hd + 1) * P)
                        for m, (w, xp) in enumerate(((w_hi, x_hi[X_A]), (w_lo, x_hi[X_A]), (w_hi, x_lo[X_A]))):
                            ins = mm(bank[A_BANK[u] + hd][:, 0:S], w[:, k, at], xp[:, k, :],
                                     start=(k == 0 and m == 0), stop=(k == KT - 1 and m == 2))
                    return ins

                split_steps(u, X_A, heads_step)
                if u == 0:
                    pe.wait_ge(xt_ready, 4)
                    for t in range(T):
                        for k in range(KT):
                            ins = mm(bank[0][:, t * NGATE:(t + 1) * NGATE], xT[0][:, k, t * P:(t + 1) * P], w_mgate[:, k, :],
                                     start=(k == 0), stop=(k == KT - 1))
                    ins.then_inc(mgate_done, 1)
                    pe.wait_ge(mgate_ready, 1)
                else:
                    pe.wait_ge(projA_read, 4)
                    for i in range(2):
                        for t in range(T):
                            nc.tensor.transpose(bank[7][0:MH, i * S + t * P:i * S + (t + 1) * P],
                                                gpre[:, t, i * MH:(i + 1) * MH], ident).then_inc(mgateT_done, 1)
            for u in range(2, 6):
                rows(u, X_A, A_BANK[u], lambda t: pe.wait_ge(projA_read, (4, 8, 8, 10)[u - 2]))
            pe.wait_ge(am_ready, 1)
            pe.wait_ge(og_ready, 2)
            for i, g in enumerate((gA[5], gA[7])):
                for t in range(T):
                    ins = nc.tensor.transpose(bank[3][:, 8 * i + MH * t:8 * i + MH * (t + 1)], g[:, t * P:(t + 1) * P],
                                              ident[0:MH, 0:MH])
            ins.then_inc(col_done, 1)
            pe.wait_ge(const_ready, 3)
            sel = c("sel").rearrange("p (h m) -> p h m", h=MH)

            def exponents(hd):
                if hd >= 2:
                    pe.wait_ge(eA_ready, 2 * (hd - 1))
                b = bank[hd % 2]
                mm(b[:, 0:S], sel[0:MH, hd, :], gA[6][:, 0:S], start=True, stop=True)
                mm(b[:, 0:P], ident_b[:, :], mask_kb[:, :], start=False, stop=True, skip_group_check=True)
                mm(b[:, S:S + P], sel[0:MH, hd, :], gA[6][:, P:S], start=True, stop=True)
                mm(b[:, S:S + P], ident_b[:, :], mask_kb[:, :], start=False, stop=True, skip_group_check=True).then_inc(eA_done, 1)

            pe.wait_ge(projA_read, 12)
            exponents(0)
            exponents(1)
            pe.wait_ge(col_ready, 2)
            pe.wait_ge(og_ready, 4)
            for hd in range(MH):
                mm(bank[4 + hd][:, 0:S], qkT[:, MH + hd, 0:P], qkT[:, hd, :], start=True, stop=True)
                mm(bank[4 + hd][:, S:S + P], qkT[:, MH + hd, P:S], qkT[:, hd, P:S], start=True, stop=True).then_inc(sA_done, 1)
            for hd in range(MH):
                if hd + 2 < MH:
                    exponents(hd + 2)
                pe.wait_ge(pA_ready, hd + 1)
                p = PA[:, hd % 2, :]
                for t, tiles in ((0, [(0, 0)]), (1, [(P, 0), (S, 1)])):
                    for n, (at, s) in enumerate(tiles):
                        mm(bank[4 + hd][:, t * MDV:(t + 1) * MDV], p[:, at:at + P], vA[:, s, hd, :],
                           start=(n == 0), stop=(n == t))
                    for n, (at, s) in enumerate(tiles):
                        ins = mm(bank[3][:, 16 + t * MH + hd:17 + t * MH + hd], p[:, at:at + P], ones[:, 0:1],
                                 start=(n == 0), stop=(n == t))
                ins.then_inc(numA_done, 1)
            transposes(xs, T * MH, hsA_ready, hsT_done)
            for u in range(2):
                rows(6 + u, X_AOUT, 4 + 2 * u)

            def moe(layer):
                g = G_MOE + layer
                transposes(h_kp, 4 * (2 * layer + 1), h_ready, xt_done)
                pe.wait_ge(xt_ready, (8, 20)[layer])
                for t in range(T):
                    for k in range(KT):
                        ins = mm(bank[4][:, t * 64:t * 64 + NR], xT[0][:, k, t * P:(t + 1) * P], w_route[:, layer, k, :],
                                 start=(k == 0), stop=(k == KT - 1))
                ins.then_inc(route_done, 1)
                pe.wait_ge(hot_ready, layer + 1)
                before = c("before")
                mm(bank[5][:, 0:NE], before, hot[2][:, 0, :], start=True, stop=True)
                mm(bank[5][:, NE:2 * NE], ones, hot[2][:, 0, :], start=True, stop=False)
                mm(bank[5][:, NE:2 * NE], before, hot[2][:, 1, :], start=False, stop=True)
                mm(bank[5][:, 2 * NE:3 * NE], ones, hot[2][:, 0, :], start=True, stop=False)
                mm(bank[5][:, 2 * NE:3 * NE], ones, hot[2][:, 1, :], start=False, stop=True).then_inc(rank_done, 1)
                pe.wait_ge(sel_ready, 2 * (layer + 1))
                pe.wait_ge(xgl_ready, T * (layer + 1))
                for k in range(KT):
                    if k >= 4:
                        pe.wait_ge(*((gather_a, 4 * layer + (k - 4) // 2 + 1) if k % 2 else (gather_v, 4 * layer + (k - 4) // 2 + 1)))
                    for t in range(T):
                        for m, rows_of in enumerate((xg_hi, xs_r)):
                            ins = mm(bank[k % 4][:, :], rows_of[:, t, k, :], Sel[:, t, :], start=(t == 0 and m == 0),
                                     stop=(t == T - 1 and m == 1))
                    ins.then_inc(gather_done, 1)
                pe.wait_ge(diag_ready, 4 * T * (layer + 1))
                for t in range(T):
                    mm(bank[6 + t][:, :], ones, diag[:, t, :, :].rearrange("p i n -> p (i n)"), start=True, stop=True).then_inc(bcast_done, 1)
                pe.wait_ge(gather_v, 4 * (layer + 1))
                pe.wait_ge(gather_a, 4 * (layer + 1))
                pe.wait_ge(bcast_ready, T * (layer + 1))
                p0 = PAIRS * layer

                def combine(i, j, t, start=False, stop=False):
                    if t == 0:
                        pe.wait_ge(y_v, p0 + j + 1 + TURN * i)
                        pe.wait_ge(y_a, p0 + j + 1 + TURN * i)
                        pe.wait_ge(gt_ready, p0 + j + 1 + TURN * i)
                    for b in range(2):
                        ins = mm(bank[2 * t + b][:, :], GT[:, j % 2, t * P:(t + 1) * P], Y[:, j % 2, b * 512:(b + 1) * 512],
                                 start=start, stop=stop)
                    if t == T - 1:
                        ins.then_inc(comb_done, 1)

                def turn(i, first=False):
                    for j in range(TURN):
                        pe.wait_ge(win_ready, 2 * (p0 + j + 1) + 2 * TURN * i)
                        if not first or j:
                            pe.wait_ge(hid_ready, p0 + j + TURN * i)
                        for m in range(2):
                            in_spare = first and 3 * j + m in SPARES
                            if in_spare:
                                pe.wait_ge(spare_up_in, 32 * (layer + 1))
                                w = [v.rearrange("p (k f) -> p k f", k=KT) for v in spare_up]
                            else:
                                n = moe_load(layer, j, m, first)
                                arrived(pe, n, i)
                                w = [pair_up(n)[:, r, :, :] for r in range(2)]
                            for k in range(KT):
                                for r in range(2):
                                    ins = mm(bank[4][r * WIN:(r + 1) * WIN, m * F:(m + 1) * F], xwin[:, j % 2, r, k, :], w[r][:, k, :],
                                             start=(k == 0), stop=(k == KT - 1))
                                if in_spare and k == KT - 1:
                                    ins.then_inc(spare_used, 1)
                                elif not in_spare and k % 4 == 3:
                                    ins.then_inc(used, 1)
                        if not first or j:
                            combine(i, j - 1, 0, start=(first and j == 1))
                        pe.wait_ge(hid_ready, p0 + j + 1 + TURN * i)
                        if not first or j:
                            pe.wait_ge(hT_ready, p0 + j + TURN * i)
                        for f in range(FT):
                            ins = nc.tensor.transpose(bank[7][:, f * P:(f + 1) * P], hid[:, f * P:(f + 1) * P], ident)
                        ins.then_inc(hT_done, 1)
                        if not first or j:
                            combine(i, j - 1, 1, start=(first and j == 1))
                        pe.wait_ge(hT_ready, p0 + j + 1 + TURN * i)
                        if first and 3 * j + 2 in SPARES:
                            pe.wait_ge(spare_in, 16 * (layer + 1))
                            w, done = pair_down_of(spare), spare_used
                        else:
                            n = moe_load(layer, j, 2, first)
                            arrived(pe, n, i)
                            w, done = pair_down(n), used
                        for b in range(2):
                            for f in range(FT):
                                for r in range(2):
                                    ins = mm(bank[5 + b][r * WIN:(r + 1) * WIN, :], hidT[:, f, r * WIN:(r + 1) * WIN],
                                             w[:, r, f, b * 512:(b + 1) * 512], start=(f == 0), stop=(f == FT - 1))
                            ins.then_inc(done, 1)

                turn(0, first=True)
                with pe.Fori(1, TURNS) as i:
                    turn(i)
                for t in range(T):
                    combine(TURNS, -1, t, stop=True)
                q = extra[layer]
                n_top = pe.value_load(table[0:1, T_COUNT:T_COUNT + 1], min_val=0, max_val=S)
                with pe.If(n_top > WIN):
                    def again(j):
                        pe.wait_ge(q["w"], 48 * j + 48)
                        pe.wait_ge(q["win"], j + 1)
                        for m in range(2):
                            w = pair_up(m)
                            for k in range(KT):
                                ins = mm(bank[4][0:WIN, m * F:(m + 1) * F], xwin[:, 0, 0, k, :], w[:, 0, k, :],
                                         start=(k == 0), stop=(k == KT - 1))
                        ins.then_inc(q["up"], 1)
                        pe.wait_ge(q["hid"], j + 1)
                        for f in range(FT):
                            ins = nc.tensor.transpose(bank[7][:, f * P:(f + 1) * P], hid[:, f * P:(f + 1) * P], ident)
                        ins.then_inc(q["hT_done"], 1)
                        pe.wait_ge(q["hT"], j + 1)
                        for b in range(2):
                            for f in range(FT):
                                ins = mm(bank[5 + b][0:WIN, :], hidT[:, f, 0:WIN], pair_down(2)[:, 0, f, b * 512:(b + 1) * 512],
                                         start=(f == 0), stop=(f == FT - 1))
                        ins.then_inc(q["down"], 1)
                        pe.wait_ge(q["gt"], j + 1)
                        pe.wait_ge(q["y"], 2 * j + 2)
                        for t in range(T):
                            for b in range(2):
                                ins = mm(bank[2 * t + b][:, :], GT[0:WIN, 0, t * P:(t + 1) * P], Y[0:WIN, 0, b * 512:(b + 1) * 512],
                                         start=False, stop=True, skip_group_check=True)
                        ins.then_inc(q["comb"], 1)

                    again(0)
                    with pe.Fori(1, MAX_EXTRA) as j:
                        again(j)

            moe(0)
            transposes(h_kp, 8, h_ready, xt_done)
            rows(8, X_KV, 4)
            pe.wait_ge(xt_ready, 16)
            pe.wait_ge(projN_read, 2)
            for b in range(2):
                for half in range(2):
                    for g in (2 * half, 2 * half + 1):
                        for t in range(T):
                            ins = nc.tensor.transpose(bank[2 * b + half][0:DH, (g % 2) * S + t * P:(g % 2) * S + (t + 1) * P],
                                                      KV[:, t, b, g * DH:(g + 1) * DH], ident)
                    ins.then_inc(cT_done, 1)
            for b in range(2):
                ins = nc.tensor.transpose(bank[6][0:DH, b * CB:(b + 1) * CB], pe_in[:, b, :], ident[0:CB, 0:CB])
            ins.then_inc(cT_done, 1)
            pe.wait_ge(cT_ready, 5)
            arrived(pe, L_CMP)

            def compress(k):
                b = k // 2
                w = ring[0:DH, L_CMP % RING, b * 2048:(b + 1) * 2048].rearrange("d (l f) -> d l f", l=CB)
                for l in range(k % 2 * CB // 2, (k % 2 + 1) * CB // 2):
                    ins = mm(bank[6 + b][0:DH, 0:(NG + 1) * NCMP].rearrange("p (g n) -> p g n", g=NG + 1), w[:, l, :],
                             cT[:, b, :, l:l + CS * (NCMP - 1) + 1:CS], start=(l == 0), stop=(l == CB - 1))
                if k % 2:
                    ins.then_inc(used, 1)

            rows(9, X_KV, 4, between=lambda k: compress(k) if k < 4 else None)
            for b in range(2):
                pe.wait_ge(c1s_ready, b + 1)
                for g in range(NG):
                    ins = mm(bank[b][0:NCMP, g * DH:(g + 1) * DH], c1s[b][:, g * NCMP:(g + 1) * NCMP], w_cmp2[:, b, :],
                             start=True, stop=True)
                ins.then_inc(c2_done, 1)
            rows(10, X_KV, 6)
            pe.wait_ge(c2_ready, 2)
            for a in range(2):
                ins = nc.tensor.transpose(bank[2][:, a * NCMP:(a + 1) * NCMP],
                                          kcn[:, 2 * a:2 * a + 2, :].rearrange("p g d -> p (g d)"), ident[0:NCMP, 0:NCMP])
            ins.then_inc(kcT_done, 1)
            for t in range(T):
                for k in range(KT):
                    ins = mm(bank[0][:, t * 64:t * 64 + NBR * NH], xT[1][:, k, t * P:(t + 1) * P], w_ngate[:, k, :],
                             start=(k == 0), stop=(k == KT - 1))
            ins.then_inc(ngate_done, 1)
            for u in range(2):
                rows(11 + u, X_Q, 4 + 2 * u, lambda t: pe.wait_ge(projN_read, 2 * u + t + 3))
            pe.wait_ge(kcT_ready, 1)
            pe.wait_ge(ngate_exp, 2)
            for i in range(6):
                if i >= 4:
                    pe.wait_ge((qkT_v, qkT_a)[i - 4], 1)
                if i == 2:
                    pe.wait_ge(projN_read, 10)
                for m in range(2):
                    for t in range(T):
                        if i < 2:
                            src = KV[:, t, 2 + 2 * i, m * P:(m + 1) * P]
                        else:
                            a, j = (i - 2) // 2, 2 * (i % 2) + m
                            src = QN[:, t, a, j, :, :].rearrange("p r d -> p (r d)")
                        ins = nc.tensor.transpose(bank[i % 4][:, m * S + t * P:m * S + (t + 1) * P], src, ident)
                ins.then_inc(qkT_done, 1)
            pe.wait_ge(qkT_v, 5)
            pe.wait_ge(qkT_a, 5)
            pe.wait_ge(qpad_ready, 2)

            def q_of(hd, t):
                return QT[:, hd // (2 * HG), hd // HG % 2, hd % HG, t * P:(t + 1) * P]

            def scores(u):
                t, hd = u // NH, u % NH
                n = P * (t + 1)
                if u >= NBUF:
                    pe.wait_ge(eN_ready, 2 * (u - NBUF + 1))
                s_bank = bank[S_BANK[u % NBUF]]
                for b in range(2):
                    mm(s_bank[:, b * n:(b + 1) * n], q_of(hd, t), KTn[:, b, hd // (2 * HG), 0:n], start=True, stop=True)
                    ins = mm(s_bank[:, b * n + t * P:b * n + n], ident_b[:, :], mask_qb[:, :], start=False, stop=True,
                             skip_group_check=True)
                ins.then_inc(sN_done, 1)

            for t in range(T):
                for hd in range(NH):
                    ins = mm(bank[4 + t][:, 16 * hd:16 * hd + NCMP], q_of(hd, t), kcT[:, hd // (2 * HG), :], start=True, stop=True)
                ins.then_inc(sc_done, 1)
                scores(t)
            scores(2)
            for i in range(8):
                t = i // 4
                pe.wait_ge(pc_ready, t + 1)
                if i >= 3:
                    pe.wait_ge(pcT_ready, i - 2)
                for m in range(4):
                    ins = nc.tensor.transpose(bank[C_BANK[i % 3]][0:NCMP, m * P:(m + 1) * P], Pc[:, t, 4 * (i % 4) + m, 0:NCMP], ident)
                ins.then_inc(pcT_done, 1)
            pe.wait_ge(pcT_ready, 8)

            def turned(u):
                n = 2 * (u // NH + 1)
                pe.wait_ge(pN_ready, 2 * (u + 1))
                if u >= 2:
                    pe.wait_ge(ptN_a, u - 1)
                for m in range(n):
                    ins = nc.tensor.transpose(bank[2 + u % 2][:, m * P:(m + 1) * P], PN[:, u % NBUF, m * P:(m + 1) * P], ident)
                ins.then_inc(ptN_done, 1)

            def outputs(w):
                t, pair = w // (NH // 2), w % (NH // 2)
                g = 2 * pair // HG
                if w % 4 == 0 and w >= 8:
                    pe.wait_ge(oN_read, w // 4 - 1)
                pe.wait_ge(ptN_a, 2 * w + 2)
                for r in range(2):
                    mm(bank[4 + w // 4 % 2][r * DH:(r + 1) * DH, (w % 4) * P:(w % 4 + 1) * P], vcn[:, g, :],
                       PcT[:, 2 * pair + r, t * P:(t + 1) * P], start=True, stop=False)
                n = 2 * (t + 1)
                for m in range(n):
                    b, s = m // (t + 1), m % (t + 1)
                    for r in range(2):
                        ins = mm(bank[4 + w // 4 % 2][r * DH:(r + 1) * DH, (w % 4) * P:(w % 4 + 1) * P],
                                 KV[:, s, 3 + 2 * b, g * DH:(g + 1) * DH], PTn[:, (2 * w + r) % 4, m * P:(m + 1) * P],
                                 start=False, stop=(m == n - 1))
                ins.then_inc(oN_done, 1)

            for u in range(T * NH):
                if u and u + 2 < T * NH:
                    scores(u + 2)
                if u >= 3 and u % 2:
                    outputs(u // 2 - 1)
                turned(u)
            outputs(T * NH // 2 - 1)
            pe.wait_ge(oN_read, 4)
            for u in range(2):
                rows(13 + u, X_NOUT, 4 + 2 * u)
            moe(1)


N_EARLY, N_SMALL = 4, 18
_INS = ['x', 'mlstm_norm', 'mlstm_w_in', 'mlstm_gate_bias', 'mlstm_head_norm', 'mlstm_w_out', 'kv_norm', 'kv_w',
        'cmp_pe_k', 'cmp_w1_k', 'cmp_w2_k', 'cmp_pe_v', 'cmp_w1_v', 'cmp_w2_v', 'nsa_norm', 'nsa_w_q', 'nsa_w_out',
        'moe_norm', 'moe_w_group', 'moe_b_group', 'moe_w_router', 'moe_b_router', 'moe_w_gate', 'moe_w_up',
        'moe_w_down', 'final_norm']


def kernel(**inputs):
    import concourse.bacc as bacc
    from concourse.bass_utils import run_bass_kernel_spmd as run

    nc = bacc.Bacc("TRN2", target_bir_lowering=False, num_devices=1,
                   dynamic_dma_scratch_size=1024)
    arrays, args = {}, []
    for name in _INS:
        a = np.ascontiguousarray(inputs[name])
        arrays[f"in_{name}"] = a
        args.append(nc.dram_tensor(f"in_{name}", a.shape, mybir.dt.from_np(a.dtype), kind="ExternalInput").ap())
    consts, place = constants()
    arrays["in_consts"] = consts
    args.append(nc.dram_tensor("in_consts", consts.shape, mybir.dt.float32, kind="ExternalInput").ap())
    args.append(nc.dram_tensor("out_h", (1, S, D), mybir.dt.float32, kind="ExternalOutput").ap())
    build(nc, *args, place, consts.shape[1])
    r = run(nc, [arrays], core_ids=[0])
    return r.results[0]["out_h"]
```
